# Optimizing a Trainium2 kernel written in Bass

```python
import math
import jax
import jax.numpy as jnp
from jax import lax
import numpy as np
import jax, jax.numpy as jnp

D_MODEL = 1024
BATCH = 1
SEQ = 512
DEPTH = 1

N_META = 16
EPS = 1e-6
DA_HEADS = 4
DA_HEAD_DIM = 64
DA_V_DIM = 2 * DA_HEAD_DIM
DA_WIDTH = DA_HEADS * DA_V_DIM
ROPE_THETA = 500000.0
ROPE_DIM = DA_HEAD_DIM // 4
Q_BLOCK = 128
GLA_HEADS = 4
GLA_DK = 64
GLA_DV = 128
GLA_WIDTH = GLA_HEADS * GLA_DV
GLA_GATE_RANK = 16
GLA_TAU = 16.0
GLA_CHUNK = 64
MIX_WIDTH = DA_WIDTH + GLA_WIDTH
IN_SIZES = (DA_HEADS * 2 * DA_HEAD_DIM, DA_HEADS * 2 * DA_HEAD_DIM, DA_WIDTH, GLA_HEADS * GLA_DK, GLA_HEADS * GLA_DK, GLA_WIDTH, GLA_WIDTH, GLA_GATE_RANK, GLA_GATE_RANK)
IN_WIDTH = sum(IN_SIZES)
PEER_HEADS = 8
PEER_NKEYS = 128
PEER_EXPERTS = PEER_NKEYS * PEER_NKEYS
PEER_KEY_DIM = 128
PEER_TOPK = 16
PEER_BLOCK = 256


def rmsnorm(x, w):
    xf = x.astype(jnp.float32)
    y = xf * lax.rsqrt(jnp.mean(xf * xf, axis=-1, keepdims=True) + EPS)
    return (y * w.astype(jnp.float32)).astype(x.dtype)

def partial_rope(x, pos):
    inv = jnp.power(ROPE_THETA, -jnp.arange(0, ROPE_DIM, 2, dtype=jnp.float32) / ROPE_DIM)
    ang = pos.astype(jnp.float32)[:, None] * inv[None, :]
    cos = jnp.cos(ang)[None, :, None, None, :]
    sin = jnp.sin(ang)[None, :, None, None, :]
    xr = x[..., :ROPE_DIM].astype(jnp.float32)
    x1, x2 = xr[..., :ROPE_DIM // 2], xr[..., ROPE_DIM // 2:]
    rot = jnp.concatenate([x1 * cos - x2 * sin, x2 * cos + x1 * sin], axis=-1)
    return jnp.concatenate([rot.astype(x.dtype), x[..., ROPE_DIM:]], axis=-1)

def diff_attention(q, k, v, lam, pos):
    B, T = q.shape[0], q.shape[1]
    q = partial_rope(q, pos) * (DA_HEAD_DIM ** -0.5)
    k = partial_rope(k, pos)
    nb = -(-T // Q_BLOCK)
    qp = jnp.pad(q, ((0, 0), (0, nb * Q_BLOCK - T), (0, 0), (0, 0), (0, 0)))
    qb = qp.reshape(B, nb, Q_BLOCK, DA_HEADS, 2, DA_HEAD_DIM).transpose(1, 0, 2, 3, 4, 5)

    def block(qi):
        s = jnp.einsum('bqhcd,bkhcd->bhcqk', qi, k).astype(jnp.float32)
        p = jax.nn.softmax(s, axis=-1)
        a = p[:, :, 0] - lam * p[:, :, 1]
        return jnp.einsum('bhqk,bkhv->bqhv', a.astype(v.dtype), v)

    o = lax.map(block, qb)
    return o.transpose(1, 0, 2, 3, 4).reshape(B, nb * Q_BLOCK, DA_HEADS, DA_V_DIM)[:, :T]

def gla_chunk_scan(q, k, v, g):
    B, L = q.shape[0], q.shape[1]
    n = L // GLA_CHUNK

    def to_chunks(a):
        return a.reshape(B, n, GLA_CHUNK, a.shape[2], a.shape[3]).transpose(1, 0, 3, 2, 4)

    mask = jnp.tril(jnp.ones((GLA_CHUNK, GLA_CHUNK), dtype=bool))[:, :, None]

    def step(state, inp):
        qc, kc, vc, gc = inp
        b = jnp.cumsum(gc, axis=2)
        rel = b[:, :, :, None, :] - b[:, :, None, :, :]
        decay = jnp.exp(jnp.where(mask, rel, -jnp.inf))
        attn = jnp.einsum('bhid,bhjd,bhijd->bhij', qc, kc, decay)
        o = jnp.einsum('bhij,bhjv->bhiv', attn, vc) + jnp.einsum('bhid,bhdv->bhiv', qc * jnp.exp(b), state)
        b_last = b[:, :, -1]
        state = state * jnp.exp(b_last)[..., None] + jnp.einsum('bhjd,bhjv->bhdv', kc * jnp.exp(b_last[:, :, None] - b), vc)
        return state, o

    state0 = jnp.zeros((B, q.shape[2], q.shape[3], v.shape[3]), jnp.float32)
    _, o = lax.scan(step, state0, (to_chunks(q), to_chunks(k), to_chunks(v), to_chunks(g)))
    return o.transpose(1, 0, 3, 2, 4).reshape(B, L, q.shape[2], v.shape[3])

def gla_bidirectional(q, k, v, g_f, g_b):
    pad = (-N_META) % GLA_CHUNK
    padf = lambda a: jnp.pad(a, ((0, 0), (pad, 0), (0, 0), (0, 0)))
    flip = lambda a: a[:, ::-1]
    qp, kp, vp = padf(q), padf(k), padf(v)
    o_f = gla_chunk_scan(qp, kp, vp, padf(g_f))
    o_b = flip(gla_chunk_scan(flip(qp), flip(kp), flip(vp), flip(padf(g_b))))
    return (o_f + o_b)[:, pad:]

def peer_ffn(x, w_q, sub_keys, u, v):
    N, D = x.shape
    nb = -(-N // PEER_BLOCK)
    xb = jnp.pad(x, ((0, nb * PEER_BLOCK - N), (0, 0))).reshape(nb, PEER_BLOCK, D)

    def block(xi):
        n = xi.shape[0]
        q = (xi @ w_q).reshape(n, PEER_HEADS, 2, PEER_KEY_DIM)
        s = jnp.einsum('nhpc,hpkc->nhpk', q, sub_keys).astype(jnp.float32)
        ts, ti = lax.top_k(s, PEER_TOPK)
        cand_s = (ts[:, :, 0, :, None] + ts[:, :, 1, None, :]).reshape(n, PEER_HEADS, PEER_TOPK * PEER_TOPK)
        cand_i = (ti[:, :, 0, :, None] * PEER_NKEYS + ti[:, :, 1, None, :]).reshape(n, PEER_HEADS, PEER_TOPK * PEER_TOPK)
        best_s, best_p = lax.top_k(cand_s, PEER_TOPK)
        idx = jnp.take_along_axis(cand_i, best_p, axis=-1)
        gate = jax.nn.softmax(best_s, axis=-1)
        act = jax.nn.gelu(jnp.einsum('nd,nhkd->nhk', xi, u[idx]).astype(jnp.float32), approximate=False)
        return jnp.einsum('nhk,nhkd->nd', (gate * act).astype(xi.dtype), v[idx])

    return lax.map(block, xb).reshape(nb * PEER_BLOCK, D)[:N]

def first_inputs(seed: int = 0) -> dict:
    key = jax.random.key(seed)
    ks = jax.random.split(key, 24)
    nrm = lambda k, shape, s: jax.random.normal(k, shape, jnp.float32) * s
    gain = lambda k, shape: 1.0 + 0.02 * jax.random.normal(k, shape, jnp.float32)
    return {
        'x': nrm(ks[0], (BATCH, SEQ, D_MODEL), 1.0),
        'meta_tokens': nrm(ks[1], (N_META, D_MODEL), 1.0),
        'ln1_w': gain(ks[2], (DEPTH, D_MODEL)),
        'w_in': nrm(ks[3], (DEPTH, D_MODEL, IN_WIDTH), D_MODEL ** -0.5),
        'da_lambda_q1': nrm(ks[4], (DEPTH, DA_HEAD_DIM), 0.1),
        'da_lambda_k1': nrm(ks[5], (DEPTH, DA_HEAD_DIM), 0.1),
        'da_lambda_q2': nrm(ks[6], (DEPTH, DA_HEAD_DIM), 0.1),
        'da_lambda_k2': nrm(ks[7], (DEPTH, DA_HEAD_DIM), 0.1),
        'da_subln_w': gain(ks[8], (DEPTH, DA_V_DIM)),
        'gla_gate_w2_f': nrm(ks[9], (DEPTH, GLA_GATE_RANK, GLA_HEADS * GLA_DK), GLA_GATE_RANK ** -0.5),
        'gla_gate_b_f': nrm(ks[10], (DEPTH, GLA_HEADS * GLA_DK), 0.1),
        'gla_gate_w2_b': nrm(ks[11], (DEPTH, GLA_GATE_RANK, GLA_HEADS * GLA_DK), GLA_GATE_RANK ** -0.5),
        'gla_gate_b_b': nrm(ks[12], (DEPTH, GLA_HEADS * GLA_DK), 0.1),
        'gla_norm_w': gain(ks[13], (DEPTH, GLA_DV)),
        'w_out': nrm(ks[14], (DEPTH, MIX_WIDTH, D_MODEL), MIX_WIDTH ** -0.5),
        'ln2_w': gain(ks[15], (DEPTH, D_MODEL)),
        'peer_w_q': nrm(ks[16], (DEPTH, D_MODEL, PEER_HEADS * 2 * PEER_KEY_DIM), D_MODEL ** -0.5),
        'peer_sub_keys': nrm(ks[17], (DEPTH, PEER_HEADS, 2, PEER_NKEYS, PEER_KEY_DIM), PEER_KEY_DIM ** -0.5),
        'peer_u': nrm(ks[18], (DEPTH, PEER_EXPERTS, D_MODEL), D_MODEL ** -0.5),
        'peer_v': nrm(ks[19], (DEPTH, PEER_EXPERTS, D_MODEL), PEER_HEADS ** -0.5),
        'final_norm_w': gain(ks[20], (D_MODEL,)),
    }

def first_block(x, meta_tokens, ln1_w, w_in, da_lambda_q1, da_lambda_k1, da_lambda_q2, da_lambda_k2, da_subln_w, gla_gate_w2_f, gla_gate_b_f, gla_gate_w2_b, gla_gate_b_b, gla_norm_w, w_out, ln2_w, peer_w_q, peer_sub_keys, peer_u, peer_v, final_norm_w):
    B = x.shape[0]
    meta = jnp.broadcast_to(meta_tokens.astype(x.dtype)[None], (B, N_META, D_MODEL))
    h = jnp.concatenate([meta, x], axis=1)
    T = h.shape[1]
    pos = jnp.arange(T)
    splits = np.cumsum(IN_SIZES)[:-1].tolist()
    for l in range(DEPTH):
        xn = rmsnorm(h, ln1_w[l])
        proj = xn @ w_in[l]
        dq, dk, dv, gq, gk, gv, gr, zf, zb = jnp.split(proj, splits, axis=-1)

        lam_init = 0.8 - 0.6 * math.exp(-0.3 * l)
        lam = (jnp.exp(jnp.sum(da_lambda_q1[l].astype(jnp.float32) * da_lambda_k1[l].astype(jnp.float32)))
               - jnp.exp(jnp.sum(da_lambda_q2[l].astype(jnp.float32) * da_lambda_k2[l].astype(jnp.float32))) + lam_init)
        da = diff_attention(dq.reshape(B, T, DA_HEADS, 2, DA_HEAD_DIM), dk.reshape(B, T, DA_HEADS, 2, DA_HEAD_DIM),
                            dv.reshape(B, T, DA_HEADS, DA_V_DIM), lam, pos)
        da = (rmsnorm(da, da_subln_w[l]) * (1.0 - lam_init)).reshape(B, T, DA_WIDTH)

        f32 = jnp.float32
        log_g_f = jax.nn.log_sigmoid((zf @ gla_gate_w2_f[l] + gla_gate_b_f[l]).astype(f32)) / GLA_TAU
        log_g_b = jax.nn.log_sigmoid((zb @ gla_gate_w2_b[l] + gla_gate_b_b[l]).astype(f32)) / GLA_TAU
        go = gla_bidirectional((gq.astype(f32) * (GLA_DK ** -0.5)).reshape(B, T, GLA_HEADS, GLA_DK),
                               gk.astype(f32).reshape(B, T, GLA_HEADS, GLA_DK),
                               gv.astype(f32).reshape(B, T, GLA_HEADS, GLA_DV),
                               log_g_f.reshape(B, T, GLA_HEADS, GLA_DK),
                               log_g_b.reshape(B, T, GLA_HEADS, GLA_DK))
        go = rmsnorm(go, gla_norm_w[l]).reshape(B, T, GLA_WIDTH).astype(h.dtype) * jax.nn.silu(gr)

        h = h + jnp.concatenate([da, go], axis=-1) @ w_out[l]
        if l == DEPTH - 1:
            h = h[:, N_META:]

        hn = rmsnorm(h, ln2_w[l])
        h = h + peer_ffn(hn.reshape(-1, D_MODEL), peer_w_q[l], peer_sub_keys[l], peer_u[l], peer_v[l]).reshape(h.shape)
    return rmsnorm(h, final_norm_w)


GRID_W = 64
CTX_LEN = 256
D_FOURIER = 256
FOURIER_GROUPS = 4
D_CONV = 256
CONV_WIDTH = 31
N_NA_HEADS = 8
NA_HEAD_DIM = 64
D_NA = N_NA_HEADS * NA_HEAD_DIM
WIN_ROWS = 8
WIN_COLS = 16
QKV_START = D_FOURIER + 2 * D_CONV
KV_START = QKV_START + D_NA
D_IN = QKV_START + 3 * D_NA
D_MIX = D_FOURIER + D_CONV + D_NA
D_FF = 4 * D_MODEL
N_MOD = 6
RMS_EPS = 1e-6
LN_EPS = 1e-5


def rms_norm(x, g):
    xf = x.astype(jnp.float32)
    y = xf * lax.rsqrt(jnp.mean(xf * xf, axis=-1, keepdims=True) + RMS_EPS)
    return (y * g.astype(jnp.float32)).astype(x.dtype)

def layer_norm(x, g, b):
    xf = x.astype(jnp.float32)
    mu = jnp.mean(xf, axis=-1, keepdims=True)
    var = jnp.mean(jnp.square(xf - mu), axis=-1, keepdims=True)
    y = (xf - mu) * lax.rsqrt(var + LN_EPS)
    return (y * g.astype(jnp.float32) + b.astype(jnp.float32)).astype(x.dtype)

def modulate(x, shift, scale):
    return x * (1 + scale) + shift

def split_heads(u):
    b, l, _ = u.shape
    qkv = u[..., QKV_START:].reshape(b, l, 3, N_NA_HEADS, NA_HEAD_DIM)
    return u[..., :D_FOURIER], u[..., D_FOURIER:QKV_START], qkv[:, :, 0], qkv[:, :, 1], qkv[:, :, 2]

def fourier_mix(u, w):
    b, l, _ = u.shape
    ug = u.reshape(b, l, FOURIER_GROUPS, D_FOURIER // FOURIER_GROUPS).astype(jnp.float32)
    f = jnp.fft.fftn(ug, axes=(1, 3), norm="ortho").real
    return f.reshape(b, l, D_FOURIER).astype(u.dtype) @ w

def conv_module(u, dw_w, dw_b, ln_g, ln_b, pw_w, pw_b):
    a, gt = jnp.split(u, 2, axis=-1)
    v = a * jax.nn.sigmoid(gt)
    pad = CONV_WIDTH // 2
    v = lax.conv_general_dilated(v, dw_w[:, None, :].astype(v.dtype), window_strides=(1,), padding=[(pad, pad)],
                                 dimension_numbers=("NWC", "WIO", "NWC"), feature_group_count=D_CONV) + dw_b
    v = jax.nn.silu(layer_norm(v, ln_g, ln_b))
    return v @ pw_w + pw_b

def context_attention(q, k, v):
    s = jnp.einsum("bqhd,bkhd->bhqk", q, k).astype(jnp.float32) * (NA_HEAD_DIM ** -0.5)
    p = jax.nn.softmax(s, axis=-1).astype(v.dtype)
    o = jnp.einsum("bhqk,bkhd->bqhd", p, v)
    return o.reshape(q.shape[0], q.shape[1], D_NA)

def neighbourhood_attention(q, k, v, k_ctx, v_ctx, rpb):
    b, l, h, dh = q.shape
    rows = l // GRID_W
    kr = min(WIN_ROWS, rows)
    r = np.arange(rows)
    row_start = np.clip(r - kr // 2, 0, rows - kr)
    key_rows = row_start[:, None] + np.arange(kr)[None, :]
    col = np.arange(GRID_W)
    col_start = np.clip(col - WIN_COLS // 2, 0, GRID_W - WIN_COLS)
    col_valid = (col[None, :] >= col_start[:, None]) & (col[None, :] < col_start[:, None] + WIN_COLS)
    row_off = key_rows - r[:, None] + (WIN_ROWS - 1)
    col_off = np.clip(col[None, :] - col[:, None] + (WIN_COLS - 1), 0, 2 * WIN_COLS - 2)
    bias = rpb[:, row_off[:, :, None, None], col_off[None, None]].astype(jnp.float32)
    bias = jnp.where(jnp.asarray(col_valid)[None, None, None], bias, -jnp.inf)
    bias = bias.transpose(0, 1, 3, 2, 4).reshape(h, rows, GRID_W, kr * GRID_W)
    qg = q.reshape(b, rows, GRID_W, h, dh)
    kg = k.reshape(b, rows, GRID_W, h, dh)[:, key_rows].reshape(b, rows, kr * GRID_W, h, dh)
    vg = v.reshape(b, rows, GRID_W, h, dh)[:, key_rows].reshape(b, rows, kr * GRID_W, h, dh)
    scale = NA_HEAD_DIM ** -0.5
    s_loc = jnp.einsum("brqhd,brkhd->bhrqk", qg, kg).astype(jnp.float32) * scale + bias[None]
    s_ctx = jnp.einsum("brqhd,bchd->bhrqc", qg, k_ctx).astype(jnp.float32) * scale
    p = jax.nn.softmax(jnp.concatenate([s_loc, s_ctx], axis=-1), axis=-1).astype(v.dtype)
    n_loc = kr * GRID_W
    o = (jnp.einsum("bhrqk,brkhd->brqhd", p[..., :n_loc], vg)
         + jnp.einsum("bhrqc,bchd->brqhd", p[..., n_loc:], v_ctx))
    return o.reshape(b, l, D_NA)

def second_inputs(seed: int = 0) -> dict:
    key = jax.random.key(seed)
    ks = jax.random.split(key, 24)

    def nrm(k, shape, scale):
        return jax.random.normal(k, shape, jnp.float32) * scale

    return {
        "x": nrm(ks[0], (BATCH, SEQ, D_MODEL), 1.0),
        "c": nrm(ks[1], (BATCH, D_MODEL), 1.0),
        "ctx": nrm(ks[2], (BATCH, CTX_LEN, D_MODEL), 1.0),
        "c_ctx": nrm(ks[3], (D_MODEL,), 1.0),
        "ada_w": nrm(ks[4], (DEPTH, D_MODEL, N_MOD * D_MODEL), D_MODEL ** -0.5),
        "ada_b": nrm(ks[5], (DEPTH, N_MOD * D_MODEL), 0.02),
        "norm1_g": 1.0 + nrm(ks[6], (DEPTH, D_MODEL), 0.05),
        "norm2_g": 1.0 + nrm(ks[7], (DEPTH, D_MODEL), 0.05),
        "w_in": nrm(ks[8], (DEPTH, D_MODEL, D_IN), D_MODEL ** -0.5),
        "w_fourier": nrm(ks[9], (DEPTH, D_FOURIER, D_FOURIER), D_FOURIER ** -0.5),
        "conv_dw_w": nrm(ks[10], (DEPTH, CONV_WIDTH, D_CONV), CONV_WIDTH ** -0.5),
        "conv_dw_b": nrm(ks[11], (DEPTH, D_CONV), 0.02),
        "conv_norm_g": 1.0 + nrm(ks[12], (DEPTH, D_CONV), 0.05),
        "conv_norm_b": nrm(ks[13], (DEPTH, D_CONV), 0.02),
        "conv_pw_w": nrm(ks[14], (DEPTH, D_CONV, D_CONV), D_CONV ** -0.5),
        "conv_pw_b": nrm(ks[15], (DEPTH, D_CONV), 0.02),
        "na_rpb": nrm(ks[16], (DEPTH, N_NA_HEADS, 2 * WIN_ROWS - 1, 2 * WIN_COLS - 1), 0.1),
        "w_out": nrm(ks[17], (DEPTH, D_MIX, D_MODEL), D_MIX ** -0.5),
        "mlp_w1": nrm(ks[18], (DEPTH, D_MODEL, D_FF), D_MODEL ** -0.5),
        "mlp_w2": nrm(ks[19], (DEPTH, D_FF, D_MODEL), D_FF ** -0.5),
        "final_norm_g": 1.0 + nrm(ks[20], (D_MODEL,), 0.05),
    }

def second_block(x, c, ctx, c_ctx, ada_w, ada_b, norm1_g, norm2_g, w_in, w_fourier, conv_dw_w, conv_dw_b,
              conv_norm_g, conv_norm_b, conv_pw_w, conv_pw_b, na_rpb, w_out, mlp_w1, mlp_w2, final_norm_g):
    h_lat, h_ctx = x, ctx
    b = x.shape[0]
    n_ctx = ctx.shape[1]
    for i in range(DEPTH):
        last = i == DEPTH - 1
        conv_p = (conv_dw_w[i], conv_dw_b[i], conv_norm_g[i], conv_norm_b[i], conv_pw_w[i], conv_pw_b[i])
        mod = (jax.nn.silu(c) @ ada_w[i] + ada_b[i])[:, None, :]
        sh1, sc1, g1, sh2, sc2, g2 = jnp.split(mod, N_MOD, axis=-1)
        n_ctx_mod = (2 if last else N_MOD) * D_MODEL
        mod_c = (jax.nn.silu(c_ctx) @ ada_w[i][:, :n_ctx_mod] + ada_b[i][:n_ctx_mod])[None, None, :]
        mods_c = jnp.split(mod_c, n_ctx_mod // D_MODEL, axis=-1)

        hn_ctx = modulate(rms_norm(h_ctx, norm1_g[i]), mods_c[0], mods_c[1])
        if last:
            kv = (hn_ctx @ w_in[i][:, KV_START:]).reshape(b, n_ctx, 2, N_NA_HEADS, NA_HEAD_DIM)
            k_ctx, v_ctx = kv[:, :, 0], kv[:, :, 1]
        else:
            uf_c, uc_c, q_ctx, k_ctx, v_ctx = split_heads(hn_ctx @ w_in[i])
            mix_ctx = jnp.concatenate([fourier_mix(uf_c, w_fourier[i]), conv_module(uc_c, *conv_p),
                                       context_attention(q_ctx, k_ctx, v_ctx)], axis=-1)

        hn_lat = modulate(rms_norm(h_lat, norm1_g[i]), sh1, sc1)
        uf, uc, q, k, v = split_heads(hn_lat @ w_in[i])
        mix_lat = jnp.concatenate([fourier_mix(uf, w_fourier[i]), conv_module(uc, *conv_p),
                                   neighbourhood_attention(q, k, v, k_ctx, v_ctx, na_rpb[i])], axis=-1)
        h_lat = h_lat + g1 * (mix_lat @ w_out[i])

        hn = modulate(rms_norm(h_lat, norm2_g[i]), sh2, sc2)
        h_lat = h_lat + g2 * (jnp.square(jax.nn.relu(hn @ mlp_w1[i])) @ mlp_w2[i])

        if not last:
            h_ctx = h_ctx + mods_c[2] * (mix_ctx @ w_out[i])
            hn_c2 = modulate(rms_norm(h_ctx, norm2_g[i]), mods_c[3], mods_c[4])
            h_ctx = h_ctx + mods_c[5] * (jnp.square(jax.nn.relu(hn_c2 @ mlp_w1[i])) @ mlp_w2[i])
    return rms_norm(h_lat, final_norm_g)


def setup_inputs(seed=0):
    out = dict(first_inputs(seed))
    for name, value in second_inputs(seed + 1).items():
        if name != "x":
            out[name + "_2"] = value
    return out


def reference(
    x, meta_tokens, ln1_w, w_in, da_lambda_q1, da_lambda_k1, da_lambda_q2, da_lambda_k2,
    da_subln_w, gla_gate_w2_f, gla_gate_b_f, gla_gate_w2_b, gla_gate_b_b, gla_norm_w, w_out,
    ln2_w, peer_w_q, peer_sub_keys, peer_u, peer_v, final_norm_w, c_2, ctx_2, c_ctx_2, ada_w_2,
    ada_b_2, norm1_g_2, norm2_g_2, w_in_2, w_fourier_2, conv_dw_w_2, conv_dw_b_2, conv_norm_g_2,
    conv_norm_b_2, conv_pw_w_2, conv_pw_b_2, na_rpb_2, w_out_2, mlp_w1_2, mlp_w2_2,
    final_norm_g_2,
):
    x = first_block(
        x, meta_tokens, ln1_w, w_in, da_lambda_q1, da_lambda_k1, da_lambda_q2, da_lambda_k2,
        da_subln_w, gla_gate_w2_f, gla_gate_b_f, gla_gate_w2_b, gla_gate_b_b, gla_norm_w, w_out,
        ln2_w, peer_w_q, peer_sub_keys, peer_u, peer_v, final_norm_w,
    )
    return second_block(
        x, c_2, ctx_2, c_ctx_2, ada_w_2, ada_b_2, norm1_g_2, norm2_g_2, w_in_2, w_fourier_2,
        conv_dw_w_2, conv_dw_b_2, conv_norm_g_2, conv_norm_b_2, conv_pw_w_2, conv_pw_b_2,
        na_rpb_2, w_out_2, mlp_w1_2, mlp_w2_2, final_norm_g_2,
    )


_drawn_inputs = setup_inputs


def setup_inputs(seed=0):
    import zlib

    import numpy as np

    out = dict(_drawn_inputs(seed))
    spreads = {}
    factors = {'da_subln_w': 3.25,
     'gla_gate_b_f': 2.976,
     'gla_gate_b_b': 3.168,
     'gla_norm_w': 3.85,
     'final_norm_w': 2.989,
     'norm1_g_2': 3.514,
     'conv_dw_b_2': 24.358,
     'conv_norm_g_2': 18.743,
     'conv_norm_b_2': 43.986,
     'conv_pw_b_2': 39.244,
     'na_rpb_2': 8.0,
     'norm2_g_2': 3.369,
     'ln2_w': 2.859}
    for name, (base, spread) in spreads.items():
        noise = np.random.default_rng([zlib.crc32(name.encode()), seed]).standard_normal(out[name].shape)
        drawn = base * np.exp(spread * noise) if base else spread * noise
        out[name] = jnp.asarray(drawn.astype(out[name].dtype))
    for name, factor in factors.items():
        out[name] = (out[name] * factor).astype(out[name].dtype)
    return out
```

```python
import math
from contextlib import ExitStack

import numpy as np

import concourse.bass as bass
import concourse.mybir as mybir

F32 = mybir.dt.float32
BF16 = mybir.dt.bfloat16
U32 = mybir.dt.uint32
ALU = mybir.AluOpType
ACT = mybir.ActivationFunctionType
AX = mybir.AxisListType

P = 128
D = 1024
KT = D // P
BANK = 512
SEQ, META = 512, 16
T = SEQ + META
HT = T // 2
DA_HEADS, DA_DIM, ROPE = 4, 64, 16
LAM_INIT = 0.8 - 0.6 * math.exp(0.0)
GLA_HEADS, GLA_RANK, GLA_TAU = 4, 16, 16.0
JT = 66
NJ = T // JT
LEAF = JT // 2
EPS, LN_EPS = 1e-6, 1e-5
PH, NK, TOPK = 8, 128, 16
PICKS = PH * TOPK
EG = 4
TC = 32
OC = 16
CTX = 256
NH2, HD2 = 8, 64
GW, ROWS, WC, WR = 64, 8, 16, 8
NBIAS = 2 * ROWS - 2
TAPS = 31
FFT_CH, FFT_G = 256, 4
KEYS2 = SEQ + CTX


class Lane:

    def __init__(self, nc, engine, name):
        self.engine, self.sem = engine, nc.alloc_semaphore(name)
        self.count, self.seen = 0, {}

    def wait(self, *signals):
        for s in signals:
            if s is None:
                continue
            if isinstance(s, list):
                self.wait(*s)
                continue
            sem, value = s
            if self.seen.get(id(sem), 0) < value:
                self.engine.wait_ge(sem, value)
                self.seen[id(sem)] = value

    def mark(self, instruction):
        instruction.then_inc(self.sem, 1)
        self.count += 1
        return (self.sem, self.count)

    @property
    def now(self):
        return (self.sem, self.count) if self.count else None


class Core:

    def __init__(self, nc):
        self.nc = nc
        self.pe = Lane(nc, nc.tensor, "pe_steps")
        self.act = Lane(nc, nc.scalar, "act_steps")
        self.dve = Lane(nc, nc.vector, "dve_steps")
        self.pool = Lane(nc, nc.gpsimd, "pool_steps")
        self.sp = Lane(nc, nc.sync, "sp_steps")
        self.psum = nc.alloc_psum_tensor("psum", [P, 8, BANK], F32)
        self.bank_free = [None] * 8
        self.dma_sems = {}

    def bank(self, i, n=BANK, m=P):
        return self.psum[0:m, i, 0:n]

    def dma(self, lane, name, out, in_, after=()):
        lane.wait(*after)
        if name not in self.dma_sems:
            self.dma_sems[name] = [self.nc.alloc_semaphore(name), 0]
        entry = self.dma_sems[name]
        lane.engine.dma_start(out, in_).then_inc(entry[0], 16)
        entry[1] += 16
        return (entry[0], entry[1])

    def fence(self):
        signals = [x.now for x in (self.pe, self.act, self.dve, self.pool)]
        for lane in (self.pe, self.act, self.dve, self.pool):
            lane.wait(*signals)


class Memory:

    def __init__(self, nc):
        self.nc, self.stack = nc, ExitStack()

    def __call__(self, name, shape, dtype=F32):
        return self.stack.enter_context(self.nc.sbuf_tensor(name, shape, dtype))

    def close(self):
        self.stack.close()


class WeightStream:
    STAGES, SPLITS = 2, 3
    SIZE = 4096

    def __init__(self, core, plan):
        nc = core.nc
        self.core, self.plan = core, plan
        self.stage = nc.alloc_sbuf_tensor("weight_stage", [P, self.STAGES, self.SIZE], F32)
        self.high = nc.alloc_sbuf_tensor("weight_high", [P, self.SPLITS, self.SIZE], BF16)
        self.low = nc.alloc_sbuf_tensor("weight_low", [P, self.SPLITS, self.SIZE], BF16)
        self.stage_free, self.used = {}, {}
        self.loaded, self.split_done = [], {}
        self.n_split = self.n_next = 0
        self.pump()
        self.split()

    def view(self, buf, slot, n):
        rows, cols = self.plan[n][1].shape[1], self.plan[n][1].shape[2]
        return buf[:, slot, 0:rows * cols].rearrange("p (r c) -> p r c", c=cols)

    def pump(self):
        while len(self.loaded) < len(self.plan):
            n = len(self.loaded)
            if n >= self.STAGES and n - self.STAGES not in self.stage_free:
                return
            slot = n % self.STAGES
            free = self.stage_free.get(n - self.STAGES, [])
            self.loaded.append(self.core.dma(self.core.sp, f"weights_in_{slot}",
                                             self.view(self.stage, slot, n), self.plan[n][1], free))

    def split(self):
        n = self.n_split
        self.n_split += 1
        if n >= len(self.plan) or self.plan[n][2]:
            return
        c, slot = self.core, n % self.SPLITS
        stage = self.view(self.stage, n % self.STAGES, n)
        high, low = self.view(self.high, slot, n), self.view(self.low, slot, n)
        free = self.used.get(n - self.SPLITS)
        c.act.wait(self.loaded[n], free)
        h = c.act.mark(c.nc.scalar.activation(high, stage, ACT.Copy))
        c.dve.wait(self.loaded[n], free, h)
        lo = c.dve.mark(c.nc.vector.tensor_tensor(low, stage, high, ALU.subtract))
        self.stage_free[n] = [h, lo]
        self.split_done[n] = lo
        self.pump()

    def next(self, name):
        n = self.n_next
        assert self.plan[n][0] == name, (self.plan[n][0], name)
        self.n_next += 1
        self.split()
        if self.plan[n][2]:
            return self.view(self.stage, n % self.STAGES, n), None, self.loaded[n]
        return (self.view(self.high, n % self.SPLITS, n), self.view(self.low, n % self.SPLITS, n),
                self.split_done[n])

    def release(self, signal):
        n = self.n_next - 1
        self.used[n] = signal
        if self.plan[n][2]:
            self.stage_free[n] = [signal]
            self.pump()


def three_products(core, out, left, right, first, last):
    pairs = ((0, 0), (0, 1), (1, 0))
    for i, (a, b) in enumerate(pairs):
        ins = core.nc.tensor.matmul(out, left[a], right[b], start=first and i == 0,
                                    stop=last and i == len(pairs) - 1)
    return ins


def split_value(core, value, high, low, after):
    core.act.wait(*after)
    h = core.act.mark(core.nc.scalar.activation(high, value, ACT.Copy))
    core.dve.wait(h, *after)
    return core.dve.mark(core.nc.vector.tensor_tensor(low, value, high, ALU.subtract))


class Net:

    def __init__(self, nc, d, out, gate_dram):
        self.nc, self.d, self.out, self.gate_dram = nc, d, out, gate_dram
        self.c = Core(nc)
        self.ring = 0


    def take(self, banks=(0, 1, 2, 3, 4, 5, 6, 7)):
        i = banks[self.ring % len(banks)]
        self.ring += 1
        self.c.pe.wait(self.c.bank_free[i])
        return i

    def take_pair(self, n=4):
        j = 2 * (self.ring % n)
        self.ring += 1
        self.c.pe.wait(self.c.bank_free[j], self.c.bank_free[j + 1])
        return j

    def free(self, i, signal):
        self.c.bank_free[i] = signal

    def pair(self, j, m=P, n=HT):
        return self.c.psum[0:m, j:j + 2, 0:n]

    def load(self, name, out, in_, after=()):
        return self.c.dma(self.c.pool, name, out, in_, after)

    def const(self, mem, name, shape):
        t = mem(name, shape)
        full = t[tuple(slice(0, n) for n in shape)]
        return t, self.load(f"in_{name}", full, self.d[name])

    def mean_square(self, square, n_tiles, n, after):
        c = self.c
        c.pe.wait(*after)
        i = self.take()
        for t in range(n_tiles):
            ins = c.nc.tensor.matmul(c.bank(i, n), self.ones[:, :], square(t),
                                     start=t == 0, stop=t == n_tiles - 1)
        return i, c.pe.mark(ins)

    def inverse_root(self, dst, banks, n, scale, eps, after):
        c = self.c
        c.act.wait(*after, c.dve.now)
        s = c.act.mark(c.nc.scalar.activation(dst, banks, ACT.Sqrt, bias=eps, scale=scale))
        c.dve.wait(s)
        return s, c.dve.mark(c.nc.vector.reciprocal(dst, dst))

    def rms(self, mem, tag, x, n, gain, after, store, shift=None, fp32_out=None):
        c, nc = self.c, self.nc
        ranges = [(0, n)] if n <= BANK else [(0, HT), (HT, n)]
        sq = mem(f"{tag}_square", [P, 2, n])
        inv = mem(f"{tag}_inverse", [P, n])
        val = mem(f"{tag}_value", [P, 2, n])
        banks = [self.take() for _ in ranges]
        free_sq = [None, None]
        for t in range(KT):
            c.act.wait(*after, free_sq[t % 2])
            s = c.act.mark(nc.scalar.activation(sq[:, t % 2, :], x[:, t, 0:n], ACT.Square))
            c.pe.wait(s)
            for b, (lo, hi) in zip(banks, ranges):
                ins = nc.tensor.matmul(c.bank(b, hi - lo), self.ones[:, :], sq[:, t % 2, lo:hi],
                                       start=t == 0, stop=t == KT - 1, skip_group_check=True)
            free_sq[t % 2] = c.pe.mark(ins)
        for b, (lo, hi) in zip(banks, ranges):
            s, last = self.inverse_root(inv[:, lo:hi], c.bank(b, hi - lo), n, 1.0 / D,
                                        self.eps[:, 0:1], [c.pe.now])
            self.free(b, s)
        done = None
        for t in range(KT):
            v = fp32_out[:, t, 0:n] if fp32_out is not None else val[:, t % 2, :]
            c.dve.wait(last, c.act.now, c.dve.now)
            s = c.dve.mark(nc.vector.scalar_tensor_tensor(v, x[:, t, 0:n], gain(t), inv[:, :],
                                                          ALU.mult, ALU.mult))
            if store is None:
                done = s
                continue
            high, low = store
            if shift is None:
                done = split_value(c, v, high[:, t, 0:n], low[:, t, 0:n], [s])
            else:
                c.act.wait(s)
                h = c.act.mark(nc.scalar.activation(high[:, t, 0:n], v, ACT.Identity,
                                                    bias=shift(t), scale=1.0))
                c.dve.wait(h, s)
                done = c.dve.mark(nc.vector.scalar_tensor_tensor(
                    low[:, t, 0:n], v, shift(t), high[:, t, 0:n], ALU.add, ALU.subtract))
        return done

    def column_product(self, out, block, cols, parts, tokens, n_k=KT, first=True, last=True, k0=0):
        high, low, _ = block
        for k in range(n_k):
            ins = three_products(self.c, out, (high[:, k, cols], low[:, k, cols]),
                                 (parts[0][:, k0 + k, tokens], parts[1][:, k0 + k, tokens]),
                                 first and k == 0, last and k == n_k - 1)
        return ins

    def token_product(self, out, block, cols, parts, tokens):
        high, low, _ = block
        for k in range(KT):
            ins = three_products(self.c, out, (parts[0][:, k, tokens], parts[1][:, k, tokens]),
                                 (high[:, k, cols], low[:, k, cols]), k == 0, k == KT - 1)
        return ins

    def linear(self, block, cols, parts, tokens, n, m, after, evacuate, **kw):
        c = self.c
        i = self.take()
        c.pe.wait(block[2], *after)
        done = c.pe.mark(self.column_product(c.bank(i, n, m), block, cols, parts, tokens, **kw))
        self.free(i, evacuate(c.bank(i, n, m), done))
        return done


    def build(self):
        c, nc, d = self.c, self.nc, self.d
        sb = nc.alloc_sbuf_tensor
        plan = []

        def weights(name, src, raw=False):
            plan.append((name, src, raw))

        w_in = d["w_in"].rearrange("(t p) n -> p t n", p=P)
        for name, lo, hi in (("z", 3072, 3104), ("gla_qk", 1536, 2048), ("gla_v", 2048, 2560),
                             ("gla_r", 2560, 3072), ("da_q", 0, 512), ("da_k", 512, 1024),
                             ("da_v", 1024, 1536)):
            weights(name, w_in[:, :, lo:hi])
        for g in range(2):
            weights("w_out", d["w_out"].rearrange("(t p) n -> p t n", p=P)[:, :, BANK * g:BANK * (g + 1)])
        for g in range(4):
            weights("peer_q", d["peer_w_q"].rearrange("(t p) n -> p t n", p=P)[:, :, BANK * g:BANK * (g + 1)])
        for g in range(NK // EG):
            weights("u", d["peer_u"][g].rearrange("p (t e) -> p t e", t=KT))
            weights("v", d["peer_v"][EG * g:EG * (g + 1)].rearrange("b p n -> p b n"))
        for g in range(12):
            weights("ada", d["ada_w"].rearrange("(t p) n -> p t n", p=P)[:, :, BANK * g:BANK * (g + 1)], True)
        w_in2 = d["w_in_2"].rearrange("(t p) n -> p t n", p=P)
        for name, lo, hi in (("k2", 1280, 1792), ("v2", 1792, 2304), ("q2", 768, 1280),
                             ("fourier_in", 0, 256), ("conv_in", 256, 768)):
            weights(name, w_in2[:, :, lo:hi])
        for g in range(2):
            weights("w_out_2", d["w_out_2"].rearrange("(t p) n -> p t n", p=P)[:, :, BANK * g:BANK * (g + 1)])
        for g in range(8):
            weights("mlp_1", d["mlp_w1"].rearrange("(t p) n -> p t n", p=P)[:, :, BANK * g:BANK * (g + 1)])
        for g in range(8):
            weights("mlp_2", d["mlp_w2"].rearrange("(t p) n -> p t n", p=P)[:, 4 * g:4 * g + 4, :])

        self.ones = sb("ones", [P, P], F32)
        self.ident = sb("identity", [P, P], F32)
        self.eps = sb("eps", [P, 2], F32)
        self.cols = sb("columns", [P, d["columns"].shape[1]], F32)
        c.pool.mark(nc.gpsimd.memset(self.ones[:, :], 1.0))
        c.pool.mark(nc.gpsimd.memset(self.eps[:, 0:1], EPS))
        c.pool.mark(nc.gpsimd.memset(self.eps[:, 1:2], LN_EPS))
        ready = [c.pool.now, self.load("in_identity", self.ident[:, :], d["identity"]),
                 self.load("in_columns", self.cols[:, :], d["columns"])]
        self.h = sb("residual", [P, KT, SEQ], F32)
        self.x_high = sb("x_high", [P, KT, T], BF16)
        self.x_low = sb("x_low", [P, KT, T], BF16)
        for lane in (c.pe, c.act, c.dve, c.pool):
            lane.wait(*ready)

        self.w = WeightStream(c, plan)
        self.mixer()
        self.experts()
        self.second()

    def col(self, name, t=0):
        at = COLUMNS[name] + t
        return self.cols[:, at:at + 1]


    def mixer(self):
        c, nc, d = self.c, self.nc, self.d
        parts = (self.x_high, self.x_low)
        outer = Memory(nc)
        z = outer("z", [2 * GLA_RANK, T])
        gqk = outer("gla_qk", [P, 4, T])
        gv = outer("gla_v", [JT, NJ, 512])
        gr, silu = self.h[:, 0:4, :], self.h[:, 4:8, :]
        da = Memory(nc)
        dq = da("da_q", [P, 4, SEQ])
        dk = da("da_k", [P, 4, T])
        dv = da("da_v", [P, 5, 512])

        first = Memory(nc)
        h0 = first("tokens_in", [P, KT, T])
        landed = self.load("in_tokens", h0[:, :, :], d["tokens"])
        xn = self.rms(first, "norm1", h0, T, lambda t: self.col("ln1", t), [landed], parts)
        c.fence()
        first.close()
        c.fence()

        def keep(lane, dst, scale=1.0):
            def evacuate(psum, done):
                lane.wait(done)
                if lane is c.act:
                    return lane.mark(nc.scalar.activation(dst, psum, ACT.Identity, scale=scale))
                return lane.mark(nc.vector.tensor_scalar(dst, psum, scale, None, ALU.mult))
            return evacuate

        def full_columns(name, dst, n_tiles, m, scales):
            block = self.w.next(name)
            for f in range(n_tiles):
                for g in range(2):
                    tokens = slice(HT * g, HT * (g + 1))
                    lane = c.act if (f + g) % 2 else c.dve
                    done = self.linear(block, slice(P * f, P * f + m), parts, tokens, HT, m, [xn],
                                       keep(lane, dst(f)[:, tokens], scales[f]))
            self.w.release(done)

        def seq_columns(name, dst):
            block = self.w.next(name)
            for f in range(4):
                lane = c.act if f % 2 else c.dve
                done = self.linear(block, slice(P * f, P * (f + 1)), parts, slice(META, T), SEQ, P,
                                   [xn], keep(lane, dst[:, f, :]))
            self.w.release(done)

        def rows(name, dst, step):
            block = self.w.next(name)
            for j in range(-(-T // step)):
                m = min(step, T - step * j)
                i = self.take()
                c.pe.wait(block[2], xn)
                done = c.pe.mark(self.token_product(c.bank(i, 512, m), block, slice(0, 512), parts,
                                                    slice(step * j, step * j + m)))
                self.free(i, keep(c.act if j % 2 else c.dve, dst[0:m, j, :])(c.bank(i, 512, m), done))
            self.w.release(done)

        full_columns("z", lambda f: z, 1, 2 * GLA_RANK, [1.0])
        full_columns("gla_qk", lambda f: gqk[:, f, :], 4, P, [0.125, 0.125, 1.0, 1.0])
        rows("gla_v", gv, JT)
        seq_columns("gla_r", gr)
        seq_columns("da_q", dq)
        full_columns("da_k", lambda f: dk[:, f, :], 4, P, [1.0] * 4)
        rows("da_v", dv, P)
        mixed_free = c.pe.now
        projected = [c.act.now, c.dve.now]
        c.fence()
        self.attention(dq, dk, dv, projected)
        da.close()
        self.linear_attention(z, gqk, gv, gr, silu, projected, mixed_free)
        c.fence()

        late = Memory(nc)
        landed = self.load("in_residual", self.h[:, :, :], d["tokens"][:, :, META:T])
        mixed = c.dve.now
        for g in range(2):
            block = self.w.next("w_out")
            for f in range(4):
                t = 4 * g + f

                def add(psum, done, t=t):
                    c.dve.wait(done, landed)
                    return c.dve.mark(nc.vector.tensor_tensor(self.h[:, t, :], psum, self.h[:, t, :],
                                                              ALU.add))
                done = self.linear(block, slice(P * f, P * (f + 1)), parts, slice(0, SEQ), SEQ, P,
                                   [mixed], add)
            self.w.release(done)
        c.fence()
        late.close()
        outer.close()

    def head_norm(self, mem, tag, o, dst, gain, after, extra=None):
        c, nc = self.c, self.nc
        sq, inv = mem[0], mem[1]
        c.act.wait(*after, c.dve.now, c.pe.now)
        s = c.act.mark(nc.scalar.activation(sq[:, :], o, ACT.Square))
        i, summed = self.mean_square(lambda t: sq[:, :], 1, SEQ, [s])
        s, last = self.inverse_root(inv[:, :], c.bank(i), SEQ, 1.0 / P, self.eps[:, 0:1], [summed])
        self.free(i, s)
        c.dve.wait(last)
        s = c.dve.mark(nc.vector.scalar_tensor_tensor(sq[:, :], o, gain, inv[:, :], ALU.mult, ALU.mult))
        if extra is not None:
            c.dve.wait(s)
            s = c.dve.mark(nc.vector.tensor_tensor(sq[:, :], sq[:, :], extra, ALU.mult))
        return split_value(c, sq[:, :], self.x_high[:, dst, 0:SEQ], self.x_low[:, dst, 0:SEQ], [s])

    def linear_attention(self, z, gqk, gv, gr, silu, projected, mixed_free):
        c, nc, d = self.c, self.nc, self.d
        mem = Memory(nc)
        w2, w2_in = self.const(mem, "gate_w2", [2 * GLA_RANK, 512])
        masks, masks_in = self.const(mem, "leaf_masks", [JT, 4, JT])
        total = mem("decay_sum", [P, 2, 2, T + 1])
        gate = Memory(nc)
        logit = gate("gate_logit", [P, T])
        soft = gate("gate_soft", [P, T])
        ones_row = gate("ones_row", [P, T])
        s = c.dve.mark(nc.vector.memset(ones_row[:, :], 1.0))
        zero = c.dve.mark(nc.vector.memset(total[:, :, :, 0:1], 0.0))
        c.pe.wait(w2_in, *projected)
        for g in range(4):
            for h in range(2):
                i = self.take()
                done = c.pe.mark(nc.tensor.matmul(c.bank(i, HT), w2[:, P * g:P * (g + 1)],
                                                  z[:, HT * h:HT * (h + 1)], start=True, stop=True))
                c.act.wait(done, c.dve.now)
                self.free(i, c.act.mark(nc.scalar.activation(
                    logit[:, HT * h:HT * (h + 1)], c.bank(i, HT), ACT.Identity,
                    bias=self.col("gate_b", g), scale=1.0)))
            c.act.wait(c.act.now)
            c.act.mark(nc.scalar.activation(soft[:, :], logit[:, :], ACT.Abs))
            c.act.wait(c.act.now)
            c.act.mark(nc.scalar.activation(soft[:, :], soft[:, :], ACT.Exp, scale=-1.0))
            c.act.wait(c.act.now)
            s = c.act.mark(nc.scalar.activation(soft[:, :], soft[:, :], ACT.Ln, bias=self.ones[:, 0:1],
                                                scale=1.0))
            c.dve.wait(s, c.dve.now)
            s = c.dve.mark(nc.vector.scalar_tensor_tensor(soft[:, :], logit[:, :], 0.0, soft[:, :],
                                                          ALU.min, ALU.subtract))
            c.dve.wait(s)
            s = c.dve.mark(nc.vector.tensor_tensor_scan(total[:, g // 2, g % 2, 1:T + 1], ones_row[:, :],
                                                        soft[:, :], 0.0, ALU.mult, ALU.add))
        c.fence()
        gate.close()

        levels = [4 * JT, 2 * JT, JT, LEAF]
        both = [[mem(f"half_{s}_{r}", [P, 2, T]) for r in range(2)] for s in levels]
        leaf = [[mem(f"leaf_{r}_{w}", [P, 2, T]) for w in range(2)] for r in range(2)]
        step = mem("decay_step", [P, 2, T])
        q, k = gqk[:, 0:2, :], gqk[:, 2:4, :]
        inv_tau = 1.0 / GLA_TAU
        for r in range(2):
            run = total[:, r, :, 1:T + 1] if r == 0 else total[:, r, :, 0:T]
            for s, dst in zip(levels, both):
                dst = dst[r]
                nb = T // (2 * s)
                mid = s - 1 if r == 0 else s
                rv = run.rearrange("p a (b n) -> p a b n", n=2 * s)
                c.dve.wait(c.act.now, c.dve.now)
                for a in range(2):
                    x = c.dve.mark(nc.vector.tensor_tensor(
                        step[:, a, :].rearrange("p (b n) -> p b n", n=2 * s), rv[:, a, :, :],
                        rv[:, a, :, mid:mid + 1].to_broadcast([P, nb, 2 * s]), ALU.subtract))
                sign_left = -inv_tau
                sign_right = inv_tau
                c.act.wait(x)
                for a in range(2):
                    sv = step[:, a, :].rearrange("p (b n) -> p b n", n=2 * s)
                    dvw = dst[:, a, :].rearrange("p (b n) -> p b n", n=2 * s)
                    c.act.mark(nc.scalar.activation(dvw[:, :, 0:s], sv[:, :, 0:s], ACT.Exp, scale=sign_left))
                    e = c.act.mark(nc.scalar.activation(dvw[:, :, s:2 * s], sv[:, :, s:2 * s], ACT.Exp,
                                                        scale=sign_right))
                c.dve.wait(e)
                for a in range(2):
                    for side, src in ((0, k if r == 0 else q), (1, q if r == 0 else k)):
                        dvw = dst[:, a, :].rearrange("p (b n) -> p b n", n=2 * s)[:, :, side * s:(side + 1) * s]
                        svw = src[:, a, :].rearrange("p (b n) -> p b n", n=2 * s)[:, :, side * s:(side + 1) * s]
                        c.dve.mark(nc.vector.tensor_tensor(dvw, dvw, svw, ALU.mult))
            mid = LEAF // 2
            rv = run.rearrange("p a (b n) -> p a b n", n=LEAF)
            c.dve.wait(c.act.now, c.dve.now)
            for a in range(2):
                x = c.dve.mark(nc.vector.tensor_tensor(
                    step[:, a, :].rearrange("p (b n) -> p b n", n=LEAF), rv[:, a, :, :],
                    rv[:, a, :, mid:mid + 1].to_broadcast([P, T // LEAF, LEAF]), ALU.subtract))
            c.act.wait(x)
            sign = inv_tau if r == 0 else -inv_tau
            c.act.mark(nc.scalar.activation(leaf[r][0][:, :, :], step[:, :, :], ACT.Exp, scale=sign))
            e = c.act.mark(nc.scalar.activation(leaf[r][1][:, :, :], step[:, :, :], ACT.Exp, scale=-sign))
            c.dve.wait(e)
            c.dve.mark(nc.vector.tensor_tensor(leaf[r][0][:, :, :], leaf[r][0][:, :, :], q, ALU.mult))
            c.dve.mark(nc.vector.tensor_tensor(leaf[r][1][:, :, :], leaf[r][1][:, :, :], k, ALU.mult))
        scaled = c.dve.now

        groups = []
        for r in range(2):
            a = both[0][r]
            for g in range(2):
                groups.append(([(4 * r + 2 * g + x, HT * (1 - r), HT, a, a) for x in range(2)], None))
        for r in range(2):
            a = both[1][r]
            groups.append(([(4 * b + 2 * r + x, 4 * JT * b + 2 * JT * (1 - r), 2 * JT, a, a)
                            for b in range(2) for x in range(2)], None))
        groups.append(([(2 * b + r, JT * (2 * b + 1 - r), JT, both[2][r], both[2][r])
                        for r in range(2) for b in range(4)], None))
        for r in range(2):
            groups.append(([(j, JT * j, JT, both[3][r], both[3][r]) for j in range(NJ)], r))
        for r in range(2):
            groups.append(([(j, JT * j, JT, leaf[r][1], leaf[r][0]) for j in range(NJ)], 2 + r))

        weight = step[0:JT, :, :]
        o = total[:, 0, 0, 0:T]
        norm = (total[:, 0, 1, 0:SEQ], total[:, 1, 0, 0:SEQ])
        c.act.wait(scaled)
        c.act.wait(*projected)
        silu_done = c.act.mark(nc.scalar.activation(silu[:, :, :], gr[:, :, :], ACT.Silu))
        c.pe.wait(scaled, masks_in)
        c.dve.wait(masks_in)
        weight_free = [None, None]
        n_group = 0
        for head in range(GLA_HEADS):
            a, at = head // 2, 64 * (head % 2)
            rows = slice(at, at + 64)
            c.pe.wait(c.bank_free[6], c.bank_free[7])
            started = [False, False]
            total_left = sum(len(p) for p, _ in groups)
            pending = None

            def apply(pending):
                pieces, slot, ready = pending
                c.pe.wait(ready)
                nonlocal_left = None
                for n, (jt, i0, ni, _, _) in enumerate(pieces):
                    half = i0 // HT
                    ins = nc.tensor.matmul(
                        self.c.psum[:, 6 + half, i0 - HT * half:i0 - HT * half + ni],
                        gv[:, jt, P * head:P * (head + 1)], weight[:, slot, ni * n:ni * (n + 1)],
                        start=not started[half], stop=True, skip_group_check=True)
                    started[half] = True
                weight_free[slot] = c.pe.mark(ins)

            for pieces, mask in groups:
                slot = n_group % 2
                n_group += 1
                j = self.take_pair(3)
                for n, (jt, i0, ni, ka, qa) in enumerate(pieces):
                    ins = nc.tensor.matmul(
                        self.c.psum[0:JT, j + ni * n // HT, ni * n % HT:ni * n % HT + ni],
                        ka[rows, a, JT * jt:JT * (jt + 1)], qa[rows, a, i0:i0 + ni],
                        start=True, stop=True, skip_group_check=True)
                done = c.pe.mark(ins)
                dst = weight[:, slot, :].rearrange("p (b n) -> p b n", n=HT)
                if mask is None:
                    lane = c.act if slot else c.dve
                    lane.wait(done, weight_free[slot])
                    if lane is c.act:
                        ready = c.act.mark(nc.scalar.activation(dst, self.pair(j, JT), ACT.Copy))
                    else:
                        ready = c.dve.mark(nc.vector.tensor_copy(dst, self.pair(j, JT)))
                else:
                    c.dve.wait(done, weight_free[slot])
                    for half in range(2):
                        ready = c.dve.mark(nc.vector.tensor_tensor(
                            dst[:, half, :].rearrange("p (a n) -> p a n", n=JT),
                            self.c.psum[0:JT, j + half, 0:HT].rearrange("p (a n) -> p a n", n=JT),
                            masks[:, mask:mask + 1, :].to_broadcast([JT, HT // JT, JT]), ALU.mult))
                self.free(j, ready)
                self.free(j + 1, ready)
                if pending:
                    apply(pending)
                pending = (pieces, slot, ready)
            apply(pending)
            c.act.wait(c.pe.now, c.dve.now)
            got = c.act.mark(nc.scalar.activation(o.rearrange("p (b n) -> p b n", n=HT),
                                                  self.pair(6), ACT.Copy))
            self.free(6, got)
            self.free(7, got)
            c.act.wait(mixed_free)
            c.dve.wait(mixed_free, silu_done, got)
            self.head_norm(norm, "gla", o[:, META:T], DA_HEADS + head, self.col("gla_norm"), [got],
                           silu[:, head, :])
        c.fence()
        mem.close()

    def attention(self, dq, dk, dv, projected):
        c, nc, d = self.c, self.nc, self.d
        mem = Memory(nc)
        cos, cos_in = self.const(mem, "rope_cos", [P, T])
        sin, sin_in = self.const(mem, "rope_sin", [P, T])
        swap, swap_in = self.const(mem, "rope_swap", [P, P])
        lam4, lam_in = self.const(mem, "lambdas", [DA_DIM, 4])
        turned = mem("rope_turned", [P, SEQ])
        lam = mem("lambda", [P, 4])

        c.dve.wait(lam_in)
        s = c.dve.mark(nc.vector.tensor_tensor(lam4[:, 0:2], lam4[:, 0:2], lam4[:, 2:4], ALU.mult))
        c.pe.wait(s)
        i = self.take()
        s = c.pe.mark(nc.tensor.matmul(c.bank(i, 2), self.ones[0:DA_DIM, :], lam4[:, 0:2], start=True, stop=True))
        c.act.wait(s)
        s = c.act.mark(nc.scalar.activation(lam[:, 0:2], c.bank(i, 2), ACT.Exp))
        self.free(i, s)
        c.dve.wait(s)
        s = c.dve.mark(nc.vector.tensor_tensor(lam[:, 2:3], lam[:, 1:2], lam[:, 0:1], ALU.subtract))
        c.dve.wait(s)
        c.dve.mark(nc.vector.tensor_scalar(lam[:, 3:4], lam[:, 2:3], -LAM_INIT, None, ALU.add))

        c.pe.wait(swap_in, *projected)
        c.dve.wait(cos_in, sin_in)
        for x, n0 in ((dq, META), (dk, 0)):
            n_all = T - n0
            ranges = [(0, SEQ)] if n_all == SEQ else [(0, HT), (HT, T)]
            for h in range(DA_HEADS):
                for lo, hi in ranges:
                    i = self.take()
                    done = c.pe.mark(nc.tensor.matmul(c.bank(i, hi - lo), swap[:, :], x[:, h, lo:hi],
                                                      start=True, stop=True))
                    c.dve.wait(done, c.dve.now)
                    s = c.dve.mark(nc.vector.tensor_tensor(turned[:, 0:hi - lo], c.bank(i, hi - lo),
                                                           sin[:, n0 + lo:n0 + hi], ALU.mult))
                    self.free(i, s)
                    s = c.dve.mark(nc.vector.tensor_tensor(x[:, h, lo:hi], x[:, h, lo:hi],
                                                           cos[:, n0 + lo:n0 + hi], ALU.mult))
                    c.dve.wait(s)
                    s = c.dve.mark(nc.vector.tensor_tensor(x[:, h, lo:hi], x[:, h, lo:hi],
                                                           turned[:, 0:hi - lo], ALU.add))
        rotated = c.dve.now

        e = mem("exp_scores", [P, 2, 2, T])
        stat = mem("softmax_stats", [P, 2, 8])
        mix = mem("mixed_scores", [P, 2, T])
        mix_t = mem("mixed_scores_t", [P, 2, 5, P])
        o = mem("da_out", [P, SEQ])
        norm = (mem("da_square", [P, SEQ]), mem("da_inverse", [P, SEQ]))
        scale = DA_DIM ** -0.5
        steps = [(h, qt) for h in range(DA_HEADS) for qt in range(SEQ // P)]
        key_tiles = [(t, min(P, T - P * t)) for t in range(5)]
        c.pe.wait(rotated)
        mixed_at, turned_at, applied_at = {}, {}, {}
        self.ring = 0

        def scores(n):
            h, qt = steps[n]
            v = n % 2
            for m in range(2):
                rows = slice(64 * m, 64 * m + 64)
                j = 2 * m
                c.pe.wait(c.bank_free[j], c.bank_free[j + 1])
                for g in range(2):
                    ins = nc.tensor.matmul(c.bank(j + g, HT), dq[rows, h, P * qt:P * (qt + 1)],
                                           dk[rows, h, HT * g:HT * (g + 1)], start=True, stop=True)
                done = c.pe.mark(ins)
                st = stat[:, v, :]
                c.dve.wait(done, mixed_at.get(n - 2))
                s = c.dve.mark(nc.vector.tensor_reduce(st[:, m:m + 1], self.pair(j), AX.XY, ALU.max))
                c.dve.wait(s)
                s = c.dve.mark(nc.vector.tensor_scalar(st[:, 2 + m:3 + m], st[:, m:m + 1], -scale, None, ALU.mult))
                c.act.wait(s, mixed_at.get(n - 2))
                s = c.act.mark(nc.scalar.activation(
                    e[:, v, m, :].rearrange("p (b n) -> p b n", n=HT), self.pair(j), ACT.Exp,
                    bias=st[:, 2 + m:3 + m], scale=scale, accum_out=st[:, 4 + m:5 + m]))
                self.free(j, s)
                self.free(j + 1, s)
            return s

        def mixing(n, exped):
            v = n % 2
            st = stat[:, v, :]
            c.dve.wait(exped, turned_at.get(n - 2))
            s = c.dve.mark(nc.vector.reciprocal(st[:, 6:8], st[:, 4:6]))
            c.dve.wait(s)
            s = c.dve.mark(nc.vector.tensor_scalar(st[:, 7:8], st[:, 7:8], lam[:, 3:4], None, ALU.mult))
            s = c.dve.mark(nc.vector.tensor_scalar(mix[:, v, :], e[:, v, 0, :], st[:, 6:7], None, ALU.mult))
            c.dve.wait(s)
            mixed_at[n] = c.dve.mark(nc.vector.scalar_tensor_tensor(
                mix[:, v, :], e[:, v, 1, :], st[:, 7:8], mix[:, v, :], ALU.mult, ALU.add))

        def applying(n):
            h, qt = steps[n]
            v = n % 2
            c.pe.wait(mixed_at[n], c.bank_free[4], c.bank_free[5])
            for t, m in key_tiles:
                bank, off = (4, P * t) if t < 4 else (5, 0)
                ins = nc.tensor.transpose(self.c.psum[0:m, bank, off:off + P], mix[:, v, P * t:P * t + m],
                                          self.ident[:, :])
            turned_at[n] = c.pe.mark(ins)
            c.act.wait(turned_at[n], applied_at.get(n - 2))
            s = c.act.mark(nc.scalar.activation(mix_t[:, v, 0:4, :].rearrange("p a b -> p (a b)"),
                                                c.bank(4), ACT.Copy))
            self.free(4, s)
            s = c.act.mark(nc.scalar.activation(mix_t[0:META, v, 4, :], c.bank(5, P, META), ACT.Copy))
            self.free(5, s)
            c.pe.wait(s)
            if qt == 0:
                c.pe.wait(c.bank_free[6])
            for t, m in key_tiles:
                ins = nc.tensor.matmul(self.c.psum[:, 6, P * qt:P * (qt + 1)], dv[0:m, t, P * h:P * (h + 1)],
                                       mix_t[0:m, v, t, :], start=t == 0, stop=t == 4)
            applied_at[n] = c.pe.mark(ins)
            if qt == SEQ // P - 1:
                c.act.wait(applied_at[n], c.dve.now)
                got = c.act.mark(nc.scalar.activation(o[:, :], c.bank(6), ACT.Copy))
                self.free(6, got)
                self.ring = 7
                self.head_norm(norm, "da", o[:, :], h, self.gain_da, [got])

        gain = mem("da_gain", [P, 1])
        c.dve.wait(c.dve.now)
        s = c.dve.mark(nc.vector.tensor_scalar(gain[:, :], self.col("da_norm"), 1.0 - LAM_INIT, None, ALU.mult))
        self.gain_da = gain[:, 0:1]
        for n in range(len(steps) + 1):
            if n < len(steps):
                exped = scores(n)
            if n >= 1:
                applying(n - 1)
            if n < len(steps):
                mixing(n, exped)
        c.fence()
        mem.close()


    def experts(self):
        c, nc, d = self.c, self.nc, self.d
        parts = (self.x_high, self.x_low)
        mem = Memory(nc)
        xn = self.rms(mem, "norm2", self.h, SEQ, lambda t: self.col("ln2", t), [c.dve.now], parts)
        c.fence()
        mem.close()
        self.route(parts, xn)

        mem = Memory(nc)
        acc = mem("expert_sum", [P, KT, SEQ])
        gates = mem("gates", [P, 2, SEQ // TC, EG, TC])
        act = mem("expert_act", [P, 2, SEQ])
        hid_high = mem("hidden_high", [P, 2, EG, SEQ], BF16)
        hid_low = mem("hidden_low", [P, 2, EG, SEQ], BF16)
        n_groups = NK // EG
        gates_in, gates_free, hidden, hidden_free = {}, {}, {}, {}
        act_free = [None, None]

        def load_gates(g):
            gates_in[g] = self.load(f"gates_in_{g % 2}", gates[:, g % 2, :, :, :],
                                    self.gate_dram[:, :, EG * g:EG * (g + 1), :].rearrange("c p b n -> p c b n"),
                                    [self.gates_written, gates_free.get(g - 2)])

        load_gates(0)
        load_gates(1)

        def up(g):
            block = self.w.next("u")
            for b in range(EG):
                def evacuate(psum, done, b=b):
                    slot = b % 2
                    c.act.wait(done, act_free[slot])
                    s = c.act.mark(nc.scalar.activation(act[:, slot, :], psum, ACT.Gelu))
                    c.dve.wait(s, gates_in[g])
                    v = act[:, slot, :].rearrange("p (c n) -> p c n", n=TC)
                    w = c.dve.mark(nc.vector.tensor_tensor(v, v, gates[:, g % 2, :, b, :], ALU.mult))
                    act_free[slot] = hidden[g] = split_value(
                        c, act[:, slot, :], hid_high[:, g % 2, b, :], hid_low[:, g % 2, b, :],
                        [w, hidden_free.get(g - 2)])
                    gates_free[g] = w
                    return s
                done = self.linear(block, slice(P * b, P * (b + 1)), parts, slice(0, SEQ), SEQ, P,
                                   [xn], evacuate)
            self.w.release(done)

        def down(g):
            block = self.w.next("v")
            c.pe.wait(block[2], hidden[g])
            for t in range(KT):
                i = self.take()
                for b in range(EG):
                    ins = three_products(c, c.bank(i), (block[0][:, b, P * t:P * (t + 1)],
                                                        block[1][:, b, P * t:P * (t + 1)]),
                                         (hid_high[:, g % 2, b, :], hid_low[:, g % 2, b, :]),
                                         b == 0, b == EG - 1)
                done = c.pe.mark(ins)
                c.dve.wait(done)
                if g == 0:
                    s = c.dve.mark(nc.vector.tensor_copy(acc[:, t, :], c.bank(i)))
                else:
                    c.dve.wait(self.acc_at[t])
                    s = c.dve.mark(nc.vector.tensor_tensor(acc[:, t, :], c.bank(i), acc[:, t, :], ALU.add))
                self.acc_at[t] = s
                self.free(i, s)
            hidden_free[g] = done
            self.w.release(done)

        self.acc_at = [None] * KT
        for g in range(n_groups):
            up(g)
            if g + 2 < n_groups:
                load_gates(g + 2)
            down(g)
        for t in range(KT):
            c.dve.wait(self.acc_at[t])
            s = c.dve.mark(nc.vector.tensor_tensor(self.h[:, t, :], self.h[:, t, :], acc[:, t, :], ALU.add))
        c.fence()
        mem.close()

    def route(self, parts, xn):
        c, nc, d = self.c, self.nc, self.d
        mem = Memory(nc)
        keys, keys_in = self.const(mem, "sub_keys", [P, 2 * PH, NK])
        iota16, iota16_in = self.const(mem, "iota_picks", [P, TOPK])
        pick_t = mem("picks_t", [P, 3, SEQ])
        pick_b = mem("picks_t_bf16", [P, 4, SEQ], BF16)

        top = Memory(nc)
        score = top("scores", [P, SEQ // P, 2 * PH, NK])
        query = top("queries", [P, 2, SEQ])
        query_free = [None, None]
        c.pe.wait(keys_in)
        for g in range(4):
            block = self.w.next("peer_q")
            for f in range(4):
                hp = 4 * g + f
                got = {}

                def keep(psum, done, hp=hp):
                    c.act.wait(done, query_free[hp % 2])
                    got[0] = c.act.mark(nc.scalar.activation(query[:, hp % 2, :], psum, ACT.Copy))
                    return got[0]
                done = self.linear(block, slice(P * f, P * (f + 1)), parts, slice(0, SEQ), SEQ, P,
                                   [xn], keep)
                i = self.take()
                c.pe.wait(got[0])
                for t in range(SEQ // P):
                    ins = nc.tensor.matmul(self.c.psum[:, i, NK * t:NK * (t + 1)],
                                           query[:, hp % 2, P * t:P * (t + 1)], keys[:, hp, :],
                                           start=True, stop=True)
                query_free[hp % 2] = c.pe.mark(ins)
                c.act.wait(query_free[hp % 2])
                s = c.act.mark(nc.scalar.activation(score[:, :, hp, :],
                                                    c.bank(i).rearrange("p (t k) -> p t k", k=NK), ACT.Copy))
                self.free(i, s)
            self.w.release(query_free[hp % 2])
        scored = c.act.now

        best = top("best_side", [P, 2 * PH, TOPK])
        best_i = top("best_side_index", [P, 2 * PH, TOPK], U32)
        best_f = top("best_side_index_f", [P, 2 * PH, TOPK])
        cand = top("pair_scores", [P, PH, TOPK, TOPK])
        pair = top("best_pair", [P, PH, TOPK])
        shifted = top("best_pair_shifted", [P, PH, TOPK])
        pair_i = top("best_pair_index", [P, PH, TOPK], U32)
        rank_i = top("best_rank_index", [P, 2, PH, TOPK], U32)
        rank = top("best_rank", [P, 2, PH, TOPK])
        hot = top("rank_hot", [P, PH, TOPK, TOPK])
        pick = top("picks", [P, 3, PICKS])
        tot = top("gate_sum", [P, 2, PH])
        LOW = -3.0e38
        c.dve.wait(scored, iota16_in)

        def top16(values, out, index):
            s = c.dve.mark(nc.vector.max(out[:, 0:8], values))
            c.dve.wait(s)
            c.dve.mark(nc.vector.max_index(index[:, 0:8], out[:, 0:8], values))
            c.dve.wait(c.dve.now)
            s = c.dve.mark(nc.vector.match_replace(values, out[:, 0:8], values, LOW))
            c.dve.wait(s)
            s = c.dve.mark(nc.vector.max(out[:, 8:16], values))
            c.dve.wait(s)
            c.dve.mark(nc.vector.max_index(index[:, 8:16], out[:, 8:16], values))

        for t in range(SEQ // P):
            c.dve.wait(c.dve.now, c.act.now)
            for hp in range(2 * PH):
                top16(score[:, t, hp, :], best[:, hp, :], best_i[:, hp, :])
            c.dve.wait(c.dve.now)
            c.dve.mark(nc.vector.tensor_copy(best_f[:, :, :], best_i[:, :, :]))
            sides = best[:, :, :].rearrange("p (h s) k -> p h s k", s=2)
            for h in range(PH):
                c.dve.mark(nc.vector.tensor_tensor(
                    cand[:, h, :, :], sides[:, h, 0, :].unsqueeze(2).to_broadcast([P, TOPK, TOPK]),
                    sides[:, h, 1, :].unsqueeze(1).to_broadcast([P, TOPK, TOPK]), ALU.add))
            c.dve.wait(c.dve.now)
            for h in range(PH):
                top16(cand[:, h, :, :].rearrange("p a b -> p (a b)"), pair[:, h, :], pair_i[:, h, :])
            c.dve.wait(c.dve.now)
            s = c.dve.mark(nc.vector.tensor_tensor(shifted[:, :, :], pair[:, :, :],
                                                   pair[:, :, 0:1].to_broadcast([P, PH, TOPK]), ALU.subtract))
            c.dve.mark(nc.vector.tensor_scalar(rank_i[:, 0, :, :], pair_i[:, :, :], 4, None,
                                               ALU.logical_shift_right))
            c.dve.mark(nc.vector.tensor_scalar(rank_i[:, 1, :, :], pair_i[:, :, :], 15, None, ALU.bitwise_and))
            c.act.wait(s)
            gate = pick[:, 2, :].rearrange("p (h k) -> p h k", k=TOPK)
            e = c.act.mark(nc.scalar.activation(gate, shifted[:, :, :], ACT.Exp))
            c.dve.wait(c.dve.now, e)
            c.dve.mark(nc.vector.tensor_reduce(tot[:, 0, :], gate, AX.X, ALU.add))
            c.dve.mark(nc.vector.tensor_copy(rank[:, :, :, :], rank_i[:, :, :, :]))
            c.dve.wait(c.dve.now)
            c.dve.mark(nc.vector.reciprocal(tot[:, 1, :], tot[:, 0, :]))
            c.dve.wait(c.dve.now)
            c.dve.mark(nc.vector.tensor_tensor(gate, gate, tot[:, 1, :].unsqueeze(2).to_broadcast([P, PH, TOPK]),
                                               ALU.mult))
            bf = best_f[:, :, :].rearrange("p (h s) k -> p h s k", s=2)
            for side in range(2):
                for h in range(PH):
                    c.dve.mark(nc.vector.tensor_tensor(
                        hot[:, h, :, :], rank[:, side, h, :].unsqueeze(2).to_broadcast([P, TOPK, TOPK]),
                        iota16[:, :].unsqueeze(1).to_broadcast([P, TOPK, TOPK]), ALU.is_equal))
                c.dve.wait(c.dve.now)
                for h in range(PH):
                    c.dve.mark(nc.vector.tensor_tensor(
                        hot[:, h, :, :], hot[:, h, :, :],
                        bf[:, h, side, :].unsqueeze(1).to_broadcast([P, TOPK, TOPK]), ALU.mult))
                c.dve.wait(c.dve.now)
                s = c.dve.mark(nc.vector.tensor_reduce(
                    pick[:, side, :].rearrange("p (h k) -> p h k", k=TOPK), hot[:, :, :, :], AX.X, ALU.add))
                c.dve.wait(s)
            i = self.take()
            c.pe.wait(c.dve.now)
            for x in range(3):
                ins = nc.tensor.transpose(self.c.psum[:, i, P * x:P * (x + 1)], pick[:, x, :], self.ident[:, :])
            done = c.pe.mark(ins)
            c.act.wait(done)
            s = c.act.mark(nc.scalar.activation(pick_t[:, :, P * t:P * (t + 1)],
                                                c.bank(i, 3 * P).rearrange("p (x n) -> p x n", n=P), ACT.Copy))
            self.free(i, s)
        c.dve.wait(c.act.now)
        c.dve.mark(nc.vector.tensor_copy(pick_b[:, 0:3, :], pick_t[:, :, :]))
        c.dve.wait(c.dve.now)
        c.dve.mark(nc.vector.tensor_tensor(pick_b[:, 3, :], pick_t[:, 2, :], pick_b[:, 2, :], ALU.subtract))
        c.fence()
        top.close()

        hot_mem = Memory(nc)
        iota32, iota_in = self.const(hot_mem, "iota_keys", [P, NK])
        iota = hot_mem("iota_bf16", [P, NK, OC], BF16)
        left = hot_mem("one_hot_a", [P, 2, NK, OC], BF16)
        right = hot_mem("one_hot_b", [P, 2, NK, OC], BF16)
        gated = hot_mem("gated_one_hot_b", [P, 2, 2, NK, OC], BF16)
        mats = hot_mem("gate_matrices", [P, 2, NK, TC])
        hot_free, mats_out = {}, {}
        c.dve.wait(c.dve.now, iota_in)
        s = c.dve.mark(nc.vector.tensor_copy(iota[:, :, :], iota32[:, :].unsqueeze(2).to_broadcast([P, NK, OC])))
        c.dve.wait(s)
        for n in range(SEQ // OC):
            v = n % 2
            tok = slice(OC * n, OC * (n + 1))

            def spread(x):
                return pick_b[:, x, tok].unsqueeze(1).to_broadcast([P, NK, OC])
            c.dve.wait(hot_free.get(n - 2))
            c.dve.mark(nc.vector.tensor_tensor(left[:, v, :, :], iota[:, :, :], spread(0), ALU.is_equal))
            s = c.dve.mark(nc.vector.tensor_tensor(right[:, v, :, :], iota[:, :, :], spread(1), ALU.is_equal))
            c.dve.wait(s)
            c.dve.mark(nc.vector.tensor_tensor(gated[:, v, 0, :, :], right[:, v, :, :], spread(2), ALU.mult))
            ready = c.dve.mark(nc.vector.tensor_tensor(gated[:, v, 1, :, :], right[:, v, :, :], spread(3), ALU.mult))
            c.pe.wait(ready)
            chunk, half = n // (TC // OC), n % (TC // OC)
            for q in range(OC // 4):
                i = self.take()
                for x in range(4):
                    tk = 4 * q + x
                    for part in range(2):
                        ins = nc.tensor.matmul(self.c.psum[:, i, NK * x:NK * (x + 1)], left[:, v, :, tk],
                                               gated[:, v, part, :, tk], start=part == 0, stop=part == 1)
                done = c.pe.mark(ins)
                at = OC * half + 4 * q
                lane = c.act
                lane.wait(done, mats_out.get(chunk - 2))
                dst = mats[:, chunk % 2, :, at:at + 4].rearrange("p b x -> p x b")
                src = c.bank(i).rearrange("p (x b) -> p x b", b=NK)
                s = lane.mark(nc.scalar.activation(dst, src, ACT.Copy))
                self.free(i, s)
            hot_free[n] = done
            if half == TC // OC - 1:
                self.gates_written = mats_out[chunk] = self.load(
                    f"gates_out_{chunk % 2}", self.gate_dram[chunk], mats[:, chunk % 2, :, :], [s])
        self.gates_written = [mats_out[chunk], mats_out[chunk - 1]]
        c.fence()
        for lane in (c.pe, c.act, c.dve, c.pool):
            lane.wait(*self.gates_written)
        hot_mem.close()
        mem.close()


    def second(self):
        c, nc, d = self.c, self.nc, self.d
        parts = (self.x_high, self.x_low)
        outer = Memory(nc)
        mem = Memory(nc)
        self.rms(mem, "final1", self.h, SEQ, lambda t: self.col("final1", t), [c.dve.now], None,
                 fp32_out=self.h)
        c.fence()
        mem.close()

        mod = outer("modulation", [P, 6 * KT, 2])
        gain1 = outer("gain1", [P, KT, 2])
        gain2 = outer("gain2", [P, KT])
        cond = outer("condition", [P, KT, 2])
        c.act.wait(c.dve.now)
        s = c.act.mark(nc.scalar.activation(cond[:, :, 0], self.cols[:, COLUMNS["c"]:COLUMNS["c"] + KT], ACT.Silu))
        s = c.act.mark(nc.scalar.activation(cond[:, :, 1], self.cols[:, COLUMNS["c_ctx"]:COLUMNS["c_ctx"] + KT],
                                            ACT.Silu))
        c.pe.wait(s)
        i = self.take()
        for g in range(12):
            block = self.w.next("ada")
            c.pe.wait(block[2])
            for f in range(4):
                at = 2 * (4 * g + f)
                for k in range(KT):
                    ins = nc.tensor.matmul(self.c.psum[:, i, at:at + 2], block[0][:, k, P * f:P * (f + 1)],
                                           cond[:, k, :], start=k == 0, stop=k == KT - 1)
            done = c.pe.mark(ins)
            self.w.release(done)
        c.dve.wait(done)
        ada_b = self.cols[:, COLUMNS["ada_b"]:COLUMNS["ada_b"] + 6 * KT]
        s = c.dve.mark(nc.vector.tensor_tensor(mod[:, :, :], c.bank(i, 12 * KT).rearrange("p (f x) -> p f x", x=2),
                                               ada_b.unsqueeze(2).to_broadcast([P, 6 * KT, 2]), ALU.add))
        self.free(i, s)
        c.dve.wait(s)
        g1 = self.cols[:, COLUMNS["norm1_2"]:COLUMNS["norm1_2"] + KT]
        g2 = self.cols[:, COLUMNS["norm2_2"]:COLUMNS["norm2_2"] + KT]
        for x in range(2):
            c.dve.mark(nc.vector.scalar_tensor_tensor(gain1[:, :, x], mod[:, KT:2 * KT, x], 1.0, g1,
                                                      ALU.add, ALU.mult))
        s = c.dve.mark(nc.vector.scalar_tensor_tensor(gain2[:, :], mod[:, 4 * KT:5 * KT, 0], 1.0, g2,
                                                      ALU.add, ALU.mult))
        c.dve.wait(s)
        c.act.wait(s)

        ctx_high = outer("ctx_high", [P, KT, CTX], BF16)
        ctx_low = outer("ctx_low", [P, KT, CTX], BF16)
        mem = Memory(nc)
        ctx = mem("ctx_in", [P, KT, CTX])
        landed = self.load("in_ctx", ctx[:, :, :], d["ctx"])
        ctx_n = self.rms(mem, "norm_ctx", ctx, CTX, lambda t: gain1[:, t, 1:2], [landed],
                         (ctx_high, ctx_low), shift=lambda t: mod[:, t, 1:2])
        xn = self.rms(mem, "norm1_2", self.h, SEQ, lambda t: gain1[:, t, 0:1], [c.dve.now], parts,
                      shift=lambda t: mod[:, t, 0:1])
        c.fence()
        mem.close()

        heads = Memory(nc)
        kt = heads("na_k", [P, 4, KEYS2])
        vt = heads("na_v", [P, KEYS2 // P, 512])
        qt = heads("na_q", [P, 4, SEQ])
        fin = heads("fourier_x", [P, 2, SEQ])
        ain = heads("conv_a", [P, 2, SEQ])
        gin = heads("conv_gate", [P, 2, SEQ])

        def keep(lane, dst, func=None):
            def evacuate(psum, done):
                lane.wait(done)
                if lane is c.act:
                    return lane.mark(nc.scalar.activation(dst, psum, func or ACT.Copy))
                return lane.mark(nc.vector.tensor_copy(dst, psum))
            return evacuate

        block = self.w.next("k2")
        for f in range(4):
            cols = slice(P * f, P * (f + 1))
            self.linear(block, cols, parts, slice(0, SEQ), SEQ, P, [xn], keep(c.dve, kt[:, f, 0:SEQ]))
            done = self.linear(block, cols, (ctx_high, ctx_low), slice(0, CTX), CTX, P, [ctx_n],
                               keep(c.act, kt[:, f, SEQ:KEYS2]))
        self.w.release(done)
        block = self.w.next("v2")
        for j in range(KEYS2 // P):
            src, at = (parts, P * j) if j < 4 else ((ctx_high, ctx_low), P * (j - 4))
            i = self.take()
            c.pe.wait(block[2])
            done = c.pe.mark(self.token_product(c.bank(i), block, slice(0, 512), src, slice(at, at + P)))
            self.free(i, keep(c.act if j % 2 else c.dve, vt[:, j, :])(c.bank(i), done))
        self.w.release(done)
        for name, dsts in (("q2", [qt[:, f, :] for f in range(4)]), ("fourier_in", [fin[:, f, :] for f in range(2)]),
                           ("conv_in", [ain[:, 0, :], ain[:, 1, :], gin[:, 0, :], gin[:, 1, :]])):
            block = self.w.next(name)
            for f, dst in enumerate(dsts):
                gate = name == "conv_in" and f >= 2
                lane = c.act if gate or f % 2 else c.dve
                done = self.linear(block, slice(P * f, P * (f + 1)), parts, slice(0, SEQ), SEQ, P, [xn],
                                   keep(lane, dst, ACT.Sigmoid if gate else None))
            self.w.release(done)
        c.fence()
        self.fourier(fin)
        self.convolution(ain, gin)
        self.neighbourhood(qt, kt, vt)
        c.fence()
        heads.close()

        mixed = c.dve.now
        for g in range(2):
            block = self.w.next("w_out_2")
            for f in range(4):
                t = 4 * g + f

                def add(psum, done, t=t):
                    c.dve.wait(done)
                    return c.dve.mark(nc.vector.scalar_tensor_tensor(
                        self.h[:, t, :], psum, mod[:, 2 * KT + t, 0:1], self.h[:, t, :], ALU.mult, ALU.add))
                done = self.linear(block, slice(P * f, P * (f + 1)), parts, slice(0, SEQ), SEQ, P,
                                   [mixed], add)
            self.w.release(done)
        c.fence()

        mem = Memory(nc)
        xn = self.rms(mem, "norm2_2", self.h, SEQ, lambda t: gain2[:, t:t + 1], [c.dve.now], parts,
                      shift=lambda t: mod[:, 3 * KT + t, 0:1])
        c.fence()
        mem.close()

        mem = Memory(nc)
        hid_high = mem("mlp_high", [P, 4 * KT, SEQ], BF16)
        hid_low = mem("mlp_low", [P, 4 * KT, SEQ], BF16)
        relu = mem("mlp_relu", [P, 2, SEQ])
        relu_free = [None, None]
        for g in range(8):
            block = self.w.next("mlp_1")
            for f in range(4):
                t = 4 * g + f

                def evacuate(psum, done, t=t):
                    r = relu[:, t % 2, :]
                    c.act.wait(done, relu_free[t % 2])
                    s = c.act.mark(nc.scalar.activation(r, psum, ACT.Relu))
                    c.dve.wait(s)
                    w = c.dve.mark(nc.vector.tensor_tensor(r, r, r, ALU.mult))
                    relu_free[t % 2] = split_value(c, r, hid_high[:, t, :], hid_low[:, t, :], [w])
                    return s
                done = self.linear(block, slice(P * f, P * (f + 1)), parts, slice(0, SEQ), SEQ, P,
                                   [xn], evacuate)
            self.w.release(done)
        hidden = c.dve.now
        c.pe.wait(hidden, *c.bank_free)
        for g in range(8):
            block = self.w.next("mlp_2")
            c.pe.wait(block[2])
            for t in range(KT):
                for k in range(4):
                    ins = three_products(c, c.bank(t), (block[0][:, k, P * t:P * (t + 1)],
                                                        block[1][:, k, P * t:P * (t + 1)]),
                                         (hid_high[:, 4 * g + k, :], hid_low[:, 4 * g + k, :]),
                                         g == 0 and k == 0, g == 7 and k == 3)
                if g == 7:
                    done = c.pe.mark(ins)
                    c.dve.wait(done)
                    self.free(t, c.dve.mark(nc.vector.scalar_tensor_tensor(
                        self.h[:, t, :], c.bank(t), mod[:, 5 * KT + t, 0:1], self.h[:, t, :],
                        ALU.mult, ALU.add)))
            done = c.pe.mark(ins) if g < 7 else done
            self.w.release(done)
        c.fence()
        mem.close()

        mem = Memory(nc)
        self.rms(mem, "final2", self.h, SEQ, lambda t: self.col("final2", t), [c.dve.now], None,
                 fp32_out=self.h)
        stored = self.c.dma(c.sp, "out_stored", self.out, self.h[:, :, :], [c.dve.now])
        c.sp.wait(stored)
        mem.close()
        outer.close()

    def fourier(self, x):
        c, nc, d = self.c, self.nc, self.d
        mem = Memory(nc)
        chan, chan_in = self.const(mem, "dft_channels", [P, 2, P])
        tok, tok_in = self.const(mem, "dft_tokens", [P, 2, 4, SEQ])
        wf, wf_in = self.const(mem, "w_fourier", [P, 2, FFT_CH])
        y = mem("dft_half", [P, 2, 4, FFT_CH])
        f = mem("dft_out", [P, 2, SEQ])
        c.pe.wait(chan_in, tok_in, wf_in)
        for part in range(2):
            for t in range(4):
                i = self.take()
                for g in range(2):
                    ins = nc.tensor.matmul(self.c.psum[:, i, P * g:P * (g + 1)], x[:, g, P * t:P * (t + 1)],
                                           chan[:, part, :], start=True, stop=True)
                done = c.pe.mark(ins)
                c.act.wait(done)
                s = c.act.mark(nc.scalar.activation(y[:, part, t, :], c.bank(i, FFT_CH), ACT.Copy))
                self.free(i, s)
        c.pe.wait(s)
        for g in range(2):
            i = self.take()
            for part in range(2):
                for t in range(4):
                    ins = nc.tensor.matmul(c.bank(i), y[:, part, t, P * g:P * (g + 1)], tok[:, part, t, :],
                                           start=part == 0 and t == 0, stop=part == 1 and t == 3)
            done = c.pe.mark(ins)
            c.act.wait(done)
            s = c.act.mark(nc.scalar.activation(f[:, g, :], c.bank(i), ACT.Copy))
            self.free(i, s)
        c.pe.wait(s)
        self.small_out(wf, f, 0, None)
        c.fence()
        mem.close()

    def small_out(self, w, x, dst, bias):
        c, nc = self.c, self.nc
        mem = Memory(nc)
        val = mem(f"small_out_{dst}", [P, 2, SEQ])
        for g in range(2):
            i = self.take()
            for k in range(2):
                ins = nc.tensor.matmul(c.bank(i), w[:, k, P * g:P * (g + 1)], x[:, k, :], start=k == 0, stop=k == 1)
            done = c.pe.mark(ins)
            c.act.wait(done)
            s = c.act.mark(nc.scalar.activation(val[:, g, :], c.bank(i), ACT.Identity, scale=1.0,
                                                bias=self.col(bias, g) if bias else 0.0))
            self.free(i, s)
            c.act.wait(s)
            split_value(c, val[:, g, :], self.x_high[:, dst + g, 0:SEQ], self.x_low[:, dst + g, 0:SEQ], [s])
        c.fence()
        mem.close()

    def convolution(self, a, gate):
        c, nc, d = self.c, self.nc, self.d
        mem = Memory(nc)
        pw, pw_in = self.const(mem, "conv_pw_w", [P, 2, 256])
        half = TAPS // 2
        v = mem("conv_padded", [P, 2, SEQ + 2 * half])
        y = mem("conv_out", [P, 2, SEQ])
        sq = mem("conv_square", [P, 2, SEQ])
        mean = mem("conv_mean", [P, SEQ])
        inv = mem("conv_inverse", [P, SEQ])
        s = c.dve.mark(nc.vector.memset(v[:, :, :], 0.0))
        c.dve.wait(s)
        s = c.dve.mark(nc.vector.tensor_tensor(v[:, :, half:half + SEQ], a[:, :, :], gate[:, :, :], ALU.mult))
        c.dve.wait(s)
        for tap in range(TAPS):
            for g in range(2):
                src = v[:, g, tap:tap + SEQ]
                w = self.cols[:, COLUMNS["conv_w"] + TAPS * g + tap:COLUMNS["conv_w"] + TAPS * g + tap + 1]
                if tap == 0:
                    c.dve.mark(nc.vector.tensor_scalar(y[:, g, :], src, w, self.col("conv_b", g), ALU.mult, ALU.add))
                else:
                    c.dve.wait((c.dve.sem, c.dve.count - 1))
                    c.dve.mark(nc.vector.scalar_tensor_tensor(y[:, g, :], src, w, y[:, g, :], ALU.mult, ALU.add))
        i, summed = self.mean_square(lambda t: y[:, t, :], 2, SEQ, [c.dve.now])
        c.act.wait(summed)
        s = c.act.mark(nc.scalar.activation(mean[:, :], c.bank(i), ACT.Copy, scale=1.0 / 256))
        self.free(i, s)
        c.dve.wait(s, c.dve.now)
        for g in range(2):
            s = c.dve.mark(nc.vector.tensor_tensor(y[:, g, :], y[:, g, :], mean[:, :], ALU.subtract))
        c.act.wait(s)
        s = c.act.mark(nc.scalar.activation(sq[:, :, :], y[:, :, :], ACT.Square))
        i, summed = self.mean_square(lambda t: sq[:, t, :], 2, SEQ, [s])
        s, last = self.inverse_root(inv[:, :], c.bank(i), SEQ, 1.0 / 256, self.eps[:, 1:2], [summed])
        self.free(i, s)
        c.dve.wait(last)
        for g in range(2):
            s = c.dve.mark(nc.vector.tensor_tensor(y[:, g, :], y[:, g, :], inv[:, :], ALU.mult))
            c.act.wait(s)
            s = c.act.mark(nc.scalar.activation(y[:, g, :], y[:, g, :], ACT.Silu, scale=self.col("conv_ln_g", g),
                                                bias=self.col("conv_ln_b", g)))
        c.pe.wait(s, pw_in)
        self.small_out(pw, y, 2, "conv_pw_b")
        c.fence()
        mem.close()

    def neighbourhood(self, q, k, v):
        c, nc, d = self.c, self.nc, self.d
        mem = Memory(nc)
        mask, mask_in = self.const(mem, "window", [P, GW])
        bias = mem("bias", [P, 2, NBIAS, GW])
        e = mem("na_exp", [P, 2, KEYS2])
        et = mem("na_exp_t", [P, 2, KEYS2 // P, P])
        stat = mem("na_stats", [P, 2, 8])
        o = mem("na_out", [P, SEQ])
        scale = HD2 ** -0.5
        steps = [(h, t) for h in range(NH2) for t in range(SEQ // P)]
        normed_at, turned_at, applied_at, bias_at = {}, {}, {}, {}
        last_add = {}
        c.dve.wait(mask_in)

        def bias_in(h):
            got = self.load(f"bias_in_{h % 2}", bias[:, h % 2, :, :], d["bias"][h], [last_add.get(h - 2)])
            c.dve.wait(got)
            bias_at[h] = c.dve.mark(nc.vector.tensor_tensor(
                bias[:, h % 2, :, :], bias[:, h % 2, :, :],
                mask[:, :].unsqueeze(1).to_broadcast([P, NBIAS, GW]), ALU.add))

        def scores(n):
            h, t = steps[n]
            x = n % 2
            rows = slice(64 * (h % 2), 64 * (h % 2) + 64)
            j = 2 * x
            c.pe.wait(c.bank_free[j], c.bank_free[j + 1])
            lhs = q[rows, h // 2, P * t:P * (t + 1)]
            nc.tensor.matmul(c.bank(j), lhs, k[rows, h // 2, 0:SEQ], start=True, stop=True)
            done = c.pe.mark(nc.tensor.matmul(c.bank(j + 1, CTX), lhs, k[rows, h // 2, SEQ:KEYS2],
                                              start=True, stop=True))
            st, es = stat[:, x, :], e[:, x, :]
            c.dve.wait(done, turned_at.get(n - 2), bias_at[h], normed_at.get(n - 2))
            first = ROWS - 2 - 2 * t
            s = c.dve.mark(nc.vector.scalar_tensor_tensor(
                es[:, 0:SEQ], c.bank(j), scale,
                bias[:, h % 2, first:first + ROWS, :].rearrange("p a b -> p (a b)"), ALU.mult, ALU.add))
            last_add[h] = s
            s2 = c.dve.mark(nc.vector.tensor_scalar(es[:, SEQ:KEYS2], c.bank(j + 1, CTX), scale, None, ALU.mult))
            self.free(j, s)
            self.free(j + 1, s2)
            c.dve.wait(s2)
            s = c.dve.mark(nc.vector.tensor_reduce(st[:, 0:1], es, AX.X, ALU.max))
            c.dve.wait(s)
            s = c.dve.mark(nc.vector.tensor_scalar(st[:, 1:2], st[:, 0:1], -1.0, None, ALU.mult))
            c.act.wait(s)
            return c.act.mark(nc.scalar.activation(es, es, ACT.Exp, bias=st[:, 1:2], scale=1.0,
                                                   accum_out=st[:, 2:3]))

        def norm(n, exped):
            x = n % 2
            st = stat[:, x, :]
            c.dve.wait(exped)
            s = c.dve.mark(nc.vector.reciprocal(st[:, 3:4], st[:, 2:3]))
            c.dve.wait(s)
            normed_at[n] = c.dve.mark(nc.vector.tensor_scalar(e[:, x, :], e[:, x, :], st[:, 3:4], None, ALU.mult))

        def applying(n):
            h, t = steps[n]
            x = n % 2
            c.pe.wait(normed_at[n], c.bank_free[4], c.bank_free[5])
            for y in range(KEYS2 // P):
                ins = nc.tensor.transpose(self.c.psum[:, 4 + y // 4, P * (y % 4):P * (y % 4 + 1)],
                                          e[:, x, P * y:P * (y + 1)], self.ident[:, :])
            turned_at[n] = c.pe.mark(ins)
            c.act.wait(turned_at[n], applied_at.get(n - 2))
            s = c.act.mark(nc.scalar.activation(et[:, x, 0:4, :].rearrange("p a b -> p (a b)"), c.bank(4), ACT.Copy))
            self.free(4, s)
            s = c.act.mark(nc.scalar.activation(et[:, x, 4:6, :].rearrange("p a b -> p (a b)"), c.bank(5, CTX),
                                                ACT.Copy))
            self.free(5, s)
            bank = 6 + h // 2 % 2
            rows = slice(64 * (h % 2), 64 * (h % 2) + 64)
            c.pe.wait(s)
            if t == 0 and h % 2 == 0:
                c.pe.wait(c.bank_free[bank])
            for y in range(KEYS2 // P):
                ins = nc.tensor.matmul(self.c.psum[rows, bank, P * t:P * (t + 1)],
                                       v[:, y, HD2 * h:HD2 * (h + 1)], et[:, x, y, :],
                                       start=y == 0, stop=y == KEYS2 // P - 1)
            applied_at[n] = c.pe.mark(ins)
            if t == SEQ // P - 1 and h % 2 == 1:
                c.act.wait(applied_at[n], c.dve.now)
                got = c.act.mark(nc.scalar.activation(o[:, :], c.bank(bank), ACT.Copy))
                self.free(bank, got)
                c.act.wait(got)
                split_value(c, o[:, :], self.x_high[:, 4 + h // 2, 0:SEQ], self.x_low[:, 4 + h // 2, 0:SEQ], [got])

        bias_in(0)
        bias_in(1)
        for n in range(len(steps) + 1):
            if n < len(steps):
                h, t = steps[n]
                if t == 0 and 1 <= h < NH2 - 1:
                    bias_in(h + 1) if h >= 1 else None
                exped = scores(n)
            if n >= 1:
                applying(n - 1)
            if n < len(steps):
                norm(n, exped)
        c.fence()
        mem.close()


_WIDTHS = (("ln1", KT), ("ln2", KT), ("final1", KT), ("da_norm", 1), ("gla_norm", 1), ("gate_b", 4),
           ("c", KT), ("c_ctx", KT), ("ada_b", 6 * KT), ("norm1_2", KT), ("norm2_2", KT), ("final2", KT),
           ("conv_w", 2 * TAPS), ("conv_b", 2), ("conv_ln_g", 2), ("conv_ln_b", 2), ("conv_pw_b", 2))
COLUMNS, _at = {}, 0
for _name, _n in _WIDTHS:
    COLUMNS[_name] = _at
    _at += _n
N_COLUMNS = _at


def shape_constants():
    out = {"identity": np.eye(P, dtype=np.float32)}
    inv = np.power(np.float32(500000.0), -np.arange(0, ROPE, 2, dtype=np.float32) / np.float32(ROPE)).astype(np.float32)
    ang = (np.arange(T, dtype=np.float32)[:, None] * inv[None, :]).astype(np.float32)
    cos, sin = np.ones((P, T), np.float32), np.zeros((P, T), np.float32)
    swap = np.zeros((P, P), np.float32)
    hr = ROPE // 2
    for o in (0, DA_DIM):
        for i in range(hr):
            cos[o + i] = cos[o + hr + i] = np.cos(ang[:, i])
            sin[o + i] = sin[o + hr + i] = np.sin(ang[:, i])
            swap[o + hr + i, o + i] = -1.0
            swap[o + i, o + hr + i] = 1.0
    out.update(rope_cos=cos, rope_sin=sin, rope_swap=swap)
    j, i = np.arange(JT)[:, None], np.arange(JT)[None, :]
    same = (j // LEAF) == (i // LEAF)
    masks = [(j < LEAF) & (i >= LEAF), (j >= LEAF) & (i < LEAF), same & (j <= i), same & (j >= i)]
    out["leaf_masks"] = np.ascontiguousarray(np.stack(masks, 1).astype(np.float32))
    out["iota_picks"] = np.broadcast_to(np.arange(TOPK, dtype=np.float32), (P, TOPK)).copy()
    out["iota_keys"] = np.broadcast_to(np.arange(NK, dtype=np.float32), (P, NK)).copy()
    m = FFT_CH // FFT_G
    a = 2 * np.pi * (np.outer(np.arange(m), np.arange(m)) % m) / m
    chan = np.zeros((P, 2, P))
    for g in range(2):
        chan[m * g:m * (g + 1), 0, m * g:m * (g + 1)] = np.cos(a)
        chan[m * g:m * (g + 1), 1, m * g:m * (g + 1)] = np.sin(a)
    out["dft_channels"] = chan.astype(np.float32)
    a = 2 * np.pi * (np.outer(np.arange(SEQ), np.arange(SEQ)) % SEQ) / SEQ
    norm = 1.0 / math.sqrt(SEQ * m)
    tok = np.stack([np.cos(a), -np.sin(a)]) * norm
    out["dft_tokens"] = np.ascontiguousarray(tok.reshape(2, 4, P, SEQ).transpose(2, 0, 1, 3)).astype(np.float32)
    col = np.arange(GW)
    start = np.clip(col - WC // 2, 0, GW - WC)
    seen = (col[None, :] >= start[:, None]) & (col[None, :] < start[:, None] + WC)
    out["window"] = np.tile(np.where(seen, 0.0, -1e30).astype(np.float32), (2, 1))
    return out


def lay_out(inputs):
    g = {k: np.asarray(v) for k, v in inputs.items()}

    def tiles(x):
        return x.reshape((x.shape[0] // P, P) + x.shape[1:]).swapaxes(0, 1)

    out = dict(shape_constants())
    tokens = np.concatenate([g["meta_tokens"], g["x"][0]], axis=0)
    out["tokens"] = tiles(tokens.T)
    out["ctx"] = tiles(g["ctx_2"][0].T)
    out["w_in"] = g["w_in"][0]
    out["w_out"] = g["w_out"][0]
    out["peer_w_q"] = g["peer_w_q"][0]
    u = g["peer_u"][0].reshape(NK, NK // EG, EG, KT, P)
    out["peer_u"] = u.transpose(1, 4, 3, 2, 0).reshape(NK // EG, P, KT * EG * NK)
    out["peer_v"] = g["peer_v"][0].reshape(NK, NK, D).transpose(1, 0, 2)
    out["sub_keys"] = g["peer_sub_keys"][0].reshape(2 * PH, NK, P).transpose(2, 0, 1)
    w2 = np.zeros((2 * GLA_RANK, 512), np.float32)
    w2[:GLA_RANK, :256] = g["gla_gate_w2_f"][0]
    w2[GLA_RANK:, 256:] = g["gla_gate_w2_b"][0]
    out["gate_w2"] = w2
    out["lambdas"] = np.stack([g[f"da_lambda_{n}"][0] for n in ("q1", "q2", "k1", "k2")], axis=1)
    out["ada_w"] = g["ada_w_2"][0]
    out["w_in_2"] = g["w_in_2"][0]
    out["w_out_2"] = g["w_out_2"][0]
    out["mlp_w1"] = g["mlp_w1_2"][0]
    out["mlp_w2"] = g["mlp_w2_2"][0]
    out["w_fourier"] = tiles(g["w_fourier_2"][0])
    out["conv_pw_w"] = tiles(g["conv_pw_w_2"][0])
    rpb = g["na_rpb_2"][0]
    row, colq = np.arange(P) // GW, np.arange(P) % GW
    off_r = np.arange(NBIAS)[None, :, None] + 1 - row[:, None, None]
    off_c = np.clip(np.arange(GW)[None, None, :] - colq[:, None, None] + WC - 1, 0, 2 * WC - 2)
    out["bias"] = rpb[:, off_r, off_c]
    gate_b = np.concatenate([g["gla_gate_b_f"][0], g["gla_gate_b_b"][0]])
    conv_w = g["conv_dw_w_2"][0].T.reshape(2, P, TAPS).transpose(1, 0, 2).reshape(P, 2 * TAPS)
    columns = {
        "ln1": tiles(g["ln1_w"][0]), "ln2": tiles(g["ln2_w"][0]), "final1": tiles(g["final_norm_w"]),
        "da_norm": tiles(g["da_subln_w"][0]), "gla_norm": tiles(g["gla_norm_w"][0]), "gate_b": tiles(gate_b),
        "c": tiles(g["c_2"][0]), "c_ctx": tiles(g["c_ctx_2"]), "ada_b": tiles(g["ada_b_2"][0]),
        "norm1_2": tiles(g["norm1_g_2"][0]), "norm2_2": tiles(g["norm2_g_2"][0]),
        "final2": tiles(g["final_norm_g_2"]), "conv_w": conv_w, "conv_b": tiles(g["conv_dw_b_2"][0]),
        "conv_ln_g": tiles(g["conv_norm_g_2"][0]), "conv_ln_b": tiles(g["conv_norm_b_2"][0]),
        "conv_pw_b": tiles(g["conv_pw_b_2"][0]),
    }
    out["columns"] = np.concatenate([columns[n] for n, _ in _WIDTHS], axis=1)
    return {k: np.ascontiguousarray(v) for k, v in out.items()}


def kernel(**inputs):
    import concourse.bacc as bacc
    from concourse.bass_utils import run_bass_kernel_spmd

    arrays = lay_out(inputs)
    nc = bacc.Bacc("TRN2", target_bir_lowering=False, num_devices=1)
    dram = {name: nc.dram_tensor(f"{name}_dram", a.shape, mybir.dt.from_np(a.dtype), kind="ExternalInput").ap()
            for name, a in arrays.items()}
    out = nc.dram_tensor("out_dram", (P, KT, SEQ), F32, kind="ExternalOutput").ap()
    gate_dram = nc.dram_tensor("gate_dram", (SEQ // TC, P, NK, TC), F32, kind="Internal").ap()
    Net(nc, dram, out, gate_dram).build()
    got = run_bass_kernel_spmd(nc, [{f"{n}_dram": a for n, a in arrays.items()}], core_ids=[0])
    y = np.asarray(got.results[0]["out_dram"])
    return np.ascontiguousarray(y.transpose(2, 1, 0).reshape(1, SEQ, D))
```

```python
import math
from contextlib import ExitStack

import numpy as np

import concourse.bass as bass
import concourse.mybir as mybir

F32 = mybir.dt.float32
BF16 = mybir.dt.bfloat16
U32 = mybir.dt.uint32
ALU = mybir.AluOpType
ACT = mybir.ActivationFunctionType
AX = mybir.AxisListType

P = 128
D = 1024
KT = D // P
BANK = 512
SEQ, META = 512, 16
T = SEQ + META
HT = T // 2
DA_HEADS, DA_DIM, ROPE = 4, 64, 16
LAM_INIT = 0.8 - 0.6 * math.exp(0.0)
GLA_HEADS, GLA_RANK, GLA_TAU = 4, 16, 16.0
JT = 66
NJ = T // JT
LEAF = JT // 2
EPS, LN_EPS = 1e-6, 1e-5
PH, NK, TOPK = 8, 128, 16
PICKS = PH * TOPK
EG = 4
TC = 32
AHEAD_TOP = 3
AHEAD = 17
OC = 16
CTX = 256
NH2, HD2 = 8, 64
GW, ROWS, WC, WR = 64, 8, 16, 8
NBIAS = 2 * ROWS - 2
TAPS = 31
FFT_CH, FFT_G = 256, 4
KEYS2 = SEQ + CTX


class Lane:

    def __init__(self, nc, engine, name):
        self.engine, self.sem = engine, nc.alloc_semaphore(name)
        self.count, self.seen = 0, {}

    def wait(self, *signals):
        for s in signals:
            if s is None:
                continue
            if isinstance(s, list):
                self.wait(*s)
                continue
            sem, value = s
            if self.seen.get(id(sem), 0) < value:
                self.engine.wait_ge(sem, value)
                self.seen[id(sem)] = value

    def mark(self, instruction):
        instruction.then_inc(self.sem, 1)
        self.count += 1
        return (self.sem, self.count)

    @property
    def now(self):
        return (self.sem, self.count) if self.count else None


class Core:

    def __init__(self, nc):
        self.nc = nc
        self.pe = Lane(nc, nc.tensor, "pe_steps")
        self.act = Lane(nc, nc.scalar, "act_steps")
        self.dve = Lane(nc, nc.vector, "dve_steps")
        self.pool = Lane(nc, nc.gpsimd, "pool_steps")
        self.sp = Lane(nc, nc.sync, "sp_steps")
        self.psum = nc.alloc_psum_tensor("psum", [P, 8, BANK], F32)
        self.bank_free = [None] * 8
        self.dma_sems = {}

    def bank(self, i, n=BANK, m=P):
        return self.psum[0:m, i, 0:n]

    def dma(self, lane, name, out, in_, after=()):
        lane.wait(*after)
        if name not in self.dma_sems:
            self.dma_sems[name] = [self.nc.alloc_semaphore(name), 0]
        entry = self.dma_sems[name]
        lane.engine.dma_start(out, in_).then_inc(entry[0], 16)
        entry[1] += 16
        return (entry[0], entry[1])

    def fence(self):
        signals = [x.now for x in (self.pe, self.act, self.dve, self.pool)]
        for lane in (self.pe, self.act, self.dve, self.pool):
            lane.wait(*signals)


class Memory:

    def __init__(self, nc):
        self.nc, self.stack = nc, ExitStack()

    def __call__(self, name, shape, dtype=F32):
        return self.stack.enter_context(self.nc.sbuf_tensor(name, shape, dtype))

    def close(self):
        self.stack.close()


class WeightStream:
    STAGES, SPLITS = 2, 3
    SIZE = 4096

    def __init__(self, core, plan):
        nc = core.nc
        self.core, self.plan = core, plan
        self.stage = nc.alloc_sbuf_tensor("weight_stage", [P, self.STAGES, self.SIZE], F32)
        self.high = nc.alloc_sbuf_tensor("weight_high", [P, self.SPLITS, self.SIZE], BF16)
        self.low = nc.alloc_sbuf_tensor("weight_low", [P, self.SPLITS, self.SIZE], BF16)
        self.stage_free, self.used = {}, {}
        self.loaded, self.split_done = [], {}
        self.n_split = self.n_next = 0
        self.pump()
        self.split()

    def view(self, buf, slot, n):
        rows, cols = self.plan[n][1].shape[1], self.plan[n][1].shape[2]
        return buf[:, slot, 0:rows * cols].rearrange("p (r c) -> p r c", c=cols)

    def pump(self):
        while len(self.loaded) < len(self.plan):
            n = len(self.loaded)
            if n >= self.STAGES and n - self.STAGES not in self.stage_free:
                return
            slot = n % self.STAGES
            free = self.stage_free.get(n - self.STAGES, [])
            self.loaded.append(self.core.dma(self.core.sp, f"weights_in_{slot}",
                                             self.view(self.stage, slot, n), self.plan[n][1], free))

    def split(self):
        n = self.n_split
        self.n_split += 1
        if n >= len(self.plan) or self.plan[n][2]:
            return
        c, slot = self.core, n % self.SPLITS
        stage = self.view(self.stage, n % self.STAGES, n)
        high, low = self.view(self.high, slot, n), self.view(self.low, slot, n)
        free = self.used.get(n - self.SPLITS)
        c.act.wait(self.loaded[n], free)
        h = c.act.mark(c.nc.scalar.activation(high, stage, ACT.Copy))
        c.pool.wait(self.loaded[n], free, h)
        lo = c.pool.mark(c.nc.gpsimd.tensor_tensor(low, stage, high, ALU.subtract))
        self.stage_free[n] = [h, lo]
        self.split_done[n] = lo
        self.pump()

    def next(self, name):
        n = self.n_next
        assert self.plan[n][0] == name, (self.plan[n][0], name)
        self.n_next += 1
        self.split()
        if self.plan[n][2]:
            return self.view(self.stage, n % self.STAGES, n), None, self.loaded[n]
        return (self.view(self.high, n % self.SPLITS, n), self.view(self.low, n % self.SPLITS, n),
                self.split_done[n])

    def release(self, signal):
        n = self.n_next - 1
        self.used[n] = signal
        if self.plan[n][2]:
            self.stage_free[n] = [signal]
            self.pump()


def three_products(core, out, left, right, first, last):
    pairs = ((0, 0), (0, 1), (1, 0))
    for i, (a, b) in enumerate(pairs):
        ins = core.nc.tensor.matmul(out, left[a], right[b], start=first and i == 0,
                                    stop=last and i == len(pairs) - 1)
    return ins


def split_value(core, value, high, low, after):
    core.act.wait(*after)
    h = core.act.mark(core.nc.scalar.activation(high, value, ACT.Copy))
    core.dve.wait(h, *after)
    return core.dve.mark(core.nc.vector.tensor_tensor(low, value, high, ALU.subtract))


class Net:

    def __init__(self, nc, d, out, gate_dram, act_dram):
        self.nc, self.d, self.out, self.gate_dram, self.act_dram = nc, d, out, gate_dram, act_dram
        self.c = Core(nc)
        self.ring = 0


    def take(self, banks=(0, 1, 2, 3, 4, 5, 6, 7)):
        i = banks[self.ring % len(banks)]
        self.ring += 1
        self.c.pe.wait(self.c.bank_free[i])
        return i

    def take_pair(self, n=4):
        j = 2 * (self.ring % n)
        self.ring += 1
        self.c.pe.wait(self.c.bank_free[j], self.c.bank_free[j + 1])
        return j

    def free(self, i, signal):
        self.c.bank_free[i] = signal

    def pair(self, j, m=P, n=HT):
        return self.c.psum[0:m, j:j + 2, 0:n]

    def load(self, name, out, in_, after=()):
        return self.c.dma(self.c.pool, name, out, in_, after)

    def const(self, mem, name, shape):
        t = mem(name, shape)
        full = t[tuple(slice(0, n) for n in shape)]
        return t, self.load(f"in_{name}", full, self.d[name])

    def mean_square(self, square, n_tiles, n, after):
        c = self.c
        c.pe.wait(*after)
        i = self.take()
        for t in range(n_tiles):
            ins = c.nc.tensor.matmul(c.bank(i, n), self.ones[:, :], square(t),
                                     start=t == 0, stop=t == n_tiles - 1)
        return i, c.pe.mark(ins)

    def inverse_root(self, dst, banks, n, scale, eps, after):
        c = self.c
        c.act.wait(*after, c.dve.now)
        s = c.act.mark(c.nc.scalar.activation(dst, banks, ACT.Sqrt, bias=eps, scale=scale))
        c.dve.wait(s)
        return s, c.dve.mark(c.nc.vector.reciprocal(dst, dst))

    def norm_buffers(self, mem, tag, n):
        self.square = mem(f"{tag}_square", [P, 4, n])
        self.inverse = mem(f"{tag}_inverse", [P, n])
        self.value = mem(f"{tag}_value", [P, 4, n])
        self.square_free = [None] * 4

    def rms(self, x, n, gain, after, store, shift=None, fp32_out=None):
        c, nc = self.c, self.nc
        ranges = [(0, n)] if n <= BANK else [(0, HT), (HT, n)]
        sq, inv, val = self.square, self.inverse, self.value
        banks = [self.take() for _ in ranges]
        parts_free = c.pe.now
        for t in range(KT):
            c.act.wait(after[t % len(after)], self.square_free[t % 4])
            s = c.act.mark(nc.scalar.activation(sq[:, t % 4, 0:n], x[:, t, 0:n], ACT.Square))
            c.pe.wait(s)
            for b, (lo, hi) in zip(banks, ranges):
                ins = nc.tensor.matmul(c.bank(b, hi - lo), self.ones[:, :], sq[:, t % 4, lo:hi],
                                       start=t == 0, stop=t == KT - 1, skip_group_check=True)
            self.square_free[t % 4] = c.pe.mark(ins)
        for b, (lo, hi) in zip(banks, ranges):
            s, last = self.inverse_root(inv[:, lo:hi], c.bank(b, hi - lo), n, 1.0 / D,
                                        self.eps[:, 0:1], [c.pe.now])
            self.free(b, s)
        done, scaled = [None] * KT, {}
        c.act.wait(parts_free)
        c.dve.wait(parts_free, last)
        for t in range(KT + 2):
            if t < KT:
                v = fp32_out[:, t, 0:n] if fp32_out is not None else val[:, t % 4, 0:n]
                c.dve.wait(done[t - 4] if t >= 4 else last)
                s = c.dve.mark(nc.vector.scalar_tensor_tensor(v, x[:, t, 0:n], gain(t), inv[:, 0:n],
                                                              ALU.mult, ALU.mult))
                if store is None:
                    done[t] = s
                    continue
                c.act.wait(s)
                h = c.act.mark(nc.scalar.activation(store[0][:, t, 0:n], v, ACT.Identity, scale=1.0,
                                                    bias=shift(t) if shift else 0.0))
                scaled[t] = (v, h)
            if store is not None and t >= 2:
                u = t - 2
                v, h = scaled[u]
                c.dve.wait(h)
                if shift is None:
                    ins = nc.vector.tensor_tensor(store[1][:, u, 0:n], v, store[0][:, u, 0:n], ALU.subtract)
                else:
                    ins = nc.vector.scalar_tensor_tensor(store[1][:, u, 0:n], v, shift(u),
                                                         store[0][:, u, 0:n], ALU.add, ALU.subtract)
                done[u] = c.dve.mark(ins)
        return done

    def column_product(self, out, block, cols, parts, tokens, after=(), n_k=KT, first=True, last=True,
                       k0=0):
        high, low, _ = block
        for k in range(n_k):
            if after:
                self.c.pe.wait(after[k % len(after)])
            ins = three_products(self.c, out, (high[:, k, cols], low[:, k, cols]),
                                 (parts[0][:, k0 + k, tokens], parts[1][:, k0 + k, tokens]),
                                 first and k == 0, last and k == n_k - 1)
        return ins

    def token_product(self, out, block, cols, parts, tokens):
        high, low, _ = block
        for k in range(KT):
            ins = three_products(self.c, out, (parts[0][:, k, tokens], parts[1][:, k, tokens]),
                                 (high[:, k, cols], low[:, k, cols]), k == 0, k == KT - 1)
        return ins

    def linear(self, block, cols, parts, tokens, n, m, after, evacuate, **kw):
        c = self.c
        i = self.take()
        c.pe.wait(block[2])
        done = c.pe.mark(self.column_product(c.bank(i, n, m), block, cols, parts, tokens, after, **kw))
        self.free(i, evacuate(c.bank(i, n, m), done))
        return done


    def build(self):
        c, nc, d = self.c, self.nc, self.d
        sb = nc.alloc_sbuf_tensor
        plan = []

        def weights(name, src, raw=False):
            plan.append((name, src, raw))

        w_in = d["w_in"].rearrange("(t p) n -> p t n", p=P)
        for name, lo, hi in (("z", 3072, 3104), ("gla_qk", 1536, 2048), ("gla_v", 2048, 2560),
                             ("gla_r", 2560, 3072), ("da_q", 0, 512), ("da_k", 512, 1024),
                             ("da_v", 1024, 1536)):
            weights(name, w_in[:, :, lo:hi])
        for g in range(12):
            weights("ada", d["ada_w"].rearrange("(t p) n -> p t n", p=P)[:, :, BANK * g:BANK * (g + 1)], True)
        for g in range(2):
            weights("w_out", d["w_out"].rearrange("(t p) n -> p t n", p=P)[:, :, BANK * g:BANK * (g + 1)])
        for g in range(4):
            weights("peer_q", d["peer_w_q"].rearrange("(t p) n -> p t n", p=P)[:, :, BANK * g:BANK * (g + 1)])
        def up(g):
            weights("u", d["peer_u"][g].rearrange("p (t e) -> p t e", t=KT))

        for g in range(AHEAD):
            up(g)
        for g in range(NK // EG):
            if AHEAD <= g + 1 < NK // EG:
                up(g + 1)
            weights("v", d["peer_v"][EG * g:EG * (g + 1)].rearrange("b p n -> p b n"))
        w_in2 = d["w_in_2"].rearrange("(t p) n -> p t n", p=P)
        for name, lo, hi in (("k2", 1280, 1792), ("v2", 1792, 2304), ("q2", 768, 1280),
                             ("fourier_in", 0, 256), ("conv_in", 256, 768)):
            weights(name, w_in2[:, :, lo:hi])
        for g in range(2):
            weights("w_out_2", d["w_out_2"].rearrange("(t p) n -> p t n", p=P)[:, :, BANK * g:BANK * (g + 1)])
        for g in range(8):
            weights("mlp_1", d["mlp_w1"].rearrange("(t p) n -> p t n", p=P)[:, :, BANK * g:BANK * (g + 1)])
        for g in range(8):
            weights("mlp_2", d["mlp_w2"].rearrange("(t p) n -> p t n", p=P)[:, 4 * g:4 * g + 4, :])

        self.ones = sb("ones", [P, P], F32)
        self.ident = sb("identity", [P, P], F32)
        self.eps = sb("eps", [P, 2], F32)
        self.cols = sb("columns", [P, d["columns"].shape[1]], F32)
        c.pool.mark(nc.gpsimd.memset(self.ones[:, :], 1.0))
        c.pool.mark(nc.gpsimd.memset(self.eps[:, 0:1], EPS))
        c.pool.mark(nc.gpsimd.memset(self.eps[:, 1:2], LN_EPS))
        ready = [c.pool.now, self.load("in_identity", self.ident[:, :], d["identity"]),
                 self.load("in_columns", self.cols[:, :], d["columns"])]
        self.mod = sb("modulation", [P, 6 * KT, 2], F32)
        self.gain1 = sb("gain1", [P, KT, 2], F32)
        self.gain2 = sb("gain2", [P, KT], F32)
        self.cond = sb("condition", [P, KT, 2], F32)
        self.h = sb("residual", [P, KT, SEQ], F32)
        self.x_high = sb("x_high", [P, KT, T], BF16)
        self.x_low = sb("x_low", [P, KT, T], BF16)
        for lane in (c.pe, c.act, c.dve, c.pool):
            lane.wait(*ready)

        self.w = WeightStream(c, plan)
        self.mixer()
        self.experts()
        self.second()

    def col(self, name, t=0):
        at = COLUMNS[name] + t
        return self.cols[:, at:at + 1]


    def mixer(self):
        c, nc, d = self.c, self.nc, self.d
        parts = (self.x_high, self.x_low)
        outer = Memory(nc)
        z = outer("z", [2 * GLA_RANK, T])
        gqk = outer("gla_qk", [P, 4, T])
        gv = outer("gla_v", [JT, NJ, 512])
        gr, silu = self.h[:, 0:4, :], self.h[:, 4:8, :]
        da = Memory(nc)
        dq = da("da_q", [P, 4, SEQ])
        dk = da("da_k", [P, 4, T])
        dv = da("da_v", [P, 5, 512])

        first = Memory(nc)
        self.norm_buffers(first, "norm1", T)
        h0 = first("tokens_in", [P, KT, T])
        landed = [self.load(f"in_tokens_{g}", h0[:, 2 * g:2 * g + 2, :], d["tokens"][:, 2 * g:2 * g + 2, :])
                  for g in range(4)]
        landed = [landed[t // 2] for t in range(KT)]
        xn = self.rms(h0, T, lambda t: self.col("ln1", t), landed, parts)

        def keep(lane, dst, scale=1.0):
            def evacuate(psum, done):
                lane.wait(done)
                if lane is c.act:
                    return lane.mark(nc.scalar.activation(dst, psum, ACT.Identity, scale=scale))
                return lane.mark(nc.vector.tensor_scalar(dst, psum, scale, None, ALU.mult))
            return evacuate

        def full_columns(name, dst, n_tiles, m, scales):
            block = self.w.next(name)
            for f in range(n_tiles):
                for g in range(2):
                    tokens = slice(HT * g, HT * (g + 1))
                    lane = c.act if (f + g) % 2 else c.dve
                    done = self.linear(block, slice(P * f, P * f + m), parts, tokens, HT, m, xn,
                                       keep(lane, dst(f)[:, tokens], scales[f]))
            self.w.release(done)

        def seq_columns(name, dst):
            block = self.w.next(name)
            for f in range(4):
                lane = c.act if f % 2 else c.dve
                done = self.linear(block, slice(P * f, P * (f + 1)), parts, slice(META, T), SEQ, P,
                                   xn, keep(lane, dst[:, f, :]))
            self.w.release(done)

        def rows(name, dst, step):
            block = self.w.next(name)
            for j in range(-(-T // step)):
                m = min(step, T - step * j)
                i = self.take()
                c.pe.wait(block[2], *xn)
                done = c.pe.mark(self.token_product(c.bank(i, 512, m), block, slice(0, 512), parts,
                                                    slice(step * j, step * j + m)))
                self.free(i, keep(c.act if j % 2 else c.dve, dst[0:m, j, :])(c.bank(i, 512, m), done))
            self.w.release(done)

        full_columns("z", lambda f: z, 1, 2 * GLA_RANK, [1.0])
        full_columns("gla_qk", lambda f: gqk[:, f, :], 4, P, [0.125, 0.125, 1.0, 1.0])
        rows("gla_v", gv, JT)
        seq_columns("gla_r", gr)
        seq_columns("da_q", dq)
        full_columns("da_k", lambda f: dk[:, f, :], 4, P, [1.0] * 4)
        rows("da_v", dv, P)
        mixed_free = c.pe.now
        projected = [c.act.now, c.dve.now]
        c.fence()
        first.close()
        self.attention(dq, dk, dv, projected)
        da.close()
        self.linear_attention(z, gqk, gv, gr, silu, projected, mixed_free)
        c.fence()

        late = Memory(nc)
        landed = self.load("in_residual", self.h[:, :, :], d["tokens"][:, :, META:T])
        mixed = c.dve.now
        self.added = []
        for g in range(2):
            block = self.w.next("w_out")
            for f in range(4):
                t = 4 * g + f

                def add(psum, done, t=t):
                    c.dve.wait(done, landed)
                    self.added.append(c.dve.mark(nc.vector.tensor_tensor(
                        self.h[:, t, :], psum, self.h[:, t, :], ALU.add)))
                    return self.added[-1]
                done = self.linear(block, slice(P * f, P * (f + 1)), parts, slice(0, SEQ), SEQ, P,
                                   [mixed], add)
            self.w.release(done)
        c.fence()
        late.close()
        outer.close()

    def head_norm(self, mem, tag, o, dst, gain, after, extra=None):
        c, nc = self.c, self.nc
        sq, inv = mem[0], mem[1]
        c.act.wait(*after, c.dve.now, c.pe.now)
        s = c.act.mark(nc.scalar.activation(sq[:, :], o, ACT.Square))
        i, summed = self.mean_square(lambda t: sq[:, :], 1, SEQ, [s])
        s, last = self.inverse_root(inv[:, :], c.bank(i), SEQ, 1.0 / P, self.eps[:, 0:1], [summed])
        self.free(i, s)
        c.dve.wait(last)
        s = c.dve.mark(nc.vector.scalar_tensor_tensor(sq[:, :], o, gain, inv[:, :], ALU.mult, ALU.mult))
        if extra is not None:
            c.dve.wait(s)
            s = c.dve.mark(nc.vector.tensor_tensor(sq[:, :], sq[:, :], extra, ALU.mult))
        return split_value(c, sq[:, :], self.x_high[:, dst, 0:SEQ], self.x_low[:, dst, 0:SEQ], [s])

    def modulation_products(self):
        c, nc, cond = self.c, self.nc, self.cond
        s = c.act.mark(nc.scalar.activation(cond[:, :, 0], self.cols[:, COLUMNS["c"]:COLUMNS["c"] + KT], ACT.Silu))
        s = c.act.mark(nc.scalar.activation(cond[:, :, 1], self.cols[:, COLUMNS["c_ctx"]:COLUMNS["c_ctx"] + KT],
                                            ACT.Silu))
        c.pe.wait(s)
        i = 7
        c.pe.wait(c.bank_free[i])
        for g in range(12):
            block = self.w.next("ada")
            c.pe.wait(block[2])
            for f in range(4):
                at = 2 * (4 * g + f)
                for k in range(KT):
                    ins = nc.tensor.matmul(self.c.psum[:, i, at:at + 2], block[0][:, k, P * f:P * (f + 1)],
                                           cond[:, k, :], start=k == 0, stop=k == KT - 1)
            done = c.pe.mark(ins)
            self.w.release(done)
        self.modulation_summed = done

    def modulation_columns(self):
        c, nc = self.c, self.nc
        mod, gain1, gain2 = self.mod, self.gain1, self.gain2
        i = 7
        c.dve.wait(self.modulation_summed)
        ada_b = self.cols[:, COLUMNS["ada_b"]:COLUMNS["ada_b"] + 6 * KT]
        s = c.dve.mark(nc.vector.tensor_tensor(mod[:, :, :], c.bank(i, 12 * KT).rearrange("p (f x) -> p f x", x=2),
                                               ada_b.unsqueeze(2).to_broadcast([P, 6 * KT, 2]), ALU.add))
        self.free(i, s)
        c.dve.wait(s)
        g1 = self.cols[:, COLUMNS["norm1_2"]:COLUMNS["norm1_2"] + KT]
        g2 = self.cols[:, COLUMNS["norm2_2"]:COLUMNS["norm2_2"] + KT]
        for x in range(2):
            c.dve.mark(nc.vector.scalar_tensor_tensor(gain1[:, :, x], mod[:, KT:2 * KT, x], 1.0, g1,
                                                      ALU.add, ALU.mult))
        s = c.dve.mark(nc.vector.scalar_tensor_tensor(gain2[:, :], mod[:, 4 * KT:5 * KT, 0], 1.0, g2,
                                                      ALU.add, ALU.mult))
        self.modulated = s


    def linear_attention(self, z, gqk, gv, gr, silu, projected, mixed_free):
        c, nc, d = self.c, self.nc, self.d
        mem = Memory(nc)
        w2, w2_in = self.const(mem, "gate_w2", [2 * GLA_RANK, 512])
        masks, masks_in = self.const(mem, "leaf_masks", [JT, 4, JT])
        total = mem("decay_sum", [P, 2, 2, T + 1])
        gate = Memory(nc)
        logit = gate("gate_logit", [P, T])
        soft = gate("gate_soft", [P, T])
        ones_row = gate("ones_row", [P, T])
        s = c.dve.mark(nc.vector.memset(ones_row[:, :], 1.0))
        zero = c.dve.mark(nc.vector.memset(total[:, :, :, 0:1], 0.0))
        c.pe.wait(w2_in, *projected)
        for g in range(4):
            for h in range(2):
                i = self.take()
                done = c.pe.mark(nc.tensor.matmul(c.bank(i, HT), w2[:, P * g:P * (g + 1)],
                                                  z[:, HT * h:HT * (h + 1)], start=True, stop=True))
                c.act.wait(done, c.dve.now)
                self.free(i, c.act.mark(nc.scalar.activation(
                    logit[:, HT * h:HT * (h + 1)], c.bank(i, HT), ACT.Identity,
                    bias=self.col("gate_b", g), scale=1.0)))
            c.act.wait(c.act.now)
            c.act.mark(nc.scalar.activation(soft[:, :], logit[:, :], ACT.Abs))
            c.act.wait(c.act.now)
            c.act.mark(nc.scalar.activation(soft[:, :], soft[:, :], ACT.Exp, scale=-1.0))
            c.act.wait(c.act.now)
            s = c.act.mark(nc.scalar.activation(soft[:, :], soft[:, :], ACT.Ln, bias=self.ones[:, 0:1],
                                                scale=1.0))
            c.dve.wait(s, c.dve.now)
            s = c.dve.mark(nc.vector.scalar_tensor_tensor(soft[:, :], logit[:, :], 0.0, soft[:, :],
                                                          ALU.min, ALU.subtract))
            c.dve.wait(s)
            s = c.dve.mark(nc.vector.tensor_tensor_scan(total[:, g // 2, g % 2, 1:T + 1], ones_row[:, :],
                                                        soft[:, :], 0.0, ALU.mult, ALU.add))
        self.modulation_products()
        for lane in (c.pe, c.act, c.dve):
            lane.wait(c.dve.now, c.act.now)
        gate.close()

        levels = [4 * JT, 2 * JT, JT, LEAF]
        both = [[mem(f"half_{s}_{r}", [P, 2, T]) for r in range(2)] for s in levels]
        leaf = [[mem(f"leaf_{r}_{w}", [P, 2, T]) for w in range(2)] for r in range(2)]
        step = mem("decay_step", [P, 2, T])
        q, k = gqk[:, 0:2, :], gqk[:, 2:4, :]
        inv_tau = 1.0 / GLA_TAU
        for r in range(2):
            run = total[:, r, :, 1:T + 1] if r == 0 else total[:, r, :, 0:T]
            for s, dst in zip(levels, both):
                dst = dst[r]
                nb = T // (2 * s)
                mid = s - 1 if r == 0 else s
                rv = run.rearrange("p a (b n) -> p a b n", n=2 * s)
                c.dve.wait(c.act.now, c.dve.now)
                for a in range(2):
                    x = c.dve.mark(nc.vector.tensor_tensor(
                        step[:, a, :].rearrange("p (b n) -> p b n", n=2 * s), rv[:, a, :, :],
                        rv[:, a, :, mid:mid + 1].to_broadcast([P, nb, 2 * s]), ALU.subtract))
                sign_left = -inv_tau
                sign_right = inv_tau
                c.act.wait(x)
                for a in range(2):
                    sv = step[:, a, :].rearrange("p (b n) -> p b n", n=2 * s)
                    dvw = dst[:, a, :].rearrange("p (b n) -> p b n", n=2 * s)
                    c.act.mark(nc.scalar.activation(dvw[:, :, 0:s], sv[:, :, 0:s], ACT.Exp, scale=sign_left))
                    e = c.act.mark(nc.scalar.activation(dvw[:, :, s:2 * s], sv[:, :, s:2 * s], ACT.Exp,
                                                        scale=sign_right))
                c.dve.wait(e)
                for a in range(2):
                    for side, src in ((0, k if r == 0 else q), (1, q if r == 0 else k)):
                        dvw = dst[:, a, :].rearrange("p (b n) -> p b n", n=2 * s)[:, :, side * s:(side + 1) * s]
                        svw = src[:, a, :].rearrange("p (b n) -> p b n", n=2 * s)[:, :, side * s:(side + 1) * s]
                        c.dve.mark(nc.vector.tensor_tensor(dvw, dvw, svw, ALU.mult))
            mid = LEAF // 2
            rv = run.rearrange("p a (b n) -> p a b n", n=LEAF)
            c.dve.wait(c.act.now, c.dve.now)
            for a in range(2):
                x = c.dve.mark(nc.vector.tensor_tensor(
                    step[:, a, :].rearrange("p (b n) -> p b n", n=LEAF), rv[:, a, :, :],
                    rv[:, a, :, mid:mid + 1].to_broadcast([P, T // LEAF, LEAF]), ALU.subtract))
            c.act.wait(x)
            sign = inv_tau if r == 0 else -inv_tau
            c.act.mark(nc.scalar.activation(leaf[r][0][:, :, :], step[:, :, :], ACT.Exp, scale=sign))
            e = c.act.mark(nc.scalar.activation(leaf[r][1][:, :, :], step[:, :, :], ACT.Exp, scale=-sign))
            c.dve.wait(e)
            c.dve.mark(nc.vector.tensor_tensor(leaf[r][0][:, :, :], leaf[r][0][:, :, :], q, ALU.mult))
            c.dve.mark(nc.vector.tensor_tensor(leaf[r][1][:, :, :], leaf[r][1][:, :, :], k, ALU.mult))
        scaled = c.dve.now
        self.modulation_columns()

        groups = []
        for r in range(2):
            a = both[0][r]
            for g in range(2):
                groups.append(([(4 * r + 2 * g + x, HT * (1 - r), HT, a, a) for x in range(2)], None))
        for r in range(2):
            a = both[1][r]
            groups.append(([(4 * b + 2 * r + x, 4 * JT * b + 2 * JT * (1 - r), 2 * JT, a, a)
                            for b in range(2) for x in range(2)], None))
        groups.append(([(2 * b + r, JT * (2 * b + 1 - r), JT, both[2][r], both[2][r])
                        for r in range(2) for b in range(4)], None))
        for r in range(2):
            groups.append(([(j, JT * j, JT, both[3][r], both[3][r]) for j in range(NJ)], r))
        for r in range(2):
            groups.append(([(j, JT * j, JT, leaf[r][1], leaf[r][0]) for j in range(NJ)], 2 + r))

        weight = step[0:JT, :, :]
        o = total[:, 0, 0, 0:T]
        norm = (total[:, 0, 1, 0:SEQ], total[:, 1, 0, 0:SEQ])
        c.act.wait(scaled)
        c.act.wait(*projected)
        silu_done = c.act.mark(nc.scalar.activation(silu[:, :, :], gr[:, :, :], ACT.Silu))
        c.pe.wait(scaled, masks_in)
        c.dve.wait(masks_in)
        weight_free = [None, None]
        n_group = 0
        for head in range(GLA_HEADS):
            a, at = head // 2, 64 * (head % 2)
            rows = slice(at, at + 64)
            c.pe.wait(c.bank_free[6], c.bank_free[7])
            started = [False, False]
            total_left = sum(len(p) for p, _ in groups)
            pending = None

            def apply(pending):
                pieces, slot, ready = pending
                c.pe.wait(ready)
                nonlocal_left = None
                for n, (jt, i0, ni, _, _) in enumerate(pieces):
                    half = i0 // HT
                    ins = nc.tensor.matmul(
                        self.c.psum[:, 6 + half, i0 - HT * half:i0 - HT * half + ni],
                        gv[:, jt, P * head:P * (head + 1)], weight[:, slot, ni * n:ni * (n + 1)],
                        start=not started[half], stop=True, skip_group_check=True)
                    started[half] = True
                weight_free[slot] = c.pe.mark(ins)

            for pieces, mask in groups:
                slot = n_group % 2
                n_group += 1
                j = self.take_pair(3)
                for n, (jt, i0, ni, ka, qa) in enumerate(pieces):
                    ins = nc.tensor.matmul(
                        self.c.psum[0:JT, j + ni * n // HT, ni * n % HT:ni * n % HT + ni],
                        ka[rows, a, JT * jt:JT * (jt + 1)], qa[rows, a, i0:i0 + ni],
                        start=True, stop=True, skip_group_check=True)
                done = c.pe.mark(ins)
                dst = weight[:, slot, :].rearrange("p (b n) -> p b n", n=HT)
                if mask is None:
                    lane = c.act if slot else c.dve
                    lane.wait(done, weight_free[slot])
                    if lane is c.act:
                        ready = c.act.mark(nc.scalar.activation(dst, self.pair(j, JT), ACT.Copy))
                    else:
                        ready = c.dve.mark(nc.vector.tensor_copy(dst, self.pair(j, JT)))
                else:
                    c.dve.wait(done, weight_free[slot])
                    for half in range(2):
                        ready = c.dve.mark(nc.vector.tensor_tensor(
                            dst[:, half, :].rearrange("p (a n) -> p a n", n=JT),
                            self.c.psum[0:JT, j + half, 0:HT].rearrange("p (a n) -> p a n", n=JT),
                            masks[:, mask:mask + 1, :].to_broadcast([JT, HT // JT, JT]), ALU.mult))
                self.free(j, ready)
                self.free(j + 1, ready)
                if pending:
                    apply(pending)
                pending = (pieces, slot, ready)
            apply(pending)
            c.act.wait(c.pe.now, c.dve.now)
            got = c.act.mark(nc.scalar.activation(o.rearrange("p (b n) -> p b n", n=HT),
                                                  self.pair(6), ACT.Copy))
            self.free(6, got)
            self.free(7, got)
            c.act.wait(mixed_free)
            c.dve.wait(mixed_free, silu_done, got)
            self.head_norm(norm, "gla", o[:, META:T], DA_HEADS + head, self.col("gla_norm"), [got],
                           silu[:, head, :])
        c.fence()
        mem.close()

    def attention(self, dq, dk, dv, projected):
        c, nc, d = self.c, self.nc, self.d
        mem = Memory(nc)
        cos, cos_in = self.const(mem, "rope_cos", [P, T])
        sin, sin_in = self.const(mem, "rope_sin", [P, T])
        swap, swap_in = self.const(mem, "rope_swap", [P, P])
        lam4, lam_in = self.const(mem, "lambdas", [DA_DIM, 4])
        turned = mem("rope_turned", [P, SEQ])
        lam = mem("lambda", [P, 4])

        c.dve.wait(lam_in)
        s = c.dve.mark(nc.vector.tensor_tensor(lam4[:, 0:2], lam4[:, 0:2], lam4[:, 2:4], ALU.mult))
        c.pe.wait(s)
        i = self.take()
        s = c.pe.mark(nc.tensor.matmul(c.bank(i, 2), self.ones[0:DA_DIM, :], lam4[:, 0:2], start=True, stop=True))
        c.act.wait(s)
        s = c.act.mark(nc.scalar.activation(lam[:, 0:2], c.bank(i, 2), ACT.Exp))
        self.free(i, s)
        c.dve.wait(s)
        s = c.dve.mark(nc.vector.tensor_tensor(lam[:, 2:3], lam[:, 1:2], lam[:, 0:1], ALU.subtract))
        c.dve.wait(s)
        c.dve.mark(nc.vector.tensor_scalar(lam[:, 3:4], lam[:, 2:3], -LAM_INIT, None, ALU.add))

        c.pe.wait(swap_in, *projected)
        c.dve.wait(cos_in, sin_in)
        for x, n0 in ((dq, META), (dk, 0)):
            n_all = T - n0
            ranges = [(0, SEQ)] if n_all == SEQ else [(0, HT), (HT, T)]
            for h in range(DA_HEADS):
                for lo, hi in ranges:
                    i = self.take()
                    done = c.pe.mark(nc.tensor.matmul(c.bank(i, hi - lo), swap[:, :], x[:, h, lo:hi],
                                                      start=True, stop=True))
                    c.dve.wait(done, c.dve.now)
                    s = c.dve.mark(nc.vector.tensor_tensor(turned[:, 0:hi - lo], c.bank(i, hi - lo),
                                                           sin[:, n0 + lo:n0 + hi], ALU.mult))
                    self.free(i, s)
                    s = c.dve.mark(nc.vector.tensor_tensor(x[:, h, lo:hi], x[:, h, lo:hi],
                                                           cos[:, n0 + lo:n0 + hi], ALU.mult))
                    c.dve.wait(s)
                    s = c.dve.mark(nc.vector.tensor_tensor(x[:, h, lo:hi], x[:, h, lo:hi],
                                                           turned[:, 0:hi - lo], ALU.add))
        rotated = c.dve.now

        e = mem("exp_scores", [P, 2, 2, T])
        stat = mem("softmax_stats", [P, 2, 8])
        mix = mem("mixed_scores", [P, 2, T])
        mix_t = mem("mixed_scores_t", [P, 2, 5, P])
        o = mem("da_out", [P, SEQ])
        norm = (mem("da_square", [P, SEQ]), mem("da_inverse", [P, SEQ]))
        scale = DA_DIM ** -0.5
        steps = [(h, qt) for h in range(DA_HEADS) for qt in range(SEQ // P)]
        key_tiles = [(t, min(P, T - P * t)) for t in range(5)]
        c.pe.wait(rotated)
        mixed_at, turned_at, applied_at = {}, {}, {}
        self.ring = 0

        def scores(n):
            h, qt = steps[n]
            v = n % 2
            for m in range(2):
                rows = slice(64 * m, 64 * m + 64)
                j = 2 * m
                c.pe.wait(c.bank_free[j], c.bank_free[j + 1])
                for g in range(2):
                    ins = nc.tensor.matmul(c.bank(j + g, HT), dq[rows, h, P * qt:P * (qt + 1)],
                                           dk[rows, h, HT * g:HT * (g + 1)], start=True, stop=True)
                done = c.pe.mark(ins)
                st = stat[:, v, :]
                c.dve.wait(done, mixed_at.get(n - 2))
                s = c.dve.mark(nc.vector.tensor_reduce(st[:, m:m + 1], self.pair(j), AX.XY, ALU.max))
                c.dve.wait(s)
                s = c.dve.mark(nc.vector.tensor_scalar(st[:, 2 + m:3 + m], st[:, m:m + 1], -scale, None, ALU.mult))
                c.act.wait(s, mixed_at.get(n - 2))
                s = c.act.mark(nc.scalar.activation(
                    e[:, v, m, :].rearrange("p (b n) -> p b n", n=HT), self.pair(j), ACT.Exp,
                    bias=st[:, 2 + m:3 + m], scale=scale, accum_out=st[:, 4 + m:5 + m]))
                self.free(j, s)
                self.free(j + 1, s)
            return s

        def mixing(n, exped):
            v = n % 2
            st = stat[:, v, :]
            c.dve.wait(exped, turned_at.get(n - 2))
            s = c.dve.mark(nc.vector.reciprocal(st[:, 6:8], st[:, 4:6]))
            c.dve.wait(s)
            s = c.dve.mark(nc.vector.tensor_scalar(st[:, 7:8], st[:, 7:8], lam[:, 3:4], None, ALU.mult))
            s = c.dve.mark(nc.vector.tensor_scalar(mix[:, v, :], e[:, v, 0, :], st[:, 6:7], None, ALU.mult))
            c.dve.wait(s)
            mixed_at[n] = c.dve.mark(nc.vector.scalar_tensor_tensor(
                mix[:, v, :], e[:, v, 1, :], st[:, 7:8], mix[:, v, :], ALU.mult, ALU.add))

        def applying(n):
            h, qt = steps[n]
            v = n % 2
            c.pe.wait(mixed_at[n], c.bank_free[4], c.bank_free[5])
            for t, m in key_tiles:
                bank, off = (4, P * t) if t < 4 else (5, 0)
                ins = nc.tensor.transpose(self.c.psum[0:m, bank, off:off + P], mix[:, v, P * t:P * t + m],
                                          self.ident[:, :])
            turned_at[n] = c.pe.mark(ins)
            c.act.wait(turned_at[n], applied_at.get(n - 2))
            s = c.act.mark(nc.scalar.activation(mix_t[:, v, 0:4, :].rearrange("p a b -> p (a b)"),
                                                c.bank(4), ACT.Copy))
            self.free(4, s)
            s = c.act.mark(nc.scalar.activation(mix_t[0:META, v, 4, :], c.bank(5, P, META), ACT.Copy))
            self.free(5, s)
            c.pe.wait(s)
            if qt == 0:
                c.pe.wait(c.bank_free[6])
            for t, m in key_tiles:
                ins = nc.tensor.matmul(self.c.psum[:, 6, P * qt:P * (qt + 1)], dv[0:m, t, P * h:P * (h + 1)],
                                       mix_t[0:m, v, t, :], start=t == 0, stop=t == 4)
            applied_at[n] = c.pe.mark(ins)
            if qt == SEQ // P - 1:
                c.act.wait(applied_at[n], c.dve.now)
                got = c.act.mark(nc.scalar.activation(o[:, :], c.bank(6), ACT.Copy))
                self.free(6, got)
                self.ring = 7
                self.head_norm(norm, "da", o[:, :], h, self.gain_da, [got])

        gain = mem("da_gain", [P, 1])
        c.dve.wait(c.dve.now)
        s = c.dve.mark(nc.vector.tensor_scalar(gain[:, :], self.col("da_norm"), 1.0 - LAM_INIT, None, ALU.mult))
        self.gain_da = gain[:, 0:1]
        for n in range(len(steps) + 1):
            if n < len(steps):
                exped = scores(n)
            if n >= 1:
                applying(n - 1)
            if n < len(steps):
                mixing(n, exped)
        c.fence()
        mem.close()


    def experts(self):
        c, nc, d = self.c, self.nc, self.d
        parts = (self.x_high, self.x_low)
        scratch = Memory(nc)
        self.norm_buffers(scratch, "norm2", SEQ)
        xn = self.rms(self.h, SEQ, lambda t: self.col("ln2", t), self.added, parts)
        self.spill = self.value
        self.spilled, self.n_spilled = [], 0
        self.xn = xn
        self.route(parts, xn)
        c.fence()
        for lane in (c.act, c.pool, c.dve):
            lane.wait(*self.spilled[-4:])
        scratch.close()

        mem = Memory(nc)
        acc = mem("expert_sum", [P, KT, SEQ])
        gates = mem("gates", [P, 2, SEQ // TC, EG, TC])
        act = mem("expert_act", [P, 2, EG, SEQ])
        hid_high = mem("hidden_high", [P, 2, EG, SEQ], BF16)
        hid_low = mem("hidden_low", [P, 2, EG, SEQ], BF16)
        n_groups = NK // EG
        loaded, gated, hidden, hidden_free = {}, {}, {}, {}

        def load_group(g):
            signals = [c.dma(c.sp, f"gates_in_{g % 2}", gates[:, g % 2, :, :, :],
                             self.gate_dram[:, :, EG * g:EG * (g + 1), :].rearrange("c p b n -> p c b n"),
                             [self.gates_written, gated.get(g - 2)])]
            if g < AHEAD:
                signals.append(c.dma(c.sp, f"act_in_{g % 2}", act[:, g % 2, :, :],
                                     self.act_dram[EG * g:EG * (g + 1)].rearrange("b p n -> p b n"),
                                     [self.spilled[EG * g:EG * (g + 1)]]))
            loaded[g] = signals

        def gate_tile(g, b, after):
            slot = g % 2
            c.dve.wait(after, *loaded[g])
            a = act[:, slot, b, :]
            v = a.rearrange("p (c n) -> p c n", n=TC)
            w = c.dve.mark(nc.vector.tensor_tensor(v, v, gates[:, slot, :, b, :], ALU.mult))
            gated[g] = hidden[g] = split_value(c, a, hid_high[:, slot, b, :], hid_low[:, slot, b, :],
                                               [w, hidden_free.get(g - 2)])

        def hidden_group(g):
            if g < AHEAD:
                for b in range(EG):
                    gate_tile(g, b, None)
                return
            block = self.w.next("u")
            for b in range(EG):
                def evacuate(psum, done, b=b):
                    c.act.wait(done, gated.get(g - 2))
                    s = c.act.mark(nc.scalar.activation(act[:, g % 2, b, :], psum, ACT.Gelu))
                    gate_tile(g, b, s)
                    return s
                done = self.linear(block, slice(P * b, P * (b + 1)), parts, slice(0, SEQ), SEQ, P,
                                   xn, evacuate)
            self.w.release(done)

        def down(g):
            block = self.w.next("v")
            c.pe.wait(block[2], hidden[g])
            for t in range(KT):
                i = self.take()
                for b in range(EG):
                    ins = three_products(c, c.bank(i), (block[0][:, b, P * t:P * (t + 1)],
                                                        block[1][:, b, P * t:P * (t + 1)]),
                                         (hid_high[:, g % 2, b, :], hid_low[:, g % 2, b, :]),
                                         b == 0, b == EG - 1)
                done = c.pe.mark(ins)
                c.dve.wait(done)
                if g == 0:
                    s = c.dve.mark(nc.vector.tensor_copy(acc[:, t, :], c.bank(i)))
                else:
                    c.dve.wait(self.acc_at[t])
                    s = c.dve.mark(nc.vector.tensor_tensor(acc[:, t, :], c.bank(i), acc[:, t, :], ALU.add))
                self.acc_at[t] = s
                self.free(i, s)
            hidden_free[g] = done
            self.w.release(done)

        self.acc_at = [None] * KT
        load_group(0)
        load_group(1)
        hidden_group(0)
        for g in range(n_groups):
            if g + 1 < n_groups:
                hidden_group(g + 1)
            if g + 2 < n_groups:
                load_group(g + 2)
            down(g)
        self.added = []
        for t in range(KT):
            c.dve.wait(self.acc_at[t])
            self.added.append(c.dve.mark(nc.vector.tensor_tensor(self.h[:, t, :], self.h[:, t, :], acc[:, t, :],
                                                                 ALU.add)))
        c.fence()
        mem.close()

    def fill(self, n):
        c, nc = self.c, self.nc
        for g in range(self.n_spilled, min(self.n_spilled + n, AHEAD)):
            block = self.w.next("u")
            for b in range(EG):
                slot, tile = b % 4, EG * g + b

                def evacuate(psum, done):
                    c.act.wait(done, self.spilled[tile - 4] if tile >= 4 else None)
                    s = c.act.mark(nc.scalar.activation(self.spill[:, slot, :], psum, ACT.Gelu))
                    self.spilled.append(c.dma(c.sp, f"act_out_{slot}", self.act_dram[tile],
                                              self.spill[:, slot, :], [s]))
                    return s
                done = self.linear(block, slice(P * b, P * (b + 1)), (self.x_high, self.x_low),
                                   slice(0, SEQ), SEQ, P, self.xn, evacuate)
            self.w.release(done)
            self.n_spilled += 1

    def route(self, parts, xn):
        c, nc, d = self.c, self.nc, self.d
        mem = Memory(nc)
        iota16, iota16_in = self.const(mem, "iota_picks", [P, TOPK])
        pick_b = mem("picks_t_bf16", [P, 4, SEQ], BF16)

        top = Memory(nc)
        keys, keys_in = self.const(top, "sub_keys", [P, 2 * PH, NK])
        score = top("scores", [P, SEQ // P, 2 * PH, NK])
        query = top("queries", [P, 2, SEQ])
        query_free = [None, None]
        c.pe.wait(keys_in)
        for g in range(4):
            block = self.w.next("peer_q")
            for f in range(4):
                hp = 4 * g + f
                got = {}

                def keep(psum, done, hp=hp):
                    c.act.wait(done, query_free[hp % 2])
                    got[0] = c.act.mark(nc.scalar.activation(query[:, hp % 2, :], psum, ACT.Copy))
                    return got[0]
                done = self.linear(block, slice(P * f, P * (f + 1)), parts, slice(0, SEQ), SEQ, P,
                                   xn, keep)
                i = self.take()
                c.pe.wait(got[0])
                for t in range(SEQ // P):
                    ins = nc.tensor.matmul(self.c.psum[:, i, NK * t:NK * (t + 1)],
                                           query[:, hp % 2, P * t:P * (t + 1)], keys[:, hp, :],
                                           start=True, stop=True)
                query_free[hp % 2] = c.pe.mark(ins)
                c.act.wait(query_free[hp % 2])
                s = c.act.mark(nc.scalar.activation(score[:, :, hp, :],
                                                    c.bank(i).rearrange("p (t k) -> p t k", k=NK), ACT.Copy))
                self.free(i, s)
            self.w.release(query_free[hp % 2])
        scored = c.act.now

        best = top("best_side", [P, 2 * PH, TOPK])
        best_i = top("best_side_index", [P, 2 * PH, TOPK], U32)
        best_f = top("best_side_index_f", [P, 2 * PH, TOPK])
        cand = top("pair_scores", [P, PH, TOPK, TOPK])
        pair = top("best_pair", [P, PH, TOPK])
        shifted = top("best_pair_shifted", [P, PH, TOPK])
        pair_i = top("best_pair_index", [P, PH, TOPK], U32)
        rank_i = top("best_rank_index", [P, 2, PH, TOPK], U32)
        rank = top("best_rank", [P, 2, PH, TOPK])
        hot = cand
        pick = top("picks", [P, 3, PICKS])
        tot = top("gate_sum", [P, 2, PH])
        LOW = -3.0e38
        c.dve.wait(scored, iota16_in)

        def top16(values, out, index):
            s = c.dve.mark(nc.vector.max(out[:, 0:8], values))
            c.dve.wait(s)
            c.dve.mark(nc.vector.max_index(index[:, 0:8], out[:, 0:8], values))
            c.dve.wait(c.dve.now)
            s = c.dve.mark(nc.vector.match_replace(values, out[:, 0:8], values, LOW))
            c.dve.wait(s)
            s = c.dve.mark(nc.vector.max(out[:, 8:16], values))
            c.dve.wait(s)
            c.dve.mark(nc.vector.max_index(index[:, 8:16], out[:, 8:16], values))

        for t in range(SEQ // P):
            c.dve.wait(c.dve.now, c.act.now)
            for hp in range(2 * PH):
                top16(score[:, t, hp, :], best[:, hp, :], best_i[:, hp, :])
            c.dve.wait(c.dve.now)
            c.dve.mark(nc.vector.tensor_copy(best_f[:, :, :], best_i[:, :, :]))
            sides = best[:, :, :].rearrange("p (h s) k -> p h s k", s=2)
            for h in range(PH):
                c.dve.mark(nc.vector.tensor_tensor(
                    cand[:, h, :, :], sides[:, h, 0, :].unsqueeze(2).to_broadcast([P, TOPK, TOPK]),
                    sides[:, h, 1, :].unsqueeze(1).to_broadcast([P, TOPK, TOPK]), ALU.add))
            c.dve.wait(c.dve.now)
            for h in range(PH):
                top16(cand[:, h, :, :].rearrange("p a b -> p (a b)"), pair[:, h, :], pair_i[:, h, :])
            c.dve.wait(c.dve.now)
            s = c.dve.mark(nc.vector.tensor_tensor(shifted[:, :, :], pair[:, :, :],
                                                   pair[:, :, 0:1].to_broadcast([P, PH, TOPK]), ALU.subtract))
            c.dve.mark(nc.vector.tensor_scalar(rank_i[:, 0, :, :], pair_i[:, :, :], 4, None,
                                               ALU.logical_shift_right))
            c.dve.mark(nc.vector.tensor_scalar(rank_i[:, 1, :, :], pair_i[:, :, :], 15, None, ALU.bitwise_and))
            c.act.wait(s)
            gate = pick[:, 2, :].rearrange("p (h k) -> p h k", k=TOPK)
            e = c.act.mark(nc.scalar.activation(gate, shifted[:, :, :], ACT.Exp))
            c.dve.wait(c.dve.now, e)
            c.dve.mark(nc.vector.tensor_reduce(tot[:, 0, :], gate, AX.X, ALU.add))
            c.dve.mark(nc.vector.tensor_copy(rank[:, :, :, :], rank_i[:, :, :, :]))
            c.dve.wait(c.dve.now)
            c.dve.mark(nc.vector.reciprocal(tot[:, 1, :], tot[:, 0, :]))
            c.dve.wait(c.dve.now)
            c.dve.mark(nc.vector.tensor_tensor(gate, gate, tot[:, 1, :].unsqueeze(2).to_broadcast([P, PH, TOPK]),
                                               ALU.mult))
            bf = best_f[:, :, :].rearrange("p (h s) k -> p h s k", s=2)
            for side in range(2):
                for h in range(PH):
                    c.dve.mark(nc.vector.tensor_tensor(
                        hot[:, h, :, :], rank[:, side, h, :].unsqueeze(2).to_broadcast([P, TOPK, TOPK]),
                        iota16[:, :].unsqueeze(1).to_broadcast([P, TOPK, TOPK]), ALU.is_equal))
                c.dve.wait(c.dve.now)
                for h in range(PH):
                    c.dve.mark(nc.vector.tensor_tensor(
                        hot[:, h, :, :], hot[:, h, :, :],
                        bf[:, h, side, :].unsqueeze(1).to_broadcast([P, TOPK, TOPK]), ALU.mult))
                c.dve.wait(c.dve.now)
                s = c.dve.mark(nc.vector.tensor_reduce(
                    pick[:, side, :].rearrange("p (h k) -> p h k", k=TOPK), hot[:, :, :, :], AX.X, ALU.add))
                c.dve.wait(s)
            self.fill(AHEAD_TOP)
            i = self.take()
            c.pe.wait(c.dve.now)
            for x in range(3):
                ins = nc.tensor.transpose(self.c.psum[:, i, P * x:P * (x + 1)], pick[:, x, :], self.ident[:, :])
            done = c.pe.mark(ins)
            c.act.wait(done)
            s = c.act.mark(nc.scalar.activation(pick_b[:, 0:3, P * t:P * (t + 1)],
                                                c.bank(i, 3 * P).rearrange("p (x n) -> p x n", n=P), ACT.Copy))
            c.dve.wait(s)
            s = c.dve.mark(nc.vector.tensor_tensor(pick_b[:, 3, P * t:P * (t + 1)],
                                                   self.c.psum[:, i, 2 * P:3 * P],
                                                   pick_b[:, 2, P * t:P * (t + 1)], ALU.subtract))
            self.free(i, s)
        c.fence()
        top.close()

        hot_mem = Memory(nc)
        iota32, iota_in = self.const(hot_mem, "iota_keys", [P, NK])
        iota = hot_mem("iota_bf16", [P, NK, OC], BF16)
        left = hot_mem("one_hot_a", [P, 2, NK, OC], BF16)
        right = hot_mem("one_hot_b", [P, 2, NK, OC], BF16)
        gated = hot_mem("gated_one_hot_b", [P, 2, 2, NK, OC], BF16)
        mats = hot_mem("gate_matrices", [P, 2, NK, TC])
        hot_free, mats_out = {}, {}
        c.dve.wait(c.dve.now, iota_in)
        s = c.dve.mark(nc.vector.tensor_copy(iota[:, :, :], iota32[:, :].unsqueeze(2).to_broadcast([P, NK, OC])))
        c.dve.wait(s)
        for n in range(SEQ // OC):
            v = n % 2
            tok = slice(OC * n, OC * (n + 1))

            def spread(x):
                return pick_b[:, x, tok].unsqueeze(1).to_broadcast([P, NK, OC])
            c.dve.wait(hot_free.get(n - 2))
            c.dve.mark(nc.vector.tensor_tensor(left[:, v, :, :], iota[:, :, :], spread(0), ALU.is_equal))
            s = c.dve.mark(nc.vector.tensor_tensor(right[:, v, :, :], iota[:, :, :], spread(1), ALU.is_equal))
            c.dve.wait(s)
            c.dve.mark(nc.vector.tensor_tensor(gated[:, v, 0, :, :], right[:, v, :, :], spread(2), ALU.mult))
            ready = c.dve.mark(nc.vector.tensor_tensor(gated[:, v, 1, :, :], right[:, v, :, :], spread(3), ALU.mult))
            c.pe.wait(ready)
            chunk, half = n // (TC // OC), n % (TC // OC)
            for q in range(OC // 4):
                i = self.take()
                for x in range(4):
                    tk = 4 * q + x
                    for part in range(2):
                        ins = nc.tensor.matmul(self.c.psum[:, i, NK * x:NK * (x + 1)], left[:, v, :, tk],
                                               gated[:, v, part, :, tk], start=part == 0, stop=part == 1)
                done = c.pe.mark(ins)
                at = OC * half + 4 * q
                lane = c.act
                lane.wait(done, mats_out.get(chunk - 2))
                dst = mats[:, chunk % 2, :, at:at + 4].rearrange("p b x -> p x b")
                src = c.bank(i).rearrange("p (x b) -> p x b", b=NK)
                s = lane.mark(nc.scalar.activation(dst, src, ACT.Copy))
                self.free(i, s)
            hot_free[n] = done
            if n % 6 == 2:
                self.fill(1)
            if half == TC // OC - 1:
                mats_out[chunk] = c.dma(c.sp, f"gates_out_{chunk % 2}", self.gate_dram[chunk],
                                        mats[:, chunk % 2, :, :], [s])
        self.gates_written = [mats_out[chunk], mats_out[chunk - 1]]
        c.fence()
        for lane in (c.pe, c.act, c.dve, c.pool):
            lane.wait(*self.gates_written)
        hot_mem.close()
        mem.close()
        self.fill(AHEAD)


    def second(self):
        c, nc, d = self.c, self.nc, self.d
        parts = (self.x_high, self.x_low)
        outer = Memory(nc)
        self.norm_buffers(outer, "norm_2", SEQ)
        residual = self.rms(self.h, SEQ, lambda t: self.col("final1", t), self.added, None,
                            fp32_out=self.h)

        mod, gain1, gain2 = self.mod, self.gain1, self.gain2

        ctx_high = outer("ctx_high", [P, KT, CTX], BF16)
        ctx_low = outer("ctx_low", [P, KT, CTX], BF16)
        heads = Memory(nc)
        kt = heads("na_k", [P, 4, KEYS2])
        vt = heads("na_v", [P, KEYS2 // P, 512])
        qt = heads("na_q", [P, 4, SEQ])
        ctx = qt[:, :, :].rearrange("p f (a n) -> p (f a) n", n=CTX)
        landed = self.load("in_ctx", ctx, d["ctx"])
        c.act.wait(self.modulated)
        xn = self.rms(self.h, SEQ, lambda t: gain1[:, t, 0:1], residual, parts,
                      shift=lambda t: mod[:, t, 0:1])
        ctx_n = self.rms(ctx, CTX, lambda t: gain1[:, t, 1:2], [landed],
                         (ctx_high, ctx_low), shift=lambda t: mod[:, t, 1:2])
        fin = heads("fourier_x", [P, 2, SEQ])
        ain = heads("conv_a", [P, 2, SEQ])
        gin = heads("conv_gate", [P, 2, SEQ])

        def keep(lane, dst, func=None):
            def evacuate(psum, done):
                lane.wait(done)
                if lane is c.act:
                    return lane.mark(nc.scalar.activation(dst, psum, func or ACT.Copy))
                return lane.mark(nc.vector.tensor_copy(dst, psum))
            return evacuate

        block = self.w.next("k2")
        for f in range(4):
            cols = slice(P * f, P * (f + 1))
            self.linear(block, cols, parts, slice(0, SEQ), SEQ, P, xn, keep(c.dve, kt[:, f, 0:SEQ]))
            done = self.linear(block, cols, (ctx_high, ctx_low), slice(0, CTX), CTX, P, ctx_n,
                               keep(c.act, kt[:, f, SEQ:KEYS2]))
        self.w.release(done)
        block = self.w.next("v2")
        for j in range(KEYS2 // P):
            src, at = (parts, P * j) if j < 4 else ((ctx_high, ctx_low), P * (j - 4))
            i = self.take()
            c.pe.wait(block[2])
            done = c.pe.mark(self.token_product(c.bank(i), block, slice(0, 512), src, slice(at, at + P)))
            self.free(i, keep(c.act if j % 2 else c.dve, vt[:, j, :])(c.bank(i), done))
        self.w.release(done)
        for name, dsts in (("q2", [qt[:, f, :] for f in range(4)]), ("fourier_in", [fin[:, f, :] for f in range(2)]),
                           ("conv_in", [ain[:, 0, :], ain[:, 1, :], gin[:, 0, :], gin[:, 1, :]])):
            block = self.w.next(name)
            for f, dst in enumerate(dsts):
                gate = name == "conv_in" and f >= 2
                lane = c.act if gate or f % 2 else c.dve
                done = self.linear(block, slice(P * f, P * (f + 1)), parts, slice(0, SEQ), SEQ, P, xn,
                                   keep(lane, dst, ACT.Sigmoid if gate else None))
            self.w.release(done)
        c.fence()
        self.fourier(fin)
        self.convolution(ain, gin)
        self.neighbourhood(qt, kt, vt)
        c.fence()
        heads.close()

        mixed = c.dve.now
        self.added = []
        for g in range(2):
            block = self.w.next("w_out_2")
            for f in range(4):
                t = 4 * g + f

                def add(psum, done, t=t):
                    c.dve.wait(done)
                    self.added.append(c.dve.mark(nc.vector.scalar_tensor_tensor(
                        self.h[:, t, :], psum, mod[:, 2 * KT + t, 0:1], self.h[:, t, :], ALU.mult, ALU.add)))
                    return self.added[-1]
                done = self.linear(block, slice(P * f, P * (f + 1)), parts, slice(0, SEQ), SEQ, P,
                                   [mixed], add)
            self.w.release(done)
        xn = self.rms(self.h, SEQ, lambda t: gain2[:, t:t + 1], self.added, parts,
                      shift=lambda t: mod[:, 3 * KT + t, 0:1])

        mem = Memory(nc)
        hid_high = mem("mlp_high", [P, 4 * KT, SEQ], BF16)
        hid_low = mem("mlp_low", [P, 4 * KT, SEQ], BF16)
        relu = self.square[:, 0:2, :]
        relu_free = [None, None]
        for g in range(8):
            block = self.w.next("mlp_1")
            for f in range(4):
                t = 4 * g + f

                def evacuate(psum, done, t=t):
                    r = relu[:, t % 2, :]
                    c.act.wait(done, relu_free[t % 2])
                    s = c.act.mark(nc.scalar.activation(r, psum, ACT.Relu))
                    c.dve.wait(s)
                    w = c.dve.mark(nc.vector.tensor_tensor(r, r, r, ALU.mult))
                    relu_free[t % 2] = split_value(c, r, hid_high[:, t, :], hid_low[:, t, :], [w])
                    return s
                done = self.linear(block, slice(P * f, P * (f + 1)), parts, slice(0, SEQ), SEQ, P,
                                   xn, evacuate)
            self.w.release(done)
        hidden = c.dve.now
        c.pe.wait(hidden, *c.bank_free)
        for g in range(8):
            block = self.w.next("mlp_2")
            c.pe.wait(block[2])
            for t in range(KT):
                for k in range(4):
                    ins = three_products(c, c.bank(t), (block[0][:, k, P * t:P * (t + 1)],
                                                        block[1][:, k, P * t:P * (t + 1)]),
                                         (hid_high[:, 4 * g + k, :], hid_low[:, 4 * g + k, :]),
                                         g == 0 and k == 0, g == 7 and k == 3)
                if g == 7:
                    done = c.pe.mark(ins)
                    c.dve.wait(done)
                    self.free(t, c.dve.mark(nc.vector.scalar_tensor_tensor(
                        self.h[:, t, :], c.bank(t), mod[:, 5 * KT + t, 0:1], self.h[:, t, :],
                        ALU.mult, ALU.add)))
            done = c.pe.mark(ins) if g < 7 else done
            self.w.release(done)
        c.fence()
        mem.close()

        self.rms(self.h, SEQ, lambda t: self.col("final2", t), [c.dve.now], None, fp32_out=self.h)
        stored = self.c.dma(c.sp, "out_stored", self.out, self.h[:, :, :], [c.dve.now])
        c.sp.wait(stored)
        outer.close()

    def fourier(self, x):
        c, nc, d = self.c, self.nc, self.d
        mem = Memory(nc)
        chan, chan_in = self.const(mem, "dft_channels", [P, 2, P])
        tok, tok_in = self.const(mem, "dft_tokens", [P, 2, 4, SEQ])
        wf, wf_in = self.const(mem, "w_fourier", [P, 2, FFT_CH])
        y = self.square[:, :, :].rearrange("p a (b n) -> p (a b) n", n=FFT_CH).rearrange("p (r t) n -> p r t n", r=2)
        f = self.value[:, 0:2, :]
        c.pe.wait(chan_in, tok_in, wf_in)
        for part in range(2):
            for t in range(4):
                i = self.take()
                for g in range(2):
                    ins = nc.tensor.matmul(self.c.psum[:, i, P * g:P * (g + 1)], x[:, g, P * t:P * (t + 1)],
                                           chan[:, part, :], start=True, stop=True)
                done = c.pe.mark(ins)
                c.act.wait(done)
                s = c.act.mark(nc.scalar.activation(y[:, part, t, :], c.bank(i, FFT_CH), ACT.Copy))
                self.free(i, s)
        c.pe.wait(s)
        for g in range(2):
            i = self.take()
            for part in range(2):
                for t in range(4):
                    ins = nc.tensor.matmul(c.bank(i), y[:, part, t, P * g:P * (g + 1)], tok[:, part, t, :],
                                           start=part == 0 and t == 0, stop=part == 1 and t == 3)
            done = c.pe.mark(ins)
            c.act.wait(done)
            s = c.act.mark(nc.scalar.activation(f[:, g, :], c.bank(i), ACT.Copy))
            self.free(i, s)
        c.pe.wait(s)
        self.small_out(wf, f, 0, None)
        c.fence()
        mem.close()

    def small_out(self, w, x, dst, bias):
        c, nc = self.c, self.nc
        val = self.value[:, 2:4, :]
        for g in range(2):
            i = self.take()
            for k in range(2):
                ins = nc.tensor.matmul(c.bank(i), w[:, k, P * g:P * (g + 1)], x[:, k, :], start=k == 0, stop=k == 1)
            done = c.pe.mark(ins)
            c.act.wait(done)
            s = c.act.mark(nc.scalar.activation(val[:, g, :], c.bank(i), ACT.Identity, scale=1.0,
                                                bias=self.col(bias, g) if bias else 0.0))
            self.free(i, s)
            c.act.wait(s)
            split_value(c, val[:, g, :], self.x_high[:, dst + g, 0:SEQ], self.x_low[:, dst + g, 0:SEQ], [s])
        c.fence()

    def convolution(self, a, gate):
        c, nc, d = self.c, self.nc, self.d
        mem = Memory(nc)
        pw, pw_in = self.const(mem, "conv_pw_w", [P, 2, 256])
        half = TAPS // 2
        v = mem("conv_padded", [P, 2, SEQ + 2 * half])
        y, sq = self.square[:, 0:2, :], self.square[:, 2:4, :]
        mean, inv = self.value[:, 0, :], self.inverse[:, 0:SEQ]
        s = c.dve.mark(nc.vector.memset(v[:, :, :], 0.0))
        c.dve.wait(s)
        s = c.dve.mark(nc.vector.tensor_tensor(v[:, :, half:half + SEQ], a[:, :, :], gate[:, :, :], ALU.mult))
        c.dve.wait(s)
        for tap in range(TAPS):
            for g in range(2):
                src = v[:, g, tap:tap + SEQ]
                w = self.cols[:, COLUMNS["conv_w"] + TAPS * g + tap:COLUMNS["conv_w"] + TAPS * g + tap + 1]
                if tap == 0:
                    c.dve.mark(nc.vector.tensor_scalar(y[:, g, :], src, w, self.col("conv_b", g), ALU.mult, ALU.add))
                else:
                    c.dve.wait((c.dve.sem, c.dve.count - 1))
                    c.dve.mark(nc.vector.scalar_tensor_tensor(y[:, g, :], src, w, y[:, g, :], ALU.mult, ALU.add))
        i, summed = self.mean_square(lambda t: y[:, t, :], 2, SEQ, [c.dve.now])
        c.act.wait(summed)
        s = c.act.mark(nc.scalar.activation(mean[:, :], c.bank(i), ACT.Copy, scale=1.0 / 256))
        self.free(i, s)
        c.dve.wait(s, c.dve.now)
        for g in range(2):
            s = c.dve.mark(nc.vector.tensor_tensor(y[:, g, :], y[:, g, :], mean[:, :], ALU.subtract))
        c.act.wait(s)
        s = c.act.mark(nc.scalar.activation(sq[:, :, :], y[:, :, :], ACT.Square))
        i, summed = self.mean_square(lambda t: sq[:, t, :], 2, SEQ, [s])
        s, last = self.inverse_root(inv[:, :], c.bank(i), SEQ, 1.0 / 256, self.eps[:, 1:2], [summed])
        self.free(i, s)
        c.dve.wait(last)
        for g in range(2):
            s = c.dve.mark(nc.vector.tensor_tensor(y[:, g, :], y[:, g, :], inv[:, :], ALU.mult))
            c.act.wait(s)
            s = c.act.mark(nc.scalar.activation(y[:, g, :], y[:, g, :], ACT.Silu, scale=self.col("conv_ln_g", g),
                                                bias=self.col("conv_ln_b", g)))
        c.pe.wait(s, pw_in)
        self.small_out(pw, y, 2, "conv_pw_b")
        c.fence()
        mem.close()

    def neighbourhood(self, q, k, v):
        c, nc, d = self.c, self.nc, self.d
        mem = Memory(nc)
        mask, mask_in = self.const(mem, "window", [P, GW])
        bias = mem("bias", [P, 2, NBIAS, GW])
        e = mem("na_exp", [P, 2, KEYS2])
        et = mem("na_exp_t", [P, 2, KEYS2 // P, P])
        stat = mem("na_stats", [P, 2, 8])
        o = mem("na_out", [P, SEQ])
        scale = HD2 ** -0.5
        steps = [(h, t) for h in range(NH2) for t in range(SEQ // P)]
        normed_at, turned_at, applied_at, bias_at = {}, {}, {}, {}
        last_add = {}
        c.dve.wait(mask_in)

        def bias_in(h):
            got = self.load(f"bias_in_{h % 2}", bias[:, h % 2, :, :], d["bias"][h], [last_add.get(h - 2)])
            c.dve.wait(got)
            bias_at[h] = c.dve.mark(nc.vector.tensor_tensor(
                bias[:, h % 2, :, :], bias[:, h % 2, :, :],
                mask[:, :].unsqueeze(1).to_broadcast([P, NBIAS, GW]), ALU.add))

        def scores(n):
            h, t = steps[n]
            x = n % 2
            rows = slice(64 * (h % 2), 64 * (h % 2) + 64)
            j = 2 * x
            c.pe.wait(c.bank_free[j], c.bank_free[j + 1])
            lhs = q[rows, h // 2, P * t:P * (t + 1)]
            nc.tensor.matmul(c.bank(j), lhs, k[rows, h // 2, 0:SEQ], start=True, stop=True)
            done = c.pe.mark(nc.tensor.matmul(c.bank(j + 1, CTX), lhs, k[rows, h // 2, SEQ:KEYS2],
                                              start=True, stop=True))
            st, es = stat[:, x, :], e[:, x, :]
            c.dve.wait(done, turned_at.get(n - 2), bias_at[h], normed_at.get(n - 2))
            first = ROWS - 2 - 2 * t
            s = c.dve.mark(nc.vector.scalar_tensor_tensor(
                es[:, 0:SEQ], c.bank(j), scale,
                bias[:, h % 2, first:first + ROWS, :].rearrange("p a b -> p (a b)"), ALU.mult, ALU.add))
            last_add[h] = s
            s2 = c.dve.mark(nc.vector.tensor_scalar(es[:, SEQ:KEYS2], c.bank(j + 1, CTX), scale, None, ALU.mult))
            self.free(j, s)
            self.free(j + 1, s2)
            c.dve.wait(s2)
            s = c.dve.mark(nc.vector.tensor_reduce(st[:, 0:1], es, AX.X, ALU.max))
            c.dve.wait(s)
            s = c.dve.mark(nc.vector.tensor_scalar(st[:, 1:2], st[:, 0:1], -1.0, None, ALU.mult))
            c.act.wait(s)
            return c.act.mark(nc.scalar.activation(es, es, ACT.Exp, bias=st[:, 1:2], scale=1.0,
                                                   accum_out=st[:, 2:3]))

        def norm(n, exped):
            x = n % 2
            st = stat[:, x, :]
            c.dve.wait(exped)
            s = c.dve.mark(nc.vector.reciprocal(st[:, 3:4], st[:, 2:3]))
            c.dve.wait(s)
            normed_at[n] = c.dve.mark(nc.vector.tensor_scalar(e[:, x, :], e[:, x, :], st[:, 3:4], None, ALU.mult))

        def applying(n):
            h, t = steps[n]
            x = n % 2
            c.pe.wait(normed_at[n], c.bank_free[4], c.bank_free[5])
            for y in range(KEYS2 // P):
                ins = nc.tensor.transpose(self.c.psum[:, 4 + y // 4, P * (y % 4):P * (y % 4 + 1)],
                                          e[:, x, P * y:P * (y + 1)], self.ident[:, :])
            turned_at[n] = c.pe.mark(ins)
            c.act.wait(turned_at[n], applied_at.get(n - 2))
            s = c.act.mark(nc.scalar.activation(et[:, x, 0:4, :].rearrange("p a b -> p (a b)"), c.bank(4), ACT.Copy))
            self.free(4, s)
            s = c.act.mark(nc.scalar.activation(et[:, x, 4:6, :].rearrange("p a b -> p (a b)"), c.bank(5, CTX),
                                                ACT.Copy))
            self.free(5, s)
            bank = 6 + h // 2 % 2
            rows = slice(64 * (h % 2), 64 * (h % 2) + 64)
            c.pe.wait(s)
            if t == 0 and h % 2 == 0:
                c.pe.wait(c.bank_free[bank])
            for y in range(KEYS2 // P):
                ins = nc.tensor.matmul(self.c.psum[rows, bank, P * t:P * (t + 1)],
                                       v[:, y, HD2 * h:HD2 * (h + 1)], et[:, x, y, :],
                                       start=y == 0, stop=y == KEYS2 // P - 1)
            applied_at[n] = c.pe.mark(ins)
            if t == SEQ // P - 1 and h % 2 == 1:
                c.act.wait(applied_at[n], c.dve.now)
                got = c.act.mark(nc.scalar.activation(o[:, :], c.bank(bank), ACT.Copy))
                self.free(bank, got)
                c.act.wait(got)
                split_value(c, o[:, :], self.x_high[:, 4 + h // 2, 0:SEQ], self.x_low[:, 4 + h // 2, 0:SEQ], [got])

        bias_in(0)
        bias_in(1)
        for n in range(len(steps) + 1):
            if n < len(steps):
                h, t = steps[n]
                if t == 0 and 1 <= h < NH2 - 1:
                    bias_in(h + 1) if h >= 1 else None
                exped = scores(n)
            if n >= 1:
                applying(n - 1)
            if n < len(steps):
                norm(n, exped)
        c.fence()
        mem.close()


_WIDTHS = (("ln1", KT), ("ln2", KT), ("final1", KT), ("da_norm", 1), ("gla_norm", 1), ("gate_b", 4),
           ("c", KT), ("c_ctx", KT), ("ada_b", 6 * KT), ("norm1_2", KT), ("norm2_2", KT), ("final2", KT),
           ("conv_w", 2 * TAPS), ("conv_b", 2), ("conv_ln_g", 2), ("conv_ln_b", 2), ("conv_pw_b", 2))
COLUMNS, _at = {}, 0
for _name, _n in _WIDTHS:
    COLUMNS[_name] = _at
    _at += _n
N_COLUMNS = _at


def shape_constants():
    out = {"identity": np.eye(P, dtype=np.float32)}
    inv = np.power(np.float32(500000.0), -np.arange(0, ROPE, 2, dtype=np.float32) / np.float32(ROPE)).astype(np.float32)
    ang = (np.arange(T, dtype=np.float32)[:, None] * inv[None, :]).astype(np.float32)
    cos, sin = np.ones((P, T), np.float32), np.zeros((P, T), np.float32)
    swap = np.zeros((P, P), np.float32)
    hr = ROPE // 2
    for o in (0, DA_DIM):
        for i in range(hr):
            cos[o + i] = cos[o + hr + i] = np.cos(ang[:, i])
            sin[o + i] = sin[o + hr + i] = np.sin(ang[:, i])
            swap[o + hr + i, o + i] = -1.0
            swap[o + i, o + hr + i] = 1.0
    out.update(rope_cos=cos, rope_sin=sin, rope_swap=swap)
    j, i = np.arange(JT)[:, None], np.arange(JT)[None, :]
    same = (j // LEAF) == (i // LEAF)
    masks = [(j < LEAF) & (i >= LEAF), (j >= LEAF) & (i < LEAF), same & (j <= i), same & (j >= i)]
    out["leaf_masks"] = np.ascontiguousarray(np.stack(masks, 1).astype(np.float32))
    out["iota_picks"] = np.broadcast_to(np.arange(TOPK, dtype=np.float32), (P, TOPK)).copy()
    out["iota_keys"] = np.broadcast_to(np.arange(NK, dtype=np.float32), (P, NK)).copy()
    m = FFT_CH // FFT_G
    a = 2 * np.pi * (np.outer(np.arange(m), np.arange(m)) % m) / m
    chan = np.zeros((P, 2, P))
    for g in range(2):
        chan[m * g:m * (g + 1), 0, m * g:m * (g + 1)] = np.cos(a)
        chan[m * g:m * (g + 1), 1, m * g:m * (g + 1)] = np.sin(a)
    out["dft_channels"] = chan.astype(np.float32)
    a = 2 * np.pi * (np.outer(np.arange(SEQ), np.arange(SEQ)) % SEQ) / SEQ
    norm = 1.0 / math.sqrt(SEQ * m)
    tok = np.stack([np.cos(a), -np.sin(a)]) * norm
    out["dft_tokens"] = np.ascontiguousarray(tok.reshape(2, 4, P, SEQ).transpose(2, 0, 1, 3)).astype(np.float32)
    col = np.arange(GW)
    start = np.clip(col - WC // 2, 0, GW - WC)
    seen = (col[None, :] >= start[:, None]) & (col[None, :] < start[:, None] + WC)
    out["window"] = np.tile(np.where(seen, 0.0, -1e30).astype(np.float32), (2, 1))
    return out


def lay_out(inputs):
    g = {k: np.asarray(v) for k, v in inputs.items()}

    def tiles(x):
        return x.reshape((x.shape[0] // P, P) + x.shape[1:]).swapaxes(0, 1)

    out = dict(shape_constants())
    tokens = np.concatenate([g["meta_tokens"], g["x"][0]], axis=0)
    out["tokens"] = tiles(tokens.T)
    out["ctx"] = tiles(g["ctx_2"][0].T)
    out["w_in"] = g["w_in"][0]
    out["w_out"] = g["w_out"][0]
    out["peer_w_q"] = g["peer_w_q"][0]
    u = g["peer_u"][0].reshape(NK, NK // EG, EG, KT, P)
    out["peer_u"] = u.transpose(1, 4, 3, 2, 0).reshape(NK // EG, P, KT * EG * NK)
    out["peer_v"] = g["peer_v"][0].reshape(NK, NK, D).transpose(1, 0, 2)
    out["sub_keys"] = g["peer_sub_keys"][0].reshape(2 * PH, NK, P).transpose(2, 0, 1)
    w2 = np.zeros((2 * GLA_RANK, 512), np.float32)
    w2[:GLA_RANK, :256] = g["gla_gate_w2_f"][0]
    w2[GLA_RANK:, 256:] = g["gla_gate_w2_b"][0]
    out["gate_w2"] = w2
    out["lambdas"] = np.stack([g[f"da_lambda_{n}"][0] for n in ("q1", "q2", "k1", "k2")], axis=1)
    out["ada_w"] = g["ada_w_2"][0]
    out["w_in_2"] = g["w_in_2"][0]
    out["w_out_2"] = g["w_out_2"][0]
    out["mlp_w1"] = g["mlp_w1_2"][0]
    out["mlp_w2"] = g["mlp_w2_2"][0]
    out["w_fourier"] = tiles(g["w_fourier_2"][0])
    out["conv_pw_w"] = tiles(g["conv_pw_w_2"][0])
    rpb = g["na_rpb_2"][0]
    row, colq = np.arange(P) // GW, np.arange(P) % GW
    off_r = np.arange(NBIAS)[None, :, None] + 1 - row[:, None, None]
    off_c = np.clip(np.arange(GW)[None, None, :] - colq[:, None, None] + WC - 1, 0, 2 * WC - 2)
    out["bias"] = rpb[:, off_r, off_c]
    gate_b = np.concatenate([g["gla_gate_b_f"][0], g["gla_gate_b_b"][0]])
    conv_w = g["conv_dw_w_2"][0].T.reshape(2, P, TAPS).transpose(1, 0, 2).reshape(P, 2 * TAPS)
    columns = {
        "ln1": tiles(g["ln1_w"][0]), "ln2": tiles(g["ln2_w"][0]), "final1": tiles(g["final_norm_w"]),
        "da_norm": tiles(g["da_subln_w"][0]), "gla_norm": tiles(g["gla_norm_w"][0]), "gate_b": tiles(gate_b),
        "c": tiles(g["c_2"][0]), "c_ctx": tiles(g["c_ctx_2"]), "ada_b": tiles(g["ada_b_2"][0]),
        "norm1_2": tiles(g["norm1_g_2"][0]), "norm2_2": tiles(g["norm2_g_2"][0]),
        "final2": tiles(g["final_norm_g_2"]), "conv_w": conv_w, "conv_b": tiles(g["conv_dw_b_2"][0]),
        "conv_ln_g": tiles(g["conv_norm_g_2"][0]), "conv_ln_b": tiles(g["conv_norm_b_2"][0]),
        "conv_pw_b": tiles(g["conv_pw_b_2"][0]),
    }
    out["columns"] = np.concatenate([columns[n] for n, _ in _WIDTHS], axis=1)
    return {k: np.ascontiguousarray(v) for k, v in out.items()}


def kernel(**inputs):
    import concourse.bacc as bacc
    from concourse.bass_utils import run_bass_kernel_spmd

    arrays = lay_out(inputs)
    nc = bacc.Bacc("TRN2", target_bir_lowering=False, num_devices=1)
    dram = {name: nc.dram_tensor(f"{name}_dram", a.shape, mybir.dt.from_np(a.dtype), kind="ExternalInput").ap()
            for name, a in arrays.items()}
    out = nc.dram_tensor("out_dram", (P, KT, SEQ), F32, kind="ExternalOutput").ap()
    gate_dram = nc.dram_tensor("gate_dram", (SEQ // TC, P, NK, TC), F32, kind="Internal").ap()
    act_dram = nc.dram_tensor("act_dram", (EG * AHEAD, P, SEQ), F32, kind="Internal").ap()
    Net(nc, dram, out, gate_dram, act_dram).build()
    got = run_bass_kernel_spmd(nc, [{f"{n}_dram": a for n, a in arrays.items()}], core_ids=[0])
    y = np.asarray(got.results[0]["out_dram"])
    return np.ascontiguousarray(y.transpose(2, 1, 0).reshape(1, SEQ, D))
```

```python
import math
from contextlib import ExitStack

import numpy as np

import concourse.bass as bass
import concourse.mybir as mybir

F32 = mybir.dt.float32
BF16 = mybir.dt.bfloat16
U32 = mybir.dt.uint32
ALU = mybir.AluOpType
ACT = mybir.ActivationFunctionType
AX = mybir.AxisListType

P = 128
D = 1024
KT = D // P
BANK = 512
SEQ, META = 512, 16
T = SEQ + META
HT = T // 2
DA_HEADS, DA_DIM, ROPE = 4, 64, 16
LAM_INIT = 0.8 - 0.6 * math.exp(0.0)
GLA_HEADS, GLA_RANK, GLA_TAU = 4, 16, 16.0
JT = 66
NJ = T // JT
LEAF = JT // 2
EPS, LN_EPS = 1e-6, 1e-5
PH, NK, TOPK = 8, 128, 16
PICKS = PH * TOPK
EG = 4
TC = 32
AHEAD = 18
GROUPS = [AHEAD] + list(range(AHEAD)) + list(range(AHEAD + 1, NK // EG))
OC = 16
CTX = 256
NH2, HD2 = 8, 64
GW, ROWS, WC, WR = 64, 8, 16, 8
NBIAS = 2 * ROWS - 2
TAPS = 31
FFT_CH, FFT_G = 256, 4
KEYS2 = SEQ + CTX


class Lane:

    def __init__(self, nc, engine, name):
        self.engine, self.sem = engine, nc.alloc_semaphore(name)
        self.count, self.seen = 0, {}

    def wait(self, *signals):
        for s in signals:
            if s is None:
                continue
            if isinstance(s, list):
                self.wait(*s)
                continue
            sem, value = s
            if self.seen.get(id(sem), 0) < value:
                self.engine.wait_ge(sem, value)
                self.seen[id(sem)] = value

    def mark(self, instruction):
        instruction.then_inc(self.sem, 1)
        self.count += 1
        return (self.sem, self.count)

    @property
    def now(self):
        return (self.sem, self.count) if self.count else None


class Core:

    def __init__(self, nc):
        self.nc = nc
        self.pe = Lane(nc, nc.tensor, "pe_steps")
        self.act = Lane(nc, nc.scalar, "act_steps")
        self.dve = Lane(nc, nc.vector, "dve_steps")
        self.pool = Lane(nc, nc.gpsimd, "pool_steps")
        self.sp = Lane(nc, nc.sync, "sp_steps")
        self.psum = nc.alloc_psum_tensor("psum", [P, 8, BANK], F32)
        self.bank_free = [None] * 8
        self.dma_sems = {}

    def bank(self, i, n=BANK, m=P):
        return self.psum[0:m, i, 0:n]

    def dma(self, lane, name, out, in_, after=()):
        lane.wait(*after)
        if name not in self.dma_sems:
            self.dma_sems[name] = [self.nc.alloc_semaphore(name), 0]
        entry = self.dma_sems[name]
        lane.engine.dma_start(out, in_).then_inc(entry[0], 16)
        entry[1] += 16
        return (entry[0], entry[1])

    def fence(self):
        signals = [x.now for x in (self.pe, self.act, self.dve, self.pool)]
        for lane in (self.pe, self.act, self.dve, self.pool):
            lane.wait(*signals)


class Memory:

    def __init__(self, nc):
        self.nc, self.stack = nc, ExitStack()

    def __call__(self, name, shape, dtype=F32):
        return self.stack.enter_context(self.nc.sbuf_tensor(name, shape, dtype))

    def close(self):
        self.stack.close()


class WeightStream:
    STAGES, SPLITS = 2, 3
    SIZE = 4096

    def __init__(self, core, plan):
        nc = core.nc
        self.core, self.plan = core, plan
        self.stage = nc.alloc_sbuf_tensor("weight_stage", [P, self.STAGES, self.SIZE], F32)
        self.high = nc.alloc_sbuf_tensor("weight_high", [P, self.SPLITS, self.SIZE], BF16)
        self.low = nc.alloc_sbuf_tensor("weight_low", [P, self.SPLITS, self.SIZE], BF16)
        self.stage_free, self.used = {}, {}
        self.loaded, self.split_done = [], {}
        self.n_split = self.n_next = 0

    def start(self, inputs):
        self.inputs = inputs
        self.pump()
        self.split()

    def view(self, buf, slot, n):
        rows, cols = self.plan[n][1].shape[1], self.plan[n][1].shape[2]
        return buf[:, slot, 0:rows * cols].rearrange("p (r c) -> p r c", c=cols)

    def pump(self):
        while len(self.loaded) < len(self.plan):
            n = len(self.loaded)
            if n >= self.STAGES and n - self.STAGES not in self.stage_free:
                return
            slot = n % self.STAGES
            free = self.stage_free.get(n - self.STAGES, self.inputs if n else [])
            self.loaded.append(self.core.dma(self.core.sp, f"weights_in_{slot}",
                                             self.view(self.stage, slot, n), self.plan[n][1], free))

    def split(self):
        n = self.n_split
        self.n_split += 1
        if n >= len(self.plan) or self.plan[n][2]:
            return
        c, slot = self.core, n % self.SPLITS
        stage = self.view(self.stage, n % self.STAGES, n)
        high, low = self.view(self.high, slot, n), self.view(self.low, slot, n)
        free = self.used.get(n - self.SPLITS)
        c.act.wait(self.loaded[n], free)
        h = c.act.mark(c.nc.scalar.activation(high, stage, ACT.Copy))
        c.pool.wait(self.loaded[n], free, h)
        lo = c.pool.mark(c.nc.gpsimd.tensor_tensor(low, stage, high, ALU.subtract))
        self.stage_free[n] = [h, lo]
        self.split_done[n] = lo
        self.pump()

    def next(self, name):
        n = self.n_next
        assert self.plan[n][0] == name, (self.plan[n][0], name)
        self.n_next += 1
        self.split()
        if self.plan[n][2]:
            return self.view(self.stage, n % self.STAGES, n), None, self.loaded[n]
        return (self.view(self.high, n % self.SPLITS, n), self.view(self.low, n % self.SPLITS, n),
                self.split_done[n])

    def release(self, signal):
        n = self.n_next - 1
        self.used[n] = signal
        if self.plan[n][2]:
            self.stage_free[n] = [signal]
            self.pump()


def three_products(core, out, left, right, first, last):
    pairs = ((0, 0), (0, 1), (1, 0))
    for i, (a, b) in enumerate(pairs):
        ins = core.nc.tensor.matmul(out, left[a], right[b], start=first and i == 0,
                                    stop=last and i == len(pairs) - 1)
    return ins


def split_value(core, value, high, low, after):
    core.act.wait(*after)
    h = core.act.mark(core.nc.scalar.activation(high, value, ACT.Copy))
    core.dve.wait(h, *after)
    return core.dve.mark(core.nc.vector.tensor_tensor(low, value, high, ALU.subtract))


class Net:

    def __init__(self, nc, d, out, gate_dram, act_dram):
        self.nc, self.d, self.out, self.gate_dram, self.act_dram = nc, d, out, gate_dram, act_dram
        self.c = Core(nc)
        self.ring = 0


    def take(self, banks=(0, 1, 2, 3, 4, 5, 6, 7)):
        i = banks[self.ring % len(banks)]
        self.ring += 1
        self.c.pe.wait(self.c.bank_free[i])
        return i

    def take_pair(self, n=4):
        j = 2 * (self.ring % n)
        self.ring += 1
        self.c.pe.wait(self.c.bank_free[j], self.c.bank_free[j + 1])
        return j

    def free(self, i, signal):
        self.c.bank_free[i] = signal

    def pair(self, j, m=P, n=HT):
        return self.c.psum[0:m, j:j + 2, 0:n]

    def load(self, name, out, in_, after=()):
        return self.c.dma(self.c.pool, name, out, in_, after)

    def const(self, mem, name, shape):
        t = mem(name, shape)
        full = t[tuple(slice(0, n) for n in shape)]
        return t, self.load(f"in_{name}", full, self.d[name])

    def mean_square(self, square, n_tiles, n, after, banks=(0, 1, 2, 3, 4, 5, 6, 7)):
        c = self.c
        c.pe.wait(*after)
        i = self.take(banks)
        for t in range(n_tiles):
            ins = c.nc.tensor.matmul(c.bank(i, n), self.ones[:, :], square(t),
                                     start=t == 0, stop=t == n_tiles - 1)
        return i, c.pe.mark(ins)

    def inverse_root(self, dst, banks, n, scale, eps, after):
        c = self.c
        c.act.wait(*after)
        s = c.act.mark(c.nc.scalar.activation(dst, banks, ACT.Sqrt, bias=eps, scale=scale))
        c.dve.wait(s)
        return s, c.dve.mark(c.nc.vector.reciprocal(dst, dst))

    def norm_buffers(self, mem, tag, n):
        self.square = mem(f"{tag}_square", [P, 4, n])
        self.inverse = mem(f"{tag}_inverse", [P, n])
        self.value = mem(f"{tag}_value", [P, 4, n])
        self.square_free = [None] * 4

    def rms(self, x, n, gain, after, store, shift=None, fp32_out=None):
        c, nc = self.c, self.nc
        ranges = [(0, n)] if n <= BANK else [(0, HT), (HT, n)]
        sq, inv, val = self.square, self.inverse, self.value
        banks = [self.take() for _ in ranges]
        parts_free = c.pe.now
        for t in range(KT):
            c.act.wait(after[t % len(after)], self.square_free[t % 4])
            s = c.act.mark(nc.scalar.activation(sq[:, t % 4, 0:n], x[:, t, 0:n], ACT.Square))
            c.pe.wait(s)
            for b, (lo, hi) in zip(banks, ranges):
                ins = nc.tensor.matmul(c.bank(b, hi - lo), self.ones[:, :], sq[:, t % 4, lo:hi],
                                       start=t == 0, stop=t == KT - 1, skip_group_check=True)
            self.square_free[t % 4] = c.pe.mark(ins)
        for b, (lo, hi) in zip(banks, ranges):
            s, last = self.inverse_root(inv[:, lo:hi], c.bank(b, hi - lo), n, 1.0 / D,
                                        self.eps[:, 0:1], [c.pe.now, c.dve.now])
            self.free(b, s)
        done, scaled = [None] * KT, {}
        c.act.wait(parts_free)
        c.dve.wait(parts_free, last)
        for t in range(KT + 2):
            if t < KT:
                v = fp32_out[:, t, 0:n] if fp32_out is not None else val[:, t % 4, 0:n]
                c.dve.wait(done[t - 4] if t >= 4 else last)
                s = c.dve.mark(nc.vector.scalar_tensor_tensor(v, x[:, t, 0:n], gain(t), inv[:, 0:n],
                                                              ALU.mult, ALU.mult))
                if store is None:
                    done[t] = s
                    continue
                c.act.wait(s)
                h = c.act.mark(nc.scalar.activation(store[0][:, t, 0:n], v, ACT.Identity, scale=1.0,
                                                    bias=shift(t) if shift else 0.0))
                scaled[t] = (v, h)
            if store is not None and t >= 2:
                u = t - 2
                v, h = scaled[u]
                c.dve.wait(h)
                if shift is None:
                    ins = nc.vector.tensor_tensor(store[1][:, u, 0:n], v, store[0][:, u, 0:n], ALU.subtract)
                else:
                    ins = nc.vector.scalar_tensor_tensor(store[1][:, u, 0:n], v, shift(u),
                                                         store[0][:, u, 0:n], ALU.add, ALU.subtract)
                done[u] = c.dve.mark(ins)
        return done

    def column_product(self, out, block, cols, parts, tokens, after=(), n_k=KT, first=True, last=True,
                       k0=0):
        high, low, _ = block
        for k in range(n_k):
            if after:
                self.c.pe.wait(after[k % len(after)])
            ins = three_products(self.c, out, (high[:, k, cols], low[:, k, cols]),
                                 (parts[0][:, k0 + k, tokens], parts[1][:, k0 + k, tokens]),
                                 first and k == 0, last and k == n_k - 1)
        return ins

    def token_product(self, out, block, cols, parts, tokens):
        high, low, _ = block
        for k in range(KT):
            ins = three_products(self.c, out, (parts[0][:, k, tokens], parts[1][:, k, tokens]),
                                 (high[:, k, cols], low[:, k, cols]), k == 0, k == KT - 1)
        return ins

    def linear(self, block, cols, parts, tokens, n, m, after, evacuate, **kw):
        c = self.c
        i = self.take()
        c.pe.wait(block[2])
        done = c.pe.mark(self.column_product(c.bank(i, n, m), block, cols, parts, tokens, after, **kw))
        self.free(i, evacuate(c.bank(i, n, m), done))
        return done


    def build(self):
        c, nc, d = self.c, self.nc, self.d
        sb = nc.alloc_sbuf_tensor
        plan = []

        def weights(name, src, raw=False):
            plan.append((name, src, raw))

        w_in = d["w_in"].rearrange("(t p) n -> p t n", p=P)
        for name, lo, hi in (("z", 3072, 3104), ("gla_qk", 1536, 2048), ("gla_v", 2048, 2560),
                             ("gla_r", 2560, 3072), ("da_q", 0, 512), ("da_k", 512, 1024),
                             ("da_v", 1024, 1536)):
            weights(name, w_in[:, :, lo:hi])
        for g in range(12):
            weights("ada", d["ada_w"].rearrange("(t p) n -> p t n", p=P)[:, :, BANK * g:BANK * (g + 1)])
        for g in range(2):
            weights("w_out", d["w_out"].rearrange("(t p) n -> p t n", p=P)[:, :, BANK * g:BANK * (g + 1)])
        for g in range(4):
            weights("peer_q", d["peer_w_q"].rearrange("(t p) n -> p t n", p=P)[:, :, BANK * g:BANK * (g + 1)])
        def up(g):
            weights("u", d["peer_u"][g].rearrange("p (t e) -> p t e", t=KT))

        for g in range(AHEAD):
            up(g)
        up(GROUPS[0])
        for i, g in enumerate(GROUPS):
            if i + 1 < len(GROUPS) and GROUPS[i + 1] >= AHEAD:
                up(GROUPS[i + 1])
            weights("v", d["peer_v"][EG * g:EG * (g + 1)].rearrange("b p n -> p b n"))
        w_in2 = d["w_in_2"].rearrange("(t p) n -> p t n", p=P)
        for name, lo, hi in (("conv_in", 256, 768), ("fourier_in", 0, 256), ("k2", 1280, 1792),
                             ("v2", 1792, 2304), ("q2", 768, 1280)):
            weights(name, w_in2[:, :, lo:hi])
        for g in range(2):
            weights("w_out_2", d["w_out_2"].rearrange("(t p) n -> p t n", p=P)[:, :, BANK * g:BANK * (g + 1)])
        for g in range(8):
            weights("mlp_1", d["mlp_w1"].rearrange("(t p) n -> p t n", p=P)[:, :, BANK * g:BANK * (g + 1)])
        for g in range(8):
            weights("mlp_2", d["mlp_w2"].rearrange("(t p) n -> p t n", p=P)[:, 4 * g:4 * g + 4, :])

        self.ones = sb("ones", [P, P], F32)
        self.ident = sb("identity", [P, P], F32)
        self.eps = sb("eps", [P, 2], F32)
        self.cols = sb("columns", [P, d["columns"].shape[1]], F32)
        c.pool.mark(nc.gpsimd.memset(self.ones[:, :], 1.0))
        c.pool.mark(nc.gpsimd.memset(self.eps[:, 0:1], EPS))
        c.pool.mark(nc.gpsimd.memset(self.eps[:, 1:2], LN_EPS))
        ready = [c.pool.now, self.load("in_identity", self.ident[:, :], d["identity"]),
                 self.load("in_columns", self.cols[:, :], d["columns"])]
        self.mod = sb("modulation", [P, 6 * KT, 2], F32)
        self.gain1 = sb("gain1", [P, KT, 2], F32)
        self.gain2 = sb("gain2", [P, KT], F32)
        self.cond = sb("condition", [P, KT, 2], F32)
        self.cond_parts = sb("condition_parts", [P, KT, 4], BF16)
        self.mod_rows = sb("modulation_rows", [P, BANK], F32)
        self.h = sb("residual", [P, KT, SEQ], F32)
        self.x_high = sb("x_high", [P, KT, T], BF16)
        self.x_low = sb("x_low", [P, KT, T], BF16)
        for lane in (c.pe, c.act, c.dve, c.pool):
            lane.wait(*ready)

        self.w = WeightStream(c, plan)
        self.mixer()
        self.experts()
        self.second()

    def col(self, name, t=0):
        at = COLUMNS[name] + t
        return self.cols[:, at:at + 1]


    def mixer(self):
        c, nc, d = self.c, self.nc, self.d
        parts = (self.x_high, self.x_low)
        outer = Memory(nc)
        z = outer("z", [2 * GLA_RANK, T])
        gqk = outer("gla_qk", [P, 4, T])
        gv = outer("gla_v", [JT, NJ, 512])
        gr = self.h[:, 0:4, :]
        da = Memory(nc)
        dq = da("da_q", [P, 4, SEQ])
        dk = da("da_k", [P, 4, T])
        dv = da("da_v", [P, 5, 512])

        first = Memory(nc)
        self.norm_buffers(first, "norm1", T)
        h0 = first("tokens_in", [P, KT, T])
        landed = [self.load(f"in_tokens_{g}", h0[:, 2 * g:2 * g + 2, :], d["tokens"][:, 2 * g:2 * g + 2, :])
                  for g in range(4)]
        self.w.start(landed)
        landed = [landed[t // 2] for t in range(KT)]
        xn = self.rms(h0, T, lambda t: self.col("ln1", t), landed, parts)
        cos, sin, swap = self.square[:, 0, :], self.square[:, 1, :], self.square[:, 2, 0:P]
        summed = list(self.square_free)
        self.rope = (cos, sin, swap, self.square[:, 3, :],
                     [self.load(f"in_{name}", dst, d[name], summed)
                      for name, dst in (("rope_cos", cos), ("rope_sin", sin), ("rope_swap", swap))])

        def keep(lane, dst, scale=1.0):
            def evacuate(psum, done):
                lane.wait(done)
                if lane is c.act:
                    return lane.mark(nc.scalar.activation(dst, psum, ACT.Identity, scale=scale))
                return lane.mark(nc.vector.tensor_scalar(dst, psum, scale, None, ALU.mult))
            return evacuate

        def full_columns(name, dst, n_tiles, m, scales):
            block = self.w.next(name)
            for f in range(n_tiles):
                for g in range(2):
                    tokens = slice(HT * g, HT * (g + 1))
                    lane = c.act if (f + g) % 2 else c.dve
                    done = self.linear(block, slice(P * f, P * f + m), parts, tokens, HT, m, xn,
                                       keep(lane, dst(f)[:, tokens], scales[f]))
            self.w.release(done)

        def seq_columns(name, dst):
            block = self.w.next(name)
            for f in range(4):
                lane = c.act if f % 2 else c.dve
                done = self.linear(block, slice(P * f, P * (f + 1)), parts, slice(META, T), SEQ, P,
                                   xn, keep(lane, dst[:, f, :]))
            self.w.release(done)

        def rows(name, dst, step, between=None):
            block = self.w.next(name)
            for j in range(-(-T // step)):
                if between is not None and j == 2:
                    between()
                m = min(step, T - step * j)
                i = self.take()
                c.pe.wait(block[2], *xn)
                done = c.pe.mark(self.token_product(c.bank(i, 512, m), block, slice(0, 512), parts,
                                                    slice(step * j, step * j + m)))
                self.free(i, keep(c.act if j % 2 else c.dve, dst[0:m, j, :])(c.bank(i, 512, m), done))
            self.w.release(done)

        full_columns("z", lambda f: z, 1, 2 * GLA_RANK, [1.0])
        full_columns("gla_qk", lambda f: gqk[:, f, :], 4, P, [0.125, 0.125, 1.0, 1.0])
        rows("gla_v", gv, JT)
        seq_columns("gla_r", gr)
        seq_columns("da_q", dq)
        full_columns("da_k", lambda f: dk[:, f, :], 4, P, [1.0] * 4)
        self.rotate(dq, META)
        rows("da_v", dv, P, lambda: self.rotate(dk, 0))
        mixed_free = c.pe.now
        projected = [c.act.now, c.dve.now]
        c.fence()
        first.close()
        self.attention(dq, dk, dv, projected)
        da.close()
        self.linear_attention(z, gqk, gv, gr, projected, mixed_free)

        c.pool.wait(c.pe.now, c.act.now, c.dve.now)
        landed = self.load("in_residual", self.h[:, :, :], d["tokens"][:, :, META:T])
        mixed = [self.mixed_at[-2]] * (KT - 1) + [self.mixed_at[-1]]
        self.added = []
        for g in range(2):
            block = self.w.next("w_out")
            for f in range(4):
                t = 4 * g + f

                def add(psum, done, t=t):
                    c.dve.wait(done, landed)
                    self.added.append(c.dve.mark(nc.vector.tensor_tensor(
                        self.h[:, t, :], psum, self.h[:, t, :], ALU.add)))
                    return self.added[-1]
                done = self.linear(block, slice(P * f, P * (f + 1)), parts, slice(0, SEQ), SEQ, P,
                                   mixed, add)
            self.w.release(done)
        c.fence()
        outer.close()

    def head_norm(self, sq, o, dst, gain, after, banks, extra=None):
        c, nc = self.c, self.nc
        inv = sq
        c.act.wait(*after, self.head_normed, self.head_summed)
        s = c.act.mark(nc.scalar.activation(sq, o, ACT.Square))
        yield
        i, summed = self.mean_square(lambda t: sq, 1, SEQ, [s], banks)
        self.head_summed = summed
        s, last = self.inverse_root(inv, c.bank(i), SEQ, 1.0 / P, self.eps[:, 0:1], [summed])
        self.free(i, s)
        yield
        c.dve.wait(last)
        s = c.dve.mark(nc.vector.scalar_tensor_tensor(sq, o, gain, inv, ALU.mult, ALU.mult))
        self.head_read = s
        if extra is not None:
            c.dve.wait(s)
            s = c.dve.mark(nc.vector.tensor_tensor(sq, sq, extra, ALU.mult))
        yield
        c.act.wait(s)
        h = c.act.mark(nc.scalar.activation(self.x_high[:, dst, 0:SEQ], sq, ACT.Copy))
        yield
        c.dve.wait(h)
        self.head_normed = c.dve.mark(nc.vector.tensor_tensor(
            self.x_low[:, dst, 0:SEQ], sq, self.x_high[:, dst, 0:SEQ], ALU.subtract))
        self.mixed_at.append(self.head_normed)

    def advance(self):
        if self.norming is not None:
            try:
                next(self.norming)
            except StopIteration:
                self.norming = None

    def start_norms(self):
        self.norming = self.head_normed = self.head_summed = self.head_read = None
        self.mixed_at = []

    def finish_norm(self):
        while self.norming is not None:
            self.advance()

    def modulation_start(self):
        c, nc, cond = self.c, self.nc, self.cond
        for x, name in enumerate(("c", "c_ctx")):
            at = COLUMNS[name]
            s = c.act.mark(nc.scalar.activation(cond[:, :, x], self.cols[:, at:at + KT], ACT.Silu))
        c.dve.wait(split_value(c, cond[:, :, :], self.cond_parts[:, :, 0:2], self.cond_parts[:, :, 2:4], [s]))
        self.cond_ready = c.dve.now
        self.modulated_blocks = 0
        self.mod_pending = None
        self.modulated = None

    def modulation_block(self, banks):
        c, nc = self.c, self.nc
        if self.mod_pending is not None:
            g, copied = self.mod_pending
            c.pe.wait(copied)
            i = self.take(banks)
            for f in range(4):
                ins = nc.tensor.transpose(c.psum[:, i, 4 * f:4 * f + 4], self.mod_rows[0:4, P * f:P * (f + 1)],
                                          self.ident[0:4, 0:4])
            turned = c.pe.mark(ins)
            c.dve.wait(turned)
            ada_b = self.cols[:, COLUMNS["ada_b"] + 4 * g:COLUMNS["ada_b"] + 4 * g + 4]
            sums = c.psum[:, i, 0:16].rearrange("p (f x) -> p f x", x=4)
            dst = self.mod[:, 4 * g:4 * g + 4, :]
            s = c.dve.mark(nc.vector.tensor_tensor(dst, sums[:, :, 0:2],
                                                   ada_b.unsqueeze(2).to_broadcast([P, 4, 2]), ALU.add))
            c.dve.wait(s)
            self.modulated = c.dve.mark(nc.vector.tensor_tensor(dst, dst, sums[:, :, 2:4], ALU.add))
            self.free(i, self.modulated)
            self.mod_turned = turned
            self.mod_pending = None
        g = self.modulated_blocks
        if g == 12:
            return
        self.modulated_blocks += 1
        high, low, split = self.w.next("ada")
        c.pe.wait(split, self.cond_ready)
        i = self.take(banks)
        for k in range(KT):
            nc.tensor.matmul(c.bank(i, BANK, 4), self.cond_parts[:, k, :], high[:, k, :], start=k == 0, stop=False)
            ins = nc.tensor.matmul(c.bank(i, BANK, 4), self.cond_parts[:, k, :], low[:, k, :], start=False,
                                   stop=k == KT - 1)
        summed = c.pe.mark(ins)
        self.w.release(summed)
        c.act.wait(summed, self.mod_turned if g else None)
        copied = c.act.mark(nc.scalar.activation(self.mod_rows[0:4, :], c.bank(i, BANK, 4), ACT.Copy))
        self.free(i, copied)
        self.mod_pending = (g, copied)

    def modulation_columns(self):
        c, nc = self.c, self.nc
        mod, gain1, gain2 = self.mod, self.gain1, self.gain2
        c.dve.wait(self.modulated)
        g1 = self.cols[:, COLUMNS["norm1_2"]:COLUMNS["norm1_2"] + KT]
        g2 = self.cols[:, COLUMNS["norm2_2"]:COLUMNS["norm2_2"] + KT]
        for x in range(2):
            c.dve.mark(nc.vector.scalar_tensor_tensor(gain1[:, :, x], mod[:, KT:2 * KT, x], 1.0, g1,
                                                      ALU.add, ALU.mult))
        s = c.dve.mark(nc.vector.scalar_tensor_tensor(gain2[:, :], mod[:, 4 * KT:5 * KT, 0], 1.0, g2,
                                                      ALU.add, ALU.mult))
        self.modulated = s


    def linear_attention(self, z, gqk, gv, gr, projected, mixed_free):
        c, nc, d = self.c, self.nc, self.d
        mem = Memory(nc)
        masks, masks_in = self.const(mem, "leaf_masks", [JT, 4, JT])
        total = mem("decay_sum", [P, 2, 2, T + 1])
        gate = Memory(nc)
        w2, w2_in = self.const(gate, "gate_w2", [2 * GLA_RANK, 512])
        logit = gate("gate_logit", [P, 4, T])
        soft = gate("gate_soft", [P, 4, T])
        ones_row = gate("ones_row", [P, T])
        s = c.dve.mark(nc.vector.memset(ones_row[:, :], 1.0))
        zero = c.dve.mark(nc.vector.memset(total[:, :, :, 0:1], 0.0))
        c.pe.wait(w2_in, *projected)
        c.act.wait(*projected)
        for g in range(4):
            for h in range(2):
                i = self.take()
                done = c.pe.mark(nc.tensor.matmul(c.bank(i, HT), w2[:, P * g:P * (g + 1)],
                                                  z[:, HT * h:HT * (h + 1)], start=True, stop=True))
                c.act.wait(done)
                biased = c.act.mark(nc.scalar.activation(
                    logit[:, g, HT * h:HT * (h + 1)], c.bank(i, HT), ACT.Identity,
                    bias=self.col("gate_b", g), scale=1.0))
                self.free(i, biased)
        c.dve.wait(biased)
        s = c.dve.mark(nc.vector.scalar_tensor_tensor(soft[:, :, :], logit[:, :, :], -1.0, logit[:, :, :],
                                                      ALU.mult, ALU.min))
        c.act.wait(s)
        s = c.act.mark(nc.scalar.activation(soft[:, :, :], soft[:, :, :], ACT.Exp))
        c.act.wait(s)
        s = c.act.mark(nc.scalar.activation(soft[:, :, :], soft[:, :, :], ACT.Ln, bias=self.ones[:, 0:1],
                                            scale=1.0))
        silu_done = c.act.mark(nc.scalar.activation(gr, gr, ACT.Silu))
        for g in range(4):
            c.dve.wait(s)
            x = c.dve.mark(nc.vector.scalar_tensor_tensor(soft[:, g, :], logit[:, g, :], 0.0, soft[:, g, :],
                                                          ALU.min, ALU.subtract))
            c.dve.wait(x, zero)
            c.dve.mark(nc.vector.tensor_tensor_scan(total[:, g // 2, g % 2, 1:T + 1], ones_row[:, :],
                                                    soft[:, g, :], 0.0, ALU.mult, ALU.add))
        for lane in (c.pe, c.act, c.dve, c.pool):
            lane.wait(c.dve.now, c.act.now)
        gate.close()

        levels = [4 * JT, 2 * JT, JT, LEAF]
        both = [[mem(f"half_{s}_{r}", [P, 2, T]) for r in range(2)] for s in levels]
        leaf = [[mem(f"leaf_{r}_{w}", [P, 2, T]) for w in range(2)] for r in range(2)]
        step = mem("decay_step", [P, 2, T])
        inv_tau = 1.0 / GLA_TAU
        step_free = {}
        ready_at = {}

        def scale(unit):
            a, level, r = unit // 10, unit % 10 // 2, unit % 2
            run = total[:, r, a, 1:T + 1] if r == 0 else total[:, r, a, 0:T]
            q, k = gqk[:, a, :], gqk[:, 2 + a, :]
            s = LEAF if level == 4 else levels[level]
            n = LEAF if level == 4 else 2 * s
            mid = LEAF // 2 if level == 4 else s - 1 + r
            slot = unit % 2
            exponent = step[:, slot, :]
            rv = run.rearrange("p (b n) -> p b n", n=n)
            c.pool.wait(step_free.get(slot))
            x = c.pool.mark(nc.gpsimd.tensor_tensor(
                exponent.rearrange("p (b n) -> p b n", n=n), rv,
                rv[:, :, mid:mid + 1].to_broadcast([P, T // n, n]), ALU.subtract))
            c.act.wait(x)
            if level == 4:
                sign = inv_tau if r == 0 else -inv_tau
                for w, src in ((0, q), (1, k)):
                    dst = leaf[r][w][:, a, :]
                    e = c.act.mark(nc.scalar.activation(dst, exponent, ACT.Exp, scale=sign * (1 - 2 * w)))
                    c.dve.wait(e)
                    ready = c.dve.mark(nc.vector.tensor_tensor(dst, dst, src, ALU.mult))
            else:
                for side, src in ((0, k if r == 0 else q), (1, q if r == 0 else k)):
                    half = slice(side * s, (side + 1) * s)
                    dst, ev, sv = [v.rearrange("p (b n) -> p b n", n=n)[:, :, half]
                                   for v in (both[level][r][:, a, :], exponent, src)]
                    e = c.act.mark(nc.scalar.activation(dst, ev, ACT.Exp, scale=inv_tau * (2 * side - 1)))
                    c.dve.wait(e)
                    ready = c.dve.mark(nc.vector.tensor_tensor(dst, dst, sv, ALU.mult))
            step_free[slot] = e
            ready_at[unit] = ready

        groups = []
        for r in range(2):
            a = both[0][r]
            for g in range(2):
                groups.append(([(4 * r + 2 * g + x, HT * (1 - r), HT, a, a) for x in range(2)], None))
        for r in range(2):
            a = both[1][r]
            groups.append(([(4 * b + 2 * r + x, 4 * JT * b + 2 * JT * (1 - r), 2 * JT, a, a)
                            for b in range(2) for x in range(2)], None))
        groups.append(([(2 * b + r, JT * (2 * b + 1 - r), JT, both[2][r], both[2][r])
                        for r in range(2) for b in range(4)], None))
        for r in range(2):
            groups.append(([(j, JT * j, JT, both[3][r], both[3][r]) for j in range(NJ)], r))
        for r in range(2):
            groups.append(([(j, JT * j, JT, leaf[r][1], leaf[r][0]) for j in range(NJ)], 2 + r))

        needs = [0, 0, 1, 1, 2, 3, 5, 6, 7, 8, 9]
        weight = [self.h[0:JT, 4:8, :].rearrange("p a n -> p (a n)")[:, T * i:T * (i + 1)] for i in range(3)]
        o = total[:, 0, 0, 0:T]
        norm = total[:, 1, 0, 0:SEQ]
        c.pe.wait(masks_in)
        c.dve.wait(masks_in)
        self.start_norms()
        c.act.wait(mixed_free)
        c.dve.wait(mixed_free, silu_done)
        jobs = [(head, x) for head in range(GLA_HEADS) for x in range(len(groups))]
        weight_free, weight_ready = {}, {}
        started = [False, False]

        def scores(n):
            head, x = jobs[n]
            pieces, mask = groups[x]
            rows = slice(64 * (head % 2), 64 * (head % 2) + 64)
            a = head // 2
            j = self.take_pair(3)
            c.pe.wait(ready_at[10 * a + needs[x]])
            for m, (jt, i0, ni, ka, qa) in enumerate(pieces):
                ins = nc.tensor.matmul(
                    self.c.psum[0:JT, j + ni * m // HT, ni * m % HT:ni * m % HT + ni],
                    ka[rows, a, JT * jt:JT * (jt + 1)], qa[rows, a, i0:i0 + ni],
                    start=True, stop=True, skip_group_check=True)
            done = c.pe.mark(ins)
            dst = weight[n % 3].rearrange("p (b n) -> p b n", n=HT)
            lane = c.dve if mask is not None or x % 2 == 0 else c.act
            lane.wait(done, weight_free.get(n - 3))
            if mask is not None:
                for half in range(2):
                    ready = c.dve.mark(nc.vector.tensor_tensor(
                        dst[:, half, :].rearrange("p (a n) -> p a n", n=JT),
                        self.c.psum[0:JT, j + half, 0:HT].rearrange("p (a n) -> p a n", n=JT),
                        masks[:, mask:mask + 1, :].to_broadcast([JT, HT // JT, JT]), ALU.mult))
            elif lane is c.act:
                ready = c.act.mark(nc.scalar.activation(dst, self.pair(j, JT), ACT.Copy))
            else:
                ready = c.dve.mark(nc.vector.tensor_copy(dst, self.pair(j, JT)))
            self.free(j, ready)
            self.free(j + 1, ready)
            weight_ready[n] = ready

        def applying(n):
            head, x = jobs[n]
            pieces, _ = groups[x]
            if x == 0:
                c.pe.wait(c.bank_free[6], c.bank_free[7])
                started[0] = started[1] = False
            c.pe.wait(weight_ready[n])
            for m, (jt, i0, ni, _, _) in enumerate(pieces):
                half = i0 // HT
                ins = nc.tensor.matmul(
                    self.c.psum[:, 6 + half, i0 - HT * half:i0 - HT * half + ni],
                    gv[:, jt, P * head:P * (head + 1)], weight[n % 3][:, ni * m:ni * (m + 1)],
                    start=not started[half], stop=True, skip_group_check=True)
                started[half] = True
            weight_free[n] = c.pe.mark(ins)
            if x == len(groups) - 1:
                self.finish_norm()
                c.act.wait(weight_free[n], self.head_read)
                got = c.act.mark(nc.scalar.activation(o.rearrange("p (b n) -> p b n", n=HT),
                                                      self.pair(6), ACT.Copy))
                self.free(6, got)
                self.free(7, got)
                self.norming = self.head_norm(norm, o[:, META:T], DA_HEADS + head, self.col("gla_norm"),
                                              [got], (0, 1, 2, 3), gr[:, head, :])

        unit = 0
        for n in range(len(jobs) + 2):
            while unit < min(20, n + 4):
                scale(unit)
                unit += 1
            if n < len(jobs):
                scores(n)
            self.advance()
            if n >= 2:
                applying(n - 2)
            if n % 5 == 4:
                self.modulation_block((0, 2, 4))
        self.finish_norm()
        while self.mod_pending is not None:
            self.modulation_block((0, 2, 4))
        self.modulation_columns()
        mem.close()

    def rotate(self, x, n0):
        c, nc = self.c, self.nc
        cos, sin, swap, turned, constants = self.rope
        n_all = T - n0
        ranges = [(0, SEQ)] if n_all == SEQ else [(0, HT), (HT, T)]
        c.pe.wait(c.act.now, c.dve.now, *constants)
        c.dve.wait(c.act.now, *constants)
        for h in range(DA_HEADS):
            for lo, hi in ranges:
                i = self.take()
                done = c.pe.mark(nc.tensor.matmul(c.bank(i, hi - lo), swap, x[:, h, lo:hi],
                                                  start=True, stop=True))
                c.dve.wait(done, c.dve.now)
                s = c.dve.mark(nc.vector.tensor_tensor(turned[:, 0:hi - lo], c.bank(i, hi - lo),
                                                       sin[:, n0 + lo:n0 + hi], ALU.mult))
                self.free(i, s)
                s = c.dve.mark(nc.vector.tensor_tensor(x[:, h, lo:hi], x[:, h, lo:hi],
                                                       cos[:, n0 + lo:n0 + hi], ALU.mult))
                c.dve.wait(s)
                c.dve.mark(nc.vector.tensor_tensor(x[:, h, lo:hi], x[:, h, lo:hi], turned[:, 0:hi - lo], ALU.add))

    def attention(self, dq, dk, dv, projected):
        c, nc, d = self.c, self.nc, self.d
        mem = Memory(nc)
        lam4, lam_in = self.const(mem, "lambdas", [DA_DIM, 4])
        lam = mem("lambda", [P, 4])

        c.dve.wait(lam_in)
        s = c.dve.mark(nc.vector.tensor_tensor(lam4[:, 0:2], lam4[:, 0:2], lam4[:, 2:4], ALU.mult))
        c.pe.wait(s)
        i = self.take()
        s = c.pe.mark(nc.tensor.matmul(c.bank(i, 2), self.ones[0:DA_DIM, :], lam4[:, 0:2], start=True, stop=True))
        c.act.wait(s)
        s = c.act.mark(nc.scalar.activation(lam[:, 0:2], c.bank(i, 2), ACT.Exp))
        self.free(i, s)
        c.dve.wait(s)
        s = c.dve.mark(nc.vector.tensor_tensor(lam[:, 2:3], lam[:, 1:2], lam[:, 0:1], ALU.subtract))
        c.dve.wait(s)
        c.dve.mark(nc.vector.tensor_scalar(lam[:, 3:4], lam[:, 2:3], -LAM_INIT, None, ALU.add))

        e = mem("exp_scores", [P, 2, 2, T])
        stat = mem("softmax_stats", [P, 2, 8])
        mix = mem("mixed_scores", [P, 2, T])
        mix_t = mem("mixed_scores_t", [P, 2, 5, P])
        o = mem("da_out", [P, SEQ])
        norm = mem("da_square", [P, SEQ])[:, :]
        scale = DA_DIM ** -0.5
        steps = [(h, qt) for h in range(DA_HEADS) for qt in range(SEQ // P)]
        key_tiles = [(t, min(P, T - P * t)) for t in range(5)]
        c.pe.wait(*projected)
        mixed_at, turned_at, applied_at, exped_at, copied_at = {}, {}, {}, {}, {}
        self.start_norms()
        self.modulation_start()
        self.ring = 0

        def scores(n):
            h, qt = steps[n]
            v = n % 2
            for m in range(2):
                rows = slice(64 * m, 64 * m + 64)
                j = 2 * m
                c.pe.wait(c.bank_free[j], c.bank_free[j + 1])
                for g in range(2):
                    ins = nc.tensor.matmul(c.bank(j + g, HT), dq[rows, h, P * qt:P * (qt + 1)],
                                           dk[rows, h, HT * g:HT * (g + 1)], start=True, stop=True)
                done = c.pe.mark(ins)
                st = stat[:, v, :]
                c.dve.wait(done, mixed_at.get(n - 2))
                s = c.dve.mark(nc.vector.tensor_reduce(st[:, m:m + 1], self.pair(j), AX.XY, ALU.max))
                c.dve.wait(s)
                s = c.dve.mark(nc.vector.tensor_scalar(st[:, 2 + m:3 + m], st[:, m:m + 1], -scale, None, ALU.mult))
                c.act.wait(s, mixed_at.get(n - 2))
                s = c.act.mark(nc.scalar.activation(
                    e[:, v, m, :].rearrange("p (b n) -> p b n", n=HT), self.pair(j), ACT.Exp,
                    bias=st[:, 2 + m:3 + m], scale=scale, accum_out=st[:, 4 + m:5 + m]))
                self.free(j, s)
                self.free(j + 1, s)
            exped_at[n] = s

        def mixing(n):
            v = n % 2
            st = stat[:, v, :]
            c.dve.wait(exped_at[n], turned_at.get(n - 2))
            s = c.dve.mark(nc.vector.reciprocal(st[:, 6:8], st[:, 4:6]))
            c.dve.wait(s)
            s = c.dve.mark(nc.vector.tensor_scalar(st[:, 7:8], st[:, 7:8], lam[:, 3:4], None, ALU.mult))
            s = c.dve.mark(nc.vector.tensor_scalar(mix[:, v, :], e[:, v, 0, :], st[:, 6:7], None, ALU.mult))
            c.dve.wait(s)
            mixed_at[n] = c.dve.mark(nc.vector.scalar_tensor_tensor(
                mix[:, v, :], e[:, v, 1, :], st[:, 7:8], mix[:, v, :], ALU.mult, ALU.add))

        def turning(n):
            v = n % 2
            c.pe.wait(mixed_at[n], c.bank_free[4], c.bank_free[5])
            for t, m in key_tiles:
                bank, off = (4, P * t) if t < 4 else (5, 0)
                ins = nc.tensor.transpose(self.c.psum[0:m, bank, off:off + P], mix[:, v, P * t:P * t + m],
                                          self.ident[:, :])
            turned_at[n] = c.pe.mark(ins)
            c.act.wait(turned_at[n], applied_at.get(n - 2))
            s = c.act.mark(nc.scalar.activation(mix_t[:, v, 0:4, :].rearrange("p a b -> p (a b)"),
                                                c.bank(4), ACT.Copy))
            self.free(4, s)
            s = c.act.mark(nc.scalar.activation(mix_t[0:META, v, 4, :], c.bank(5, P, META), ACT.Copy))
            self.free(5, s)
            copied_at[n] = s

        def applying(n):
            h, qt = steps[n]
            v = n % 2
            c.pe.wait(copied_at[n])
            if qt == 0:
                c.pe.wait(c.bank_free[6])
            for t, m in key_tiles:
                ins = nc.tensor.matmul(self.c.psum[:, 6, P * qt:P * (qt + 1)], dv[0:m, t, P * h:P * (h + 1)],
                                       mix_t[0:m, v, t, :], start=t == 0, stop=t == 4)
            applied_at[n] = c.pe.mark(ins)
            if qt == SEQ // P - 1:
                self.finish_norm()
                c.act.wait(applied_at[n], self.head_read)
                got = c.act.mark(nc.scalar.activation(o[:, :], c.bank(6), ACT.Copy))
                self.free(6, got)
                self.norming = self.head_norm(norm, o[:, :], h, self.gain_da, [got], (7,))

        gain = mem("da_gain", [P, 1])
        c.dve.wait(c.dve.now)
        s = c.dve.mark(nc.vector.tensor_scalar(gain[:, :], self.col("da_norm"), 1.0 - LAM_INIT, None, ALU.mult))
        self.gain_da = gain[:, 0:1]
        for n in range(len(steps) + 3):
            if n < len(steps):
                scores(n)
            self.advance()
            if 0 <= n - 1 < len(steps):
                mixing(n - 1)
            if 0 <= n - 2 < len(steps):
                turning(n - 2)
            self.advance()
            if n >= 3:
                applying(n - 3)
            if n % 4 == 3:
                self.modulation_block((7,))
        self.finish_norm()
        c.fence()
        mem.close()


    def experts(self):
        c, nc, d = self.c, self.nc, self.d
        parts = (self.x_high, self.x_low)
        scratch = Memory(nc)
        self.norm_buffers(scratch, "norm2", SEQ)
        xn = self.rms(self.h, SEQ, lambda t: self.col("ln2", t), self.added, parts)
        self.spill = self.value
        self.spilled, self.n_spilled = [], 0
        self.xn = xn
        self.route(parts, xn)
        c.fence()
        for lane in (c.act, c.pool, c.dve):
            lane.wait(*self.spilled[-4:])
        scratch.close()

        mem = Memory(nc)
        acc = mem("expert_sum", [P, KT, SEQ])
        gates = mem("gates", [P, 2, SEQ // TC, EG, TC])
        act = mem("expert_act", [P, 2, EG, SEQ])
        hid_high = mem("hidden_high", [P, 2, EG, SEQ], BF16)
        hid_low = mem("hidden_low", [P, 2, EG, SEQ], BF16)
        n_groups = NK // EG
        loaded, gated, hidden, hidden_free = {}, {}, {}, {}

        def load_group(n):
            g = GROUPS[n]
            signals = [c.dma(c.sp, f"gates_in_{n % 2}", gates[:, n % 2, :, :, :],
                             self.gate_dram[:, :, EG * g:EG * (g + 1), :].rearrange("c p b n -> p c b n"),
                             [self.gates_written, gated.get(n - 2)])]
            if g < AHEAD:
                signals.append(c.dma(c.sp, f"act_in_{n % 2}", act[:, n % 2, :, :],
                                     self.act_dram[EG * g:EG * (g + 1)].rearrange("b p n -> p b n"),
                                     [self.spilled[EG * g:EG * (g + 1)]]))
            loaded[n] = signals

        def gate_tile(n, b, after):
            slot = n % 2
            c.dve.wait(after, *loaded[n])
            a = act[:, slot, b, :]
            v = a.rearrange("p (c n) -> p c n", n=TC)
            w = c.dve.mark(nc.vector.tensor_tensor(v, v, gates[:, slot, :, b, :], ALU.mult))
            gated[n] = hidden[n] = split_value(c, a, hid_high[:, slot, b, :], hid_low[:, slot, b, :],
                                               [w, hidden_free.get(n - 2)])

        def hidden_group(n):
            if GROUPS[n] < AHEAD:
                for b in range(EG):
                    gate_tile(n, b, None)
                return
            block = self.w.next("u")
            for b in range(EG):
                def evacuate(psum, done, b=b):
                    c.act.wait(done, gated.get(n - 2))
                    s = c.act.mark(nc.scalar.activation(act[:, n % 2, b, :], psum, ACT.Gelu))
                    computed.append((b, s))
                    return s
                computed = []
                done = self.linear(block, slice(P * b, P * (b + 1)), parts, slice(0, SEQ), SEQ, P,
                                   xn, evacuate)
                if n > 0:
                    gate_tile(n, *computed[0])
                else:
                    first_tiles.extend(computed)
            self.w.release(done)
            for b, s in first_tiles:
                gate_tile(n, b, s)
            first_tiles.clear()

        first_tiles = []

        def down(n):
            block = self.w.next("v")
            c.pe.wait(block[2], hidden[n])
            for t in range(KT):
                i = self.take()
                for b in range(EG):
                    ins = three_products(c, c.bank(i), (block[0][:, b, P * t:P * (t + 1)],
                                                        block[1][:, b, P * t:P * (t + 1)]),
                                         (hid_high[:, n % 2, b, :], hid_low[:, n % 2, b, :]),
                                         b == 0, b == EG - 1)
                done = c.pe.mark(ins)
                c.dve.wait(done)
                if n == 0:
                    s = c.dve.mark(nc.vector.tensor_copy(acc[:, t, :], c.bank(i)))
                else:
                    c.dve.wait(self.acc_at[t])
                    s = c.dve.mark(nc.vector.tensor_tensor(acc[:, t, :], c.bank(i), acc[:, t, :], ALU.add))
                self.acc_at[t] = s
                self.free(i, s)
                if n == n_groups - 1:
                    c.dve.wait(s)
                    self.added.append(c.dve.mark(nc.vector.tensor_tensor(
                        self.h[:, t, :], self.h[:, t, :], acc[:, t, :], ALU.add)))
            hidden_free[n] = done
            self.w.release(done)

        self.acc_at = [None] * KT
        self.added = []
        load_group(0)
        load_group(1)
        hidden_group(0)
        for n in range(n_groups):
            if n + 1 < n_groups:
                hidden_group(n + 1)
            if n + 2 < n_groups:
                load_group(n + 2)
            down(n)
        c.fence()
        mem.close()

    def fill(self, n):
        c, nc = self.c, self.nc
        for tile in range(self.n_spilled, min(self.n_spilled + n, AHEAD * EG)):
            b, slot = tile % EG, tile % 4
            if b == 0:
                self.fill_block = self.w.next("u")

            def evacuate(psum, done):
                c.act.wait(done, self.spilled[tile - 4] if tile >= 4 else None)
                s = c.act.mark(nc.scalar.activation(self.spill[:, slot, :], psum, ACT.Gelu))
                self.spilled.append(c.dma(c.sp, f"act_out_{slot}", self.act_dram[tile],
                                          self.spill[:, slot, :], [s]))
                return s
            done = self.linear(self.fill_block, slice(P * b, P * (b + 1)), (self.x_high, self.x_low),
                               slice(0, SEQ), SEQ, P, self.xn, evacuate)
            if b == EG - 1:
                self.w.release(done)
            self.n_spilled += 1

    def route(self, parts, xn):
        c, nc, d = self.c, self.nc, self.d
        mem = Memory(nc)
        iota16, iota16_in = self.const(mem, "iota_picks", [P, TOPK])
        pick_b = mem("picks_t_bf16", [P, 4, SEQ], BF16)

        top = Memory(nc)
        keys, keys_in = self.const(top, "sub_keys", [P, 2 * PH, NK])
        score = top("scores", [P, SEQ // P, 2 * PH, NK])
        query = top("queries", [P, 2, SEQ])
        query_free = [None, None]
        c.pe.wait(keys_in)
        for g in range(4):
            block = self.w.next("peer_q")
            for f in range(4):
                hp = 4 * g + f
                got = {}

                def keep(psum, done, hp=hp):
                    c.act.wait(done, query_free[hp % 2])
                    got[0] = c.act.mark(nc.scalar.activation(query[:, hp % 2, :], psum, ACT.Copy))
                    return got[0]
                done = self.linear(block, slice(P * f, P * (f + 1)), parts, slice(0, SEQ), SEQ, P,
                                   xn, keep)
                i = self.take()
                c.pe.wait(got[0])
                for t in range(SEQ // P):
                    ins = nc.tensor.matmul(self.c.psum[:, i, NK * t:NK * (t + 1)],
                                           query[:, hp % 2, P * t:P * (t + 1)], keys[:, hp, :],
                                           start=True, stop=True)
                query_free[hp % 2] = c.pe.mark(ins)
                c.act.wait(query_free[hp % 2])
                s = c.act.mark(nc.scalar.activation(score[:, :, hp, :],
                                                    c.bank(i).rearrange("p (t k) -> p t k", k=NK), ACT.Copy))
                self.free(i, s)
            self.w.release(query_free[hp % 2])
        picks_turned = scored = c.act.now

        best = top("best_side", [P, 2 * PH, TOPK])
        best_i = top("best_side_index", [P, 2 * PH, TOPK], U32)
        best_f = top("best_side_index_f", [P, 2 * PH, TOPK])
        cand = top("pair_scores", [P, PH, TOPK, TOPK])
        pair = top("best_pair", [P, PH, TOPK])
        shifted = top("best_pair_shifted", [P, PH, TOPK])
        pair_i = top("best_pair_index", [P, PH, TOPK], U32)
        rank_i = top("best_rank_index", [P, 2, PH, TOPK], U32)
        rank = top("best_rank", [P, 2, PH, TOPK])
        hot = cand
        pick = top("picks", [P, 3, PICKS])
        tot = top("gate_sum", [P, 2, PH])
        LOW = -3.0e38
        c.dve.wait(scored, iota16_in)

        def top16(values, out, index):
            s = c.dve.mark(nc.vector.max(out[:, 0:8], values))
            c.dve.wait(s)
            c.dve.mark(nc.vector.max_index(index[:, 0:8], out[:, 0:8], values))
            c.dve.wait(c.dve.now)
            s = c.dve.mark(nc.vector.match_replace(values, out[:, 0:8], values, LOW))
            c.dve.wait(s)
            s = c.dve.mark(nc.vector.max(out[:, 8:16], values))
            c.dve.wait(s)
            c.dve.mark(nc.vector.max_index(index[:, 8:16], out[:, 8:16], values))

        self.fill(2 * EG)
        for t in range(SEQ // P):
            c.dve.wait(c.dve.now, picks_turned)
            for hp in range(2 * PH):
                top16(score[:, t, hp, :], best[:, hp, :], best_i[:, hp, :])
            c.dve.wait(c.dve.now)
            c.dve.mark(nc.vector.tensor_copy(best_f[:, :, :], best_i[:, :, :]))
            sides = best[:, :, :].rearrange("p (h s) k -> p h s k", s=2)
            for h in range(PH):
                c.dve.mark(nc.vector.tensor_tensor(
                    cand[:, h, :, :], sides[:, h, 0, :].unsqueeze(2).to_broadcast([P, TOPK, TOPK]),
                    sides[:, h, 1, :].unsqueeze(1).to_broadcast([P, TOPK, TOPK]), ALU.add))
            c.dve.wait(c.dve.now)
            for h in range(PH):
                top16(cand[:, h, :, :].rearrange("p a b -> p (a b)"), pair[:, h, :], pair_i[:, h, :])
            c.dve.wait(c.dve.now)
            s = c.dve.mark(nc.vector.tensor_tensor(shifted[:, :, :], pair[:, :, :],
                                                   pair[:, :, 0:1].to_broadcast([P, PH, TOPK]), ALU.subtract))
            c.dve.mark(nc.vector.tensor_scalar(rank_i[:, 0, :, :], pair_i[:, :, :], 4, None,
                                               ALU.logical_shift_right))
            c.dve.mark(nc.vector.tensor_scalar(rank_i[:, 1, :, :], pair_i[:, :, :], 15, None, ALU.bitwise_and))
            c.act.wait(s)
            gate = pick[:, 2, :].rearrange("p (h k) -> p h k", k=TOPK)
            e = c.act.mark(nc.scalar.activation(gate, shifted[:, :, :], ACT.Exp))
            self.fill(EG)
            c.dve.wait(c.dve.now, e)
            c.dve.mark(nc.vector.tensor_reduce(tot[:, 0, :], gate, AX.X, ALU.add))
            c.dve.mark(nc.vector.tensor_copy(rank[:, :, :, :], rank_i[:, :, :, :]))
            c.dve.wait(c.dve.now)
            c.dve.mark(nc.vector.reciprocal(tot[:, 1, :], tot[:, 0, :]))
            c.dve.wait(c.dve.now)
            c.dve.mark(nc.vector.tensor_tensor(gate, gate, tot[:, 1, :].unsqueeze(2).to_broadcast([P, PH, TOPK]),
                                               ALU.mult))
            bf = best_f[:, :, :].rearrange("p (h s) k -> p h s k", s=2)
            for side in range(2):
                for h in range(PH):
                    c.dve.mark(nc.vector.tensor_tensor(
                        hot[:, h, :, :], rank[:, side, h, :].unsqueeze(2).to_broadcast([P, TOPK, TOPK]),
                        iota16[:, :].unsqueeze(1).to_broadcast([P, TOPK, TOPK]), ALU.is_equal))
                c.dve.wait(c.dve.now)
                for h in range(PH):
                    c.dve.mark(nc.vector.tensor_tensor(
                        hot[:, h, :, :], hot[:, h, :, :],
                        bf[:, h, side, :].unsqueeze(1).to_broadcast([P, TOPK, TOPK]), ALU.mult))
                c.dve.wait(c.dve.now)
                s = c.dve.mark(nc.vector.tensor_reduce(
                    pick[:, side, :].rearrange("p (h k) -> p h k", k=TOPK), hot[:, :, :, :], AX.X, ALU.add))
                c.dve.wait(s)
            i = self.take()
            c.pe.wait(c.dve.now)
            for x in range(3):
                ins = nc.tensor.transpose(self.c.psum[:, i, P * x:P * (x + 1)], pick[:, x, :], self.ident[:, :])
            done = c.pe.mark(ins)
            c.act.wait(done)
            picks_turned = s = c.act.mark(nc.scalar.activation(pick_b[:, 0:3, P * t:P * (t + 1)],
                                                c.bank(i, 3 * P).rearrange("p (x n) -> p x n", n=P), ACT.Copy))
            c.dve.wait(s)
            s = c.dve.mark(nc.vector.tensor_tensor(pick_b[:, 3, P * t:P * (t + 1)],
                                                   self.c.psum[:, i, 2 * P:3 * P],
                                                   pick_b[:, 2, P * t:P * (t + 1)], ALU.subtract))
            self.free(i, s)
            if t < SEQ // P - 1:
                self.fill(2 * EG)
        c.fence()
        top.close()

        hot_mem = Memory(nc)
        iota32, iota_in = self.const(hot_mem, "iota_keys", [P, NK])
        iota = hot_mem("iota_bf16", [P, NK, OC], BF16)
        left = hot_mem("one_hot_a", [P, 2, NK, OC], BF16)
        right = hot_mem("one_hot_b", [P, 2, NK, OC], BF16)
        gated = hot_mem("gated_one_hot_b", [P, 2, 2, NK, OC], BF16)
        mats = hot_mem("gate_matrices", [P, 2, NK, TC])
        hot_free, mats_out = {}, {}
        c.dve.wait(c.dve.now, iota_in)
        s = c.dve.mark(nc.vector.tensor_copy(iota[:, :, :], iota32[:, :].unsqueeze(2).to_broadcast([P, NK, OC])))
        c.dve.wait(s)
        for n in range(SEQ // OC):
            v = n % 2
            tok = slice(OC * n, OC * (n + 1))

            def spread(x):
                return pick_b[:, x, tok].unsqueeze(1).to_broadcast([P, NK, OC])
            c.dve.wait(hot_free.get(n - 2))
            c.dve.mark(nc.vector.tensor_tensor(left[:, v, :, :], iota[:, :, :], spread(0), ALU.is_equal))
            s = c.dve.mark(nc.vector.tensor_tensor(right[:, v, :, :], iota[:, :, :], spread(1), ALU.is_equal))
            c.dve.wait(s)
            c.dve.mark(nc.vector.tensor_tensor(gated[:, v, 0, :, :], right[:, v, :, :], spread(2), ALU.mult))
            ready = c.dve.mark(nc.vector.tensor_tensor(gated[:, v, 1, :, :], right[:, v, :, :], spread(3), ALU.mult))
            c.pe.wait(ready)
            chunk, half = n // (TC // OC), n % (TC // OC)
            for q in range(OC // 4):
                i = self.take()
                for x in range(4):
                    tk = 4 * q + x
                    for part in range(2):
                        ins = nc.tensor.matmul(self.c.psum[:, i, NK * x:NK * (x + 1)], left[:, v, :, tk],
                                               gated[:, v, part, :, tk], start=part == 0, stop=part == 1)
                done = c.pe.mark(ins)
                at = OC * half + 4 * q
                lane = c.act
                lane.wait(done, mats_out.get(chunk - 2))
                dst = mats[:, chunk % 2, :, at:at + 4].rearrange("p b x -> p x b")
                src = c.bank(i).rearrange("p (x b) -> p x b", b=NK)
                s = lane.mark(nc.scalar.activation(dst, src, ACT.Copy))
                self.free(i, s)
            hot_free[n] = done
            if n % 4 != 2:
                self.fill(1)
            if half == TC // OC - 1:
                mats_out[chunk] = c.dma(c.sp, f"gates_out_{chunk % 2}", self.gate_dram[chunk],
                                        mats[:, chunk % 2, :, :], [s])
        self.gates_written = [mats_out[chunk], mats_out[chunk - 1]]
        c.fence()
        for lane in (c.pe, c.act, c.dve, c.pool):
            lane.wait(*self.gates_written)
        hot_mem.close()
        mem.close()
        self.fill(AHEAD * EG)


    def second(self):
        c, nc, d = self.c, self.nc, self.d
        parts = (self.x_high, self.x_low)
        outer = Memory(nc)
        self.norm_buffers(outer, "norm_2", SEQ)
        residual = self.rms(self.h, SEQ, lambda t: self.col("final1", t), self.added, None,
                            fp32_out=self.h)

        mod, gain1, gain2 = self.mod, self.gain1, self.gain2

        ctx_high = outer("ctx_high", [P, KT, CTX], BF16)
        ctx_low = outer("ctx_low", [P, KT, CTX], BF16)
        heads = Memory(nc)
        kt = heads("na_k", [P, 4, KEYS2])
        vt = heads("na_v", [P, KEYS2 // P, 512])
        qt = heads("na_q", [P, 4, SEQ])
        ctx = qt[:, :, :].rearrange("p f (a n) -> p (f a) n", n=CTX)
        landed = self.load("in_ctx", ctx, d["ctx"])
        c.act.wait(self.modulated)
        xn = self.rms(self.h, SEQ, lambda t: gain1[:, t, 0:1], residual, parts,
                      shift=lambda t: mod[:, t, 0:1])
        fin = heads("fourier_x", [P, 2, SEQ])
        conv = heads("conv_padded", [P, 2, SEQ + 2 * (TAPS // 2)])
        gin = heads("conv_gate", [P, 2, SEQ])
        wf, wf_in = self.const(heads, "w_fourier", [P, 2, FFT_CH])
        pw, pw_in = self.const(heads, "conv_pw_w", [P, 2, 256])
        dft = Memory(nc)
        chan = self.mod_rows[:, 0:2 * P].rearrange("p (a b) -> p a b", a=2)
        chan_in = self.load("in_dft_channels", chan, d["dft_channels"])
        tok, tok_in = self.const(dft, "dft_tokens", [P, 2, 4, SEQ])
        transformed = self.value[:, 0:2, :]

        def keep(dst, func=ACT.Copy):
            def evacuate(psum, done):
                c.act.wait(done)
                return c.act.mark(nc.scalar.activation(dst, psum, func))
            return evacuate

        def columns(name, dsts):
            block = self.w.next(name)
            for f, dst in enumerate(dsts):
                done = self.linear(block, slice(P * f, P * (f + 1)), parts, slice(0, SEQ), SEQ, P, xn, keep(*dst))
            self.w.release(done)

        half = TAPS // 2
        zeroed = c.dve.mark(nc.vector.memset(conv[:, :, :], 0.0))
        c.act.wait(zeroed)
        columns("conv_in", [(conv[:, g, half:half + SEQ],) for g in range(2)]
                + [(gin[:, g, :], ACT.Sigmoid) for g in range(2)])
        ctx_n = self.rms(ctx, CTX, lambda t: gain1[:, t, 1:2], [landed],
                         (ctx_high, ctx_low), shift=lambda t: mod[:, t, 1:2])
        taps = self.convolution(conv, gin)
        next(taps)
        columns("fourier_in", [(fin[:, f, :],) for f in range(2)])
        c.pe.wait(c.act.now, chan_in, tok_in)
        c.act.wait(*ctx_n)
        self.fourier(fin, chan, tok, vt[:, 0:4, :], transformed)

        block = self.w.next("k2")
        for f in range(4):
            cols = slice(P * f, P * (f + 1))
            self.linear(block, cols, parts, slice(0, SEQ), SEQ, P, xn, keep(kt[:, f, 0:SEQ]))
            done = self.linear(block, cols, (ctx_high, ctx_low), slice(0, CTX), CTX, P, ctx_n,
                               keep(kt[:, f, SEQ:KEYS2]))
        self.w.release(done)
        block = self.w.next("v2")
        c.act.wait(c.pe.now)
        for j in range(KEYS2 // P):
            src, at = (parts, P * j) if j < 4 else ((ctx_high, ctx_low), P * (j - 4))
            i = self.take()
            c.pe.wait(block[2])
            done = c.pe.mark(self.token_product(c.bank(i), block, slice(0, 512), src, slice(at, at + P)))
            self.free(i, keep(vt[:, j, :])(c.bank(i), done))
            if j in (1, 3, 5):
                next(taps)
        self.w.release(done)
        columns("q2", [(qt[:, f, :],) for f in range(4)])
        c.fence()
        dft.close()
        c.pe.wait(wf_in, pw_in)
        normed = self.square[:, 0:2, :]

        def small_outs():
            self.small_out(wf, transformed, 0, None)
            return self.small_out(pw, normed, 2, "conv_pw_b")
        self.neighbourhood(qt, kt, vt, small_outs)
        c.fence()
        heads.close()

        mixed = c.dve.now
        self.added = []
        for g in range(2):
            block = self.w.next("w_out_2")
            for f in range(4):
                t = 4 * g + f

                def add(psum, done, t=t):
                    c.dve.wait(done)
                    self.added.append(c.dve.mark(nc.vector.scalar_tensor_tensor(
                        self.h[:, t, :], psum, mod[:, 2 * KT + t, 0:1], self.h[:, t, :], ALU.mult, ALU.add)))
                    return self.added[-1]
                done = self.linear(block, slice(P * f, P * (f + 1)), parts, slice(0, SEQ), SEQ, P,
                                   [mixed], add)
            self.w.release(done)
        xn = self.rms(self.h, SEQ, lambda t: gain2[:, t:t + 1], self.added, parts,
                      shift=lambda t: mod[:, 3 * KT + t, 0:1])

        mem = Memory(nc)
        hid_high = mem("mlp_high", [P, 4 * KT, SEQ], BF16)
        hid_low = mem("mlp_low", [P, 4 * KT, SEQ], BF16)
        relu = self.square[:, 0:2, :]
        relu_free = [None, None]
        for g in range(8):
            block = self.w.next("mlp_1")
            for f in range(4):
                t = 4 * g + f

                def evacuate(psum, done, t=t):
                    r = relu[:, t % 2, :]
                    c.act.wait(done, relu_free[t % 2])
                    s = c.act.mark(nc.scalar.activation(r, psum, ACT.Relu))
                    c.dve.wait(s)
                    w = c.dve.mark(nc.vector.tensor_tensor(r, r, r, ALU.mult))
                    relu_free[t % 2] = split_value(c, r, hid_high[:, t, :], hid_low[:, t, :], [w])
                    return s
                done = self.linear(block, slice(P * f, P * (f + 1)), parts, slice(0, SEQ), SEQ, P,
                                   xn, evacuate)
            self.w.release(done)
        hidden = c.dve.now
        added = []
        c.pe.wait(hidden, *c.bank_free)
        for g in range(8):
            block = self.w.next("mlp_2")
            c.pe.wait(block[2])
            for t in range(KT):
                for k in range(4):
                    ins = three_products(c, c.bank(t), (block[0][:, k, P * t:P * (t + 1)],
                                                        block[1][:, k, P * t:P * (t + 1)]),
                                         (hid_high[:, 4 * g + k, :], hid_low[:, 4 * g + k, :]),
                                         g == 0 and k == 0, g == 7 and k == 3)
                if g == 7:
                    done = c.pe.mark(ins)
                    c.dve.wait(done)
                    added.append(c.dve.mark(nc.vector.scalar_tensor_tensor(
                        self.h[:, t, :], c.bank(t), mod[:, 5 * KT + t, 0:1], self.h[:, t, :],
                        ALU.mult, ALU.add)))
                    self.free(t, added[-1])
            done = c.pe.mark(ins) if g < 7 else done
            self.w.release(done)

        c.act.wait(hidden)
        done = self.rms(self.h, SEQ, lambda t: self.col("final2", t), added, None, fp32_out=self.h)
        for t in range(0, KT, 2):
            stored = self.c.dma(c.sp, "out_stored", self.out[:, t:t + 2, :], self.h[:, t:t + 2, :], [done[t + 1]])
        c.sp.wait(stored)
        mem.close()
        outer.close()

    def fourier(self, x, chan, tok, place, f):
        c, nc = self.c, self.nc
        y = place.rearrange("p a (b n) -> p (a b) n", n=FFT_CH).rearrange("p (r t) n -> p r t n", r=2)
        for part in range(2):
            for t in range(4):
                i = self.take()
                for g in range(2):
                    ins = nc.tensor.matmul(self.c.psum[:, i, P * g:P * (g + 1)], x[:, g, P * t:P * (t + 1)],
                                           chan[:, part, :], start=True, stop=True)
                done = c.pe.mark(ins)
                c.act.wait(done)
                s = c.act.mark(nc.scalar.activation(y[:, part, t, :], c.bank(i, FFT_CH), ACT.Copy))
                self.free(i, s)
        c.pe.wait(s)
        for g in range(2):
            i = self.take()
            for part in range(2):
                for t in range(4):
                    ins = nc.tensor.matmul(c.bank(i), y[:, part, t, P * g:P * (g + 1)], tok[:, part, t, :],
                                           start=part == 0 and t == 0, stop=part == 1 and t == 3)
            done = c.pe.mark(ins)
            c.act.wait(done)
            s = c.act.mark(nc.scalar.activation(f[:, g, :], c.bank(i), ACT.Copy))
            self.free(i, s)

    def small_out(self, w, x, dst, bias):
        c, nc = self.c, self.nc
        val = self.value[:, 2:4, :]
        c.act.wait(c.dve.now)
        for g in range(2):
            i = self.take()
            for k in range(2):
                ins = nc.tensor.matmul(c.bank(i), w[:, k, P * g:P * (g + 1)], x[:, k, :], start=k == 0, stop=k == 1)
            done = c.pe.mark(ins)
            c.act.wait(done)
            s = c.act.mark(nc.scalar.activation(val[:, g, :], c.bank(i), ACT.Identity, scale=1.0,
                                                bias=self.col(bias, g) if bias else 0.0))
            self.free(i, s)
            done = split_value(c, val[:, g, :], self.x_high[:, dst + g, 0:SEQ],
                               self.x_low[:, dst + g, 0:SEQ], [s])
        return done

    def convolution(self, v, gate):
        c, nc = self.c, self.nc
        half = TAPS // 2
        y, sq = self.square[:, 0:2, :], self.square[:, 2:4, :]
        mean, inv = self.value[:, 3, :], self.inverse[:, 0:SEQ]
        c.dve.wait(c.act.now, c.pe.now)
        inner = v[:, :, half:half + SEQ]
        s = c.dve.mark(nc.vector.tensor_tensor(inner, inner, gate[:, :, :], ALU.mult))
        c.dve.wait(s)
        for tap in range(TAPS):
            for g in range(2):
                src = v[:, g, tap:tap + SEQ]
                at = COLUMNS["conv_w"] + TAPS * g + tap
                w = self.cols[:, at:at + 1]
                if tap == 0:
                    c.dve.mark(nc.vector.tensor_scalar(y[:, g, :], src, w, self.col("conv_b", g), ALU.mult, ALU.add))
                else:
                    c.dve.wait((c.dve.sem, c.dve.count - 1))
                    c.dve.mark(nc.vector.scalar_tensor_tensor(y[:, g, :], src, w, y[:, g, :], ALU.mult, ALU.add))
        convolved = c.dve.now
        yield
        i, summed = self.mean_square(lambda t: y[:, t, :], 2, SEQ, [convolved])
        c.act.wait(summed)
        s = c.act.mark(nc.scalar.activation(mean, c.bank(i), ACT.Copy, scale=1.0 / 256))
        self.free(i, s)
        c.dve.wait(s, convolved)
        for g in range(2):
            s = c.dve.mark(nc.vector.tensor_tensor(y[:, g, :], y[:, g, :], mean, ALU.subtract))
        c.act.wait(s)
        squared = c.act.mark(nc.scalar.activation(sq, y, ACT.Square))
        yield
        i, summed = self.mean_square(lambda t: sq[:, t, :], 2, SEQ, [squared])
        s, last = self.inverse_root(inv, c.bank(i), SEQ, 1.0 / 256, self.eps[:, 1:2], [summed])
        self.free(i, s)
        yield
        c.dve.wait(last)
        for g in range(2):
            s = c.dve.mark(nc.vector.tensor_tensor(y[:, g, :], y[:, g, :], inv, ALU.mult))
            c.act.wait(s)
            c.act.mark(nc.scalar.activation(y[:, g, :], y[:, g, :], ACT.Silu, scale=self.col("conv_ln_g", g),
                                            bias=self.col("conv_ln_b", g)))
        yield

    def neighbourhood(self, q, k, v, meanwhile):
        c, nc, d = self.c, self.nc, self.d
        mem = Memory(nc)
        mask, mask_in = self.const(mem, "window", [P, GW])
        bias = mem("bias", [P, 2, NBIAS, GW])
        e = mem("na_exp", [P, 3, KEYS2])
        et = self.value[:, 0:3, :].rearrange("p a (b m) -> p (a b) m", m=P).rearrange("p (x b) m -> p x b m", x=2)
        stat = mem("na_stats", [P, 2, 8])
        o = self.inverse
        scale = HD2 ** -0.5
        steps = [(h, t) for h in range(NH2) for t in range(SEQ // P)]
        exped_at, normed_at, turned_at, copied_at, applied_at, bias_at = {}, {}, {}, {}, {}, {}
        out_split = [None]
        last_add = {}

        def bias_in(h):
            bias_at[h] = self.load(f"bias_in_{h % 2}", bias[:, h % 2, :, :], d["bias"][h],
                                   [last_add.get(h - 2)])

        def bias_masked(h):
            c.dve.wait(mask_in, bias_at[h])
            bias_at[h] = c.dve.mark(nc.vector.tensor_tensor(
                bias[:, h % 2, :, :], bias[:, h % 2, :, :],
                mask[:, :].unsqueeze(1).to_broadcast([P, NBIAS, GW]), ALU.add))

        def scores(n):
            h, t = steps[n]
            x = n % 2
            rows = slice(64 * (h % 2), 64 * (h % 2) + 64)
            j = 2 * x
            c.pe.wait(c.bank_free[j], c.bank_free[j + 1])
            lhs = q[rows, h // 2, P * t:P * (t + 1)]
            nc.tensor.matmul(c.bank(j), lhs, k[rows, h // 2, 0:SEQ], start=True, stop=True)
            done = c.pe.mark(nc.tensor.matmul(c.bank(j + 1, CTX), lhs, k[rows, h // 2, SEQ:KEYS2],
                                              start=True, stop=True))
            st, es = stat[:, x, :], e[:, n % 3, :]
            c.dve.wait(done, turned_at.get(n - 3), bias_at[h], normed_at.get(n - 2))
            first = ROWS - 2 - 2 * t
            s = c.dve.mark(nc.vector.scalar_tensor_tensor(
                es[:, 0:SEQ], c.bank(j), scale,
                bias[:, h % 2, first:first + ROWS, :].rearrange("p a b -> p (a b)"), ALU.mult, ALU.add))
            last_add[h] = s
            s2 = c.dve.mark(nc.vector.tensor_scalar(es[:, SEQ:KEYS2], c.bank(j + 1, CTX), scale, None, ALU.mult))
            self.free(j, s)
            self.free(j + 1, s2)
            c.dve.wait(s2)
            s = c.dve.mark(nc.vector.tensor_reduce(st[:, 0:1], es, AX.X, ALU.max))
            c.dve.wait(s)
            s = c.dve.mark(nc.vector.tensor_scalar(st[:, 1:2], st[:, 0:1], -1.0, None, ALU.mult))
            c.act.wait(s)
            exped_at[n] = c.act.mark(nc.scalar.activation(es, es, ACT.Exp, bias=st[:, 1:2], scale=1.0,
                                                          accum_out=st[:, 2:3]))

        def norm(n):
            st = stat[:, n % 2, :]
            c.dve.wait(exped_at[n])
            s = c.dve.mark(nc.vector.reciprocal(st[:, 3:4], st[:, 2:3]))
            c.dve.wait(s)
            normed_at[n] = c.dve.mark(nc.vector.tensor_scalar(e[:, n % 3, :], e[:, n % 3, :], st[:, 3:4], None, ALU.mult))

        def turning(n):
            x = n % 2
            c.pe.wait(normed_at[n], c.bank_free[4], c.bank_free[5])
            for y in range(KEYS2 // P):
                ins = nc.tensor.transpose(self.c.psum[:, 4 + y // 4, P * (y % 4):P * (y % 4 + 1)],
                                          e[:, n % 3, P * y:P * (y + 1)], self.ident[:, :])
            turned_at[n] = c.pe.mark(ins)
            c.act.wait(turned_at[n], applied_at.get(n - 2))
            s = c.act.mark(nc.scalar.activation(et[:, x, 0:4, :].rearrange("p a b -> p (a b)"), c.bank(4), ACT.Copy))
            self.free(4, s)
            s = c.act.mark(nc.scalar.activation(et[:, x, 4:6, :].rearrange("p a b -> p (a b)"), c.bank(5, CTX),
                                                ACT.Copy))
            self.free(5, s)
            copied_at[n] = s

        def applying(n):
            h, t = steps[n]
            x = n % 2
            bank = 6 + h // 2 % 2
            rows = slice(64 * (h % 2), 64 * (h % 2) + 64)
            c.pe.wait(copied_at[n])
            if t == 0 and h % 2 == 0:
                c.pe.wait(c.bank_free[bank])
            for y in range(KEYS2 // P):
                ins = nc.tensor.matmul(self.c.psum[rows, bank, P * t:P * (t + 1)],
                                       v[:, y, HD2 * h:HD2 * (h + 1)], et[:, x, y, :],
                                       start=y == 0, stop=y == KEYS2 // P - 1)
            applied_at[n] = c.pe.mark(ins)
            if t == SEQ // P - 1 and h % 2 == 1:
                c.act.wait(applied_at[n], out_split[0])
                got = c.act.mark(nc.scalar.activation(o[:, 0:SEQ], c.bank(bank), ACT.Copy))
                self.free(bank, got)
                out_split[0] = split_value(c, o[:, 0:SEQ], self.x_high[:, 4 + h // 2, 0:SEQ],
                                           self.x_low[:, 4 + h // 2, 0:SEQ], [got])

        for h in range(2):
            bias_in(h)
        c.act.wait(meanwhile())
        for h in range(2):
            bias_masked(h)
        for n in range(len(steps) + 3):
            if n < len(steps):
                h, t = steps[n]
                if t == 0 and 1 <= h < NH2 - 1:
                    bias_in(h + 1)
                if t == 3 and 1 <= h < NH2 - 1:
                    bias_masked(h + 1)
                scores(n)
            if 0 <= n - 1 < len(steps):
                norm(n - 1)
            if 0 <= n - 2 < len(steps):
                turning(n - 2)
            if n >= 3:
                applying(n - 3)
        c.fence()
        mem.close()


_WIDTHS = (("ln1", KT), ("ln2", KT), ("final1", KT), ("da_norm", 1), ("gla_norm", 1), ("gate_b", 4),
           ("c", KT), ("c_ctx", KT), ("ada_b", 6 * KT), ("norm1_2", KT), ("norm2_2", KT), ("final2", KT),
           ("conv_w", 2 * TAPS), ("conv_b", 2), ("conv_ln_g", 2), ("conv_ln_b", 2), ("conv_pw_b", 2))
COLUMNS, _at = {}, 0
for _name, _n in _WIDTHS:
    COLUMNS[_name] = _at
    _at += _n
N_COLUMNS = _at


def shape_constants():
    out = {"identity": np.eye(P, dtype=np.float32)}
    inv = np.power(np.float32(500000.0), -np.arange(0, ROPE, 2, dtype=np.float32) / np.float32(ROPE)).astype(np.float32)
    ang = (np.arange(T, dtype=np.float32)[:, None] * inv[None, :]).astype(np.float32)
    cos, sin = np.ones((P, T), np.float32), np.zeros((P, T), np.float32)
    swap = np.zeros((P, P), np.float32)
    hr = ROPE // 2
    for o in (0, DA_DIM):
        for i in range(hr):
            cos[o + i] = cos[o + hr + i] = np.cos(ang[:, i])
            sin[o + i] = sin[o + hr + i] = np.sin(ang[:, i])
            swap[o + hr + i, o + i] = -1.0
            swap[o + i, o + hr + i] = 1.0
    out.update(rope_cos=cos, rope_sin=sin, rope_swap=swap)
    j, i = np.arange(JT)[:, None], np.arange(JT)[None, :]
    same = (j // LEAF) == (i // LEAF)
    masks = [(j < LEAF) & (i >= LEAF), (j >= LEAF) & (i < LEAF), same & (j <= i), same & (j >= i)]
    out["leaf_masks"] = np.ascontiguousarray(np.stack(masks, 1).astype(np.float32))
    out["iota_picks"] = np.broadcast_to(np.arange(TOPK, dtype=np.float32), (P, TOPK)).copy()
    out["iota_keys"] = np.broadcast_to(np.arange(NK, dtype=np.float32), (P, NK)).copy()
    m = FFT_CH // FFT_G
    a = 2 * np.pi * (np.outer(np.arange(m), np.arange(m)) % m) / m
    chan = np.zeros((P, 2, P))
    for g in range(2):
        chan[m * g:m * (g + 1), 0, m * g:m * (g + 1)] = np.cos(a)
        chan[m * g:m * (g + 1), 1, m * g:m * (g + 1)] = np.sin(a)
    out["dft_channels"] = chan.astype(np.float32)
    a = 2 * np.pi * (np.outer(np.arange(SEQ), np.arange(SEQ)) % SEQ) / SEQ
    norm = 1.0 / math.sqrt(SEQ * m)
    tok = np.stack([np.cos(a), -np.sin(a)]) * norm
    out["dft_tokens"] = np.ascontiguousarray(tok.reshape(2, 4, P, SEQ).transpose(2, 0, 1, 3)).astype(np.float32)
    col = np.arange(GW)
    start = np.clip(col - WC // 2, 0, GW - WC)
    seen = (col[None, :] >= start[:, None]) & (col[None, :] < start[:, None] + WC)
    out["window"] = np.tile(np.where(seen, 0.0, -1e30).astype(np.float32), (2, 1))
    return out


def lay_out(inputs):
    g = {k: np.asarray(v) for k, v in inputs.items()}

    def tiles(x):
        return x.reshape((x.shape[0] // P, P) + x.shape[1:]).swapaxes(0, 1)

    out = dict(shape_constants())
    tokens = np.concatenate([g["meta_tokens"], g["x"][0]], axis=0)
    out["tokens"] = tiles(tokens.T)
    out["ctx"] = tiles(g["ctx_2"][0].T)
    out["w_in"] = g["w_in"][0]
    out["w_out"] = g["w_out"][0]
    out["peer_w_q"] = g["peer_w_q"][0]
    u = g["peer_u"][0].reshape(NK, NK // EG, EG, KT, P)
    out["peer_u"] = u.transpose(1, 4, 3, 2, 0).reshape(NK // EG, P, KT * EG * NK)
    out["peer_v"] = g["peer_v"][0].reshape(NK, NK, D).transpose(1, 0, 2)
    out["sub_keys"] = g["peer_sub_keys"][0].reshape(2 * PH, NK, P).transpose(2, 0, 1)
    w2 = np.zeros((2 * GLA_RANK, 512), np.float32)
    w2[:GLA_RANK, :256] = g["gla_gate_w2_f"][0]
    w2[GLA_RANK:, 256:] = g["gla_gate_w2_b"][0]
    out["gate_w2"] = w2
    out["lambdas"] = np.stack([g[f"da_lambda_{n}"][0] for n in ("q1", "q2", "k1", "k2")], axis=1)
    out["ada_w"] = g["ada_w_2"][0]
    out["w_in_2"] = g["w_in_2"][0]
    out["w_out_2"] = g["w_out_2"][0]
    out["mlp_w1"] = g["mlp_w1_2"][0]
    out["mlp_w2"] = g["mlp_w2_2"][0]
    out["w_fourier"] = tiles(g["w_fourier_2"][0])
    out["conv_pw_w"] = tiles(g["conv_pw_w_2"][0])
    rpb = g["na_rpb_2"][0]
    row, colq = np.arange(P) // GW, np.arange(P) % GW
    off_r = np.arange(NBIAS)[None, :, None] + 1 - row[:, None, None]
    off_c = np.clip(np.arange(GW)[None, None, :] - colq[:, None, None] + WC - 1, 0, 2 * WC - 2)
    out["bias"] = rpb[:, off_r, off_c]
    gate_b = np.concatenate([g["gla_gate_b_f"][0], g["gla_gate_b_b"][0]])
    conv_w = g["conv_dw_w_2"][0].T.reshape(2, P, TAPS).transpose(1, 0, 2).reshape(P, 2 * TAPS)
    columns = {
        "ln1": tiles(g["ln1_w"][0]), "ln2": tiles(g["ln2_w"][0]), "final1": tiles(g["final_norm_w"]),
        "da_norm": tiles(g["da_subln_w"][0]), "gla_norm": tiles(g["gla_norm_w"][0]), "gate_b": tiles(gate_b),
        "c": tiles(g["c_2"][0]), "c_ctx": tiles(g["c_ctx_2"]), "ada_b": tiles(g["ada_b_2"][0]),
        "norm1_2": tiles(g["norm1_g_2"][0]), "norm2_2": tiles(g["norm2_g_2"][0]),
        "final2": tiles(g["final_norm_g_2"]), "conv_w": conv_w, "conv_b": tiles(g["conv_dw_b_2"][0]),
        "conv_ln_g": tiles(g["conv_norm_g_2"][0]), "conv_ln_b": tiles(g["conv_norm_b_2"][0]),
        "conv_pw_b": tiles(g["conv_pw_b_2"][0]),
    }
    out["columns"] = np.concatenate([columns[n] for n, _ in _WIDTHS], axis=1)
    return {k: np.ascontiguousarray(v) for k, v in out.items()}


def kernel(**inputs):
    import concourse.bacc as bacc
    from concourse.bass_utils import run_bass_kernel_spmd

    arrays = lay_out(inputs)
    nc = bacc.Bacc("TRN2", target_bir_lowering=False, num_devices=1)
    dram = {name: nc.dram_tensor(f"{name}_dram", a.shape, mybir.dt.from_np(a.dtype), kind="ExternalInput").ap()
            for name, a in arrays.items()}
    out = nc.dram_tensor("out_dram", (P, KT, SEQ), F32, kind="ExternalOutput").ap()
    gate_dram = nc.dram_tensor("gate_dram", (SEQ // TC, P, NK, TC), F32, kind="Internal").ap()
    act_dram = nc.dram_tensor("act_dram", (EG * AHEAD, P, SEQ), F32, kind="Internal").ap()
    Net(nc, dram, out, gate_dram, act_dram).build()
    got = run_bass_kernel_spmd(nc, [{f"{n}_dram": a for n, a in arrays.items()}], core_ids=[0])
    y = np.asarray(got.results[0]["out_dram"])
    return np.ascontiguousarray(y.transpose(2, 1, 0).reshape(1, SEQ, D))
```
